# Optimizing a Trainium2 kernel written in Bass

```python
import jax, jax.numpy as jnp
from jax import lax
import numpy as np

D_MODEL = 1024
BATCH = 1
SEQ = 256
DEPTH = 2

HEAD_DIM = 64
Q_BLOCK = 128
MLA_HEADS = 4
MLA_Q_RANK = 256
MLA_KV_RANK = 128
MLA_NOPE = 64
MLA_ROPE = 32
MLA_QK = MLA_NOPE + MLA_ROPE
MLA_V = 64
ROPE_THETA = 10000.0
SWA_Q_HEADS = 8
SWA_KV_HEADS = 2
SWA_WINDOW = 128
SB_HEADS = 4

WIDTH_A = MLA_HEADS * MLA_V
WIDTH_B = SWA_Q_HEADS * HEAD_DIM
WIDTH_C = SB_HEADS * HEAD_DIM
MIX_WIDTH = WIDTH_A + WIDTH_B + WIDTH_C

COLS_A = MLA_Q_RANK + MLA_KV_RANK + MLA_ROPE
COLS_B = (SWA_Q_HEADS + 2 * SWA_KV_HEADS) * HEAD_DIM
COLS_C = 3 * SB_HEADS * HEAD_DIM
IN_COLS = COLS_A + COLS_B + COLS_C

D_FF = 2816
N_EXPERTS = 8
TOP_K = 2
D_FF_EXPERT = 3584
MOE_BLOCK = 256
N_DENSE = (DEPTH + 1) // 2
N_MOE = DEPTH // 2

RMS_EPS = 1e-6
NEG = -1e30

kernel_name = "hybrid_mla_swa_stickbreaking_moe"

def rms_norm(x, g):
    xf = x.astype(jnp.float32)
    y = xf * lax.rsqrt(jnp.mean(xf * xf, axis=-1, keepdims=True) + RMS_EPS)
    return (y * g.astype(jnp.float32)).astype(x.dtype)

def rope(x, pos):
    half = x.shape[-1] // 2
    inv = ROPE_THETA ** (-jnp.arange(half, dtype=jnp.float32) / half)
    ang = pos.astype(jnp.float32)[:, None] * inv[None, :]
    cos = jnp.cos(ang)[None, :, None, :]
    sin = jnp.sin(ang)[None, :, None, :]
    xf = x.astype(jnp.float32)
    x1, x2 = xf[..., :half], xf[..., half:]
    return jnp.concatenate([x1 * cos - x2 * sin, x1 * sin + x2 * cos], axis=-1).astype(x.dtype)

def alibi_slopes(n):
    return jnp.exp2(-8.0 * jnp.arange(1, n + 1, dtype=jnp.float32) / n)

def to_query_blocks(q):
    B, S, H, D = q.shape
    return q.reshape(B, S // Q_BLOCK, Q_BLOCK, H, D).transpose(1, 0, 3, 2, 4)

def from_query_blocks(o):
    nb, B, QB, H, D = o.shape
    return o.transpose(1, 0, 2, 3, 4).reshape(B, nb * QB, H * D)

def dense_causal_softmax(q, k, v, scale):
    S = q.shape[1]
    key_pos = jnp.arange(S)

    def one_block(args):
        qi, bi = args
        s = jnp.einsum('bhqd,bkhd->bhqk', qi, k, preferred_element_type=jnp.float32) * scale
        q_pos = bi * Q_BLOCK + jnp.arange(Q_BLOCK)
        s = jnp.where(key_pos[None, :] <= q_pos[:, None], s, NEG)
        p = jax.nn.softmax(s, axis=-1).astype(v.dtype)
        return jnp.einsum('bhqk,bkhd->bqhd', p, v)

    o = lax.map(one_block, (to_query_blocks(q), jnp.arange(S // Q_BLOCK)))
    return from_query_blocks(o)

def mla_mixer(cols, pos, cq_norm_g, w_uq, ckv_norm_g, w_ukv, qn_g, kn_g):
    B, S, _ = cols.shape
    c_q = cols[..., :MLA_Q_RANK]
    c_kv = cols[..., MLA_Q_RANK:MLA_Q_RANK + MLA_KV_RANK]
    k_pe = cols[..., MLA_Q_RANK + MLA_KV_RANK:]
    q = (rms_norm(c_q, cq_norm_g) @ w_uq).reshape(B, S, MLA_HEADS, MLA_QK)
    kv = (rms_norm(c_kv, ckv_norm_g) @ w_ukv).reshape(B, S, MLA_HEADS, MLA_NOPE + MLA_V)
    k_nope, v = kv[..., :MLA_NOPE], kv[..., MLA_NOPE:]
    k = jnp.concatenate([k_nope, jnp.broadcast_to(k_pe[:, :, None, :], (B, S, MLA_HEADS, MLA_ROPE))], axis=-1)
    q = rms_norm(q, qn_g)
    k = rms_norm(k, kn_g)
    q = jnp.concatenate([q[..., :MLA_NOPE], rope(q[..., MLA_NOPE:], pos)], axis=-1)
    k = jnp.concatenate([k[..., :MLA_NOPE], rope(k[..., MLA_NOPE:], pos)], axis=-1)
    return dense_causal_softmax(q, k, v, MLA_QK ** -0.5)

def swa_sink_mixer(cols, qn_g, kn_g, sinks):
    B, S, _ = cols.shape
    W, Hq, Hkv, D = SWA_WINDOW, SWA_Q_HEADS, SWA_KV_HEADS, HEAD_DIM
    G = Hq // Hkv
    nb = S // W
    q = rms_norm(cols[..., :Hq * D].reshape(B, S, Hq, D), qn_g)
    k = rms_norm(cols[..., Hq * D:(Hq + Hkv) * D].reshape(B, S, Hkv, D), kn_g)
    v = cols[..., (Hq + Hkv) * D:].reshape(B, S, Hkv, D)

    def band(t):
        tp = jnp.pad(t, ((0, 0), (W, 0), (0, 0), (0, 0))).reshape(B, nb + 1, W, Hkv, D)
        return jnp.concatenate([tp[:, :-1], tp[:, 1:]], axis=2)

    kb, vb = band(k), band(v)
    qb = q.reshape(B, nb, W, Hkv, G, D)
    s = jnp.einsum('bnqhgd,bnkhd->bnhgqk', qb, kb, preferred_element_type=jnp.float32) * (D ** -0.5)
    dist = jnp.arange(W)[:, None] + W - jnp.arange(2 * W)[None, :]
    blk = jnp.arange(nb)[:, None, None]
    valid = (dist >= 0) & (dist < W) & (blk * W + jnp.arange(2 * W)[None, None, :] - W >= 0)
    slopes = alibi_slopes(Hq).reshape(Hkv, G)
    s = s - slopes[None, None, :, :, None, None] * dist.astype(jnp.float32)
    s = jnp.where(valid[None, :, None, None], s, NEG)
    sink = sinks.astype(jnp.float32).reshape(1, 1, Hkv, G, 1, 1)
    m = jnp.maximum(jnp.max(s, axis=-1, keepdims=True), sink)
    p = jnp.exp(s - m)
    probs = p / (jnp.sum(p, axis=-1, keepdims=True) + jnp.exp(sink - m))
    o = jnp.einsum('bnhgqk,bnkhd->bnqhgd', probs.astype(v.dtype), vb)
    return o.reshape(B, S, Hq * D)

def stick_breaking_mixer(cols):
    B, S, _ = cols.shape
    H, D = SB_HEADS, HEAD_DIM
    q = cols[..., :H * D].reshape(B, S, H, D)
    k = cols[..., H * D:2 * H * D].reshape(B, S, H, D)
    v = cols[..., 2 * H * D:].reshape(B, S, H, D)
    key_pos = jnp.arange(S)
    scale = D ** -0.5

    def one_block(args):
        qi, bi = args
        z = jnp.einsum('bhqd,bkhd->bhqk', qi, k, preferred_element_type=jnp.float32) * scale
        q_pos = bi * Q_BLOCK + jnp.arange(Q_BLOCK)
        mask = key_pos[None, :] < q_pos[:, None]
        log_1m_beta = jnp.where(mask, jax.nn.log_sigmoid(-z), 0.0)
        between = lax.cumsum(log_1m_beta, axis=3, reverse=True) - log_1m_beta
        a = jnp.where(mask, jnp.exp(jax.nn.log_sigmoid(z) + between), 0.0).astype(v.dtype)
        return jnp.einsum('bhqk,bkhd->bqhd', a, v)

    o = lax.map(one_block, (to_query_blocks(q), jnp.arange(S // Q_BLOCK)))
    return from_query_blocks(o)

def swiglu(h, w_gate, w_up, w_down):
    return (jax.nn.silu(h @ w_gate) * (h @ w_up)) @ w_down

def moe_swiglu(h, router_w, w_gate, w_up, w_down):
    B, S, D = h.shape
    N = B * S
    xf = h.reshape(N, D)
    logits = (xf @ router_w).astype(jnp.float32)
    top_logits, top_idx = lax.top_k(logits, TOP_K)
    gates = jax.nn.softmax(top_logits, axis=-1).astype(h.dtype)
    flat_e = top_idx.reshape(-1)
    flat_tok = jnp.repeat(jnp.arange(N, dtype=jnp.int32), TOP_K)
    flat_g = gates.reshape(-1)
    order = jnp.argsort(flat_e)
    sorted_e = flat_e[order]
    counts = jnp.bincount(flat_e, length=N_EXPERTS)
    padded = (counts + MOE_BLOCK - 1) // MOE_BLOCK * MOE_BLOCK
    start = jnp.cumsum(counts) - counts
    pend = jnp.cumsum(padded)
    pstart = pend - padded
    dest = pstart[sorted_e] + (jnp.arange(N * TOP_K) - start[sorted_e])
    P = N * TOP_K + N_EXPERTS * MOE_BLOCK
    n_blk = P // MOE_BLOCK
    slot_tok = jnp.zeros((P,), jnp.int32).at[dest].set(flat_tok[order])
    slot_gate = jnp.zeros((P,), h.dtype).at[dest].set(flat_g[order])
    blk_e = jnp.minimum(jnp.searchsorted(pend, jnp.arange(n_blk) * MOE_BLOCK, side='right'), N_EXPERTS - 1)
    xs = xf[slot_tok].reshape(n_blk, MOE_BLOCK, D)

    def expert_block(args):
        xb, e = args
        return swiglu(xb, w_gate[e], w_up[e], w_down[e])

    ys = lax.map(expert_block, (xs, blk_e)).reshape(P, D) * slot_gate[:, None]
    return jnp.zeros((N, D), h.dtype).at[slot_tok].add(ys).reshape(B, S, D)

def setup_inputs(seed: int = 0) -> dict:
    keys = jax.random.split(jax.random.key(seed), 22)

    def nrm(i, shape, scale):
        return jax.random.normal(keys[i], shape, jnp.float32) * scale

    def gain(i, shape):
        return 1.0 + nrm(i, shape, 0.02)

    L = DEPTH
    return {
        "x": nrm(0, (BATCH, SEQ, D_MODEL), 1.0),
        "attn_norm_g": gain(1, (L, D_MODEL)),
        "w_in": nrm(2, (L, D_MODEL, IN_COLS), D_MODEL ** -0.5),
        "mla_cq_norm_g": gain(3, (L, MLA_Q_RANK)),
        "mla_w_uq": nrm(4, (L, MLA_Q_RANK, MLA_HEADS * MLA_QK), MLA_Q_RANK ** -0.5),
        "mla_ckv_norm_g": gain(5, (L, MLA_KV_RANK)),
        "mla_w_ukv": nrm(6, (L, MLA_KV_RANK, MLA_HEADS * (MLA_NOPE + MLA_V)), MLA_KV_RANK ** -0.5),
        "mla_qn_g": gain(7, (L, MLA_QK)),
        "mla_kn_g": gain(8, (L, MLA_QK)),
        "swa_qn_g": gain(9, (L, HEAD_DIM)),
        "swa_kn_g": gain(10, (L, HEAD_DIM)),
        "swa_sinks": nrm(11, (L, SWA_Q_HEADS), 1.0),
        "out_norm_g": gain(12, (L, MIX_WIDTH)),
        "w_out": nrm(13, (L, MIX_WIDTH, D_MODEL), MIX_WIDTH ** -0.5),
        "ffn_norm_g": gain(14, (L, D_MODEL)),
        "dense_w_gate": nrm(15, (N_DENSE, D_MODEL, D_FF), D_MODEL ** -0.5),
        "dense_w_up": nrm(16, (N_DENSE, D_MODEL, D_FF), D_MODEL ** -0.5),
        "dense_w_down": nrm(17, (N_DENSE, D_FF, D_MODEL), D_FF ** -0.5),
        "router_w": nrm(18, (N_MOE, D_MODEL, N_EXPERTS), D_MODEL ** -0.5),
        "moe_w_gate": nrm(19, (N_MOE, N_EXPERTS, D_MODEL, D_FF_EXPERT), D_MODEL ** -0.5),
        "moe_w_up": nrm(20, (N_MOE, N_EXPERTS, D_MODEL, D_FF_EXPERT), D_MODEL ** -0.5),
        "moe_w_down": nrm(21, (N_MOE, N_EXPERTS, D_FF_EXPERT, D_MODEL), D_FF_EXPERT ** -0.5),
    }

def reference(x, attn_norm_g, w_in, mla_cq_norm_g, mla_w_uq, mla_ckv_norm_g, mla_w_ukv,
              mla_qn_g, mla_kn_g, swa_qn_g, swa_kn_g, swa_sinks, out_norm_g, w_out,
              ffn_norm_g, dense_w_gate, dense_w_up, dense_w_down, router_w,
              moe_w_gate, moe_w_up, moe_w_down):
    pos = jnp.arange(x.shape[1])
    for layer in range(DEPTH):
        h = rms_norm(x, attn_norm_g[layer])
        cols = h @ w_in[layer]
        o_a = mla_mixer(cols[..., :COLS_A], pos, mla_cq_norm_g[layer], mla_w_uq[layer],
                        mla_ckv_norm_g[layer], mla_w_ukv[layer], mla_qn_g[layer], mla_kn_g[layer])
        o_b = swa_sink_mixer(cols[..., COLS_A:COLS_A + COLS_B], swa_qn_g[layer], swa_kn_g[layer],
                             swa_sinks[layer])
        o_c = stick_breaking_mixer(cols[..., COLS_A + COLS_B:])
        g = out_norm_g[layer]
        mix = jnp.concatenate([
            rms_norm(o_a, g[:WIDTH_A]),
            rms_norm(o_b, g[WIDTH_A:WIDTH_A + WIDTH_B]),
            rms_norm(o_c, g[WIDTH_A + WIDTH_B:]),
        ], axis=-1)
        x = x + mix @ w_out[layer]
        h = rms_norm(x, ffn_norm_g[layer])
        j = layer // 2
        if layer % 2 == 0:
            x = x + swiglu(h, dense_w_gate[j], dense_w_up[j], dense_w_down[j])
        else:
            x = x + moe_swiglu(h, router_w[j], moe_w_gate[j], moe_w_up[j], moe_w_down[j])
    return x


_drawn_inputs = setup_inputs


def setup_inputs(seed=0):
    import zlib

    import numpy as np

    out = dict(_drawn_inputs(seed))
    spreads = {}
    factors = {'mla_cq_norm_g': 5.825,
     'mla_ckv_norm_g': 3.363,
     'mla_qn_g': 6.924,
     'mla_kn_g': 4.023,
     'swa_qn_g': 3.949,
     'swa_kn_g': 2.982,
     'ffn_norm_g': 2.784}
    for name, (base, spread) in spreads.items():
        noise = np.random.default_rng([zlib.crc32(name.encode()), seed]).standard_normal(out[name].shape)
        drawn = base * np.exp(spread * noise) if base else spread * noise
        out[name] = __import__('jax').numpy.asarray(drawn.astype(out[name].dtype))
    for name, factor in factors.items():
        out[name] = (out[name] * factor).astype(out[name].dtype)
    return out
```

```python
from contextlib import ExitStack

import numpy as np

import concourse.bass as bass
from concourse import mybir

F32 = mybir.dt.float32
I32 = mybir.dt.int32
U32 = mybir.dt.uint32
ALU = mybir.AluOpType
ACT = mybir.ActivationFunctionType
AX = mybir.AxisListType

P = 128
D = 1024
T = 256
TT = T // P
KD = D // P
DEPTH = 2
HD = 64
QR, KVR, NOPE, ROPE = 256, 128, 64, 32
HA, HB, HKV, HC = 4, 8, 2, 4
QK = NOPE + ROPE
C_CKV = QR
C_KPE = QR + KVR
C_BQ = C_KPE + ROPE
C_BK = C_BQ + HB * HD
C_BV = C_BK + HKV * HD
C_CQ = C_BV + HKV * HD
C_CK = C_CQ + HC * HD
C_CV = C_CK + HC * HD
IN_COLS = C_CV + HC * HD
COL_CHUNKS = [(0, C_BQ), (C_BQ, 512), (C_BQ + 512, 512), (C_BQ + 1024, 512)]
FF = 2816
NE = 8
FE = 3584
CH = 512
NCH = FE // CH
EPS = 1e-6
NEG = -1e30
SEG = 3 * P
GROUP = P

CONST = {}
_at = 0
for _name, _w in (("ident", P), ("cos", TT * 16), ("sin", TT * 16), ("causal", SEG), ("negdist", SEG),
                  ("stick_add", SEG), ("stick_mul", SEG), ("neg_tri", P), ("neg_ones", P), ("ones", P),
                  ("rank_tri", P), ("iota", 2 * GROUP), ("swa_scale", TT * (HB + HKV)), ("mla_scale", TT * 2 * HA)):
    CONST[_name] = (_at, _w)
    _at += _w
N_CONST = _at

SMALL = {}
_at = 0
for _l in range(DEPTH):
    for _name, _w in (("attn_g", KD), ("ffn_g", KD), ("out_g", KD), ("cq_g", 2), ("ckv_g", 1), ("swa_q_g", 1),
                      ("swa_k_g", 1), ("qn_g", QK), ("kn_g", QK), ("sinks", HB)):
        SMALL[_name, _l] = (_at, _w)
        _at += _w
SMALL["router"] = (_at, KD * NE)
N_SMALL = _at + KD * NE

RING = 7
UNIT = KD * CH
UNITS = []
for _l in range(DEPTH):
    UNITS += [("in", _l, n) for n in range(4)] + [("out", _l, n) for n in range(2)]
    if _l % 2 == 0:
        UNITS += [(w, _l, n) for n in range((FF + CH - 1) // CH) for w in ("gate", "up", "down")]
UNIT_NO = {u: n for n, u in enumerate(UNITS)}
N_UNITS = len(UNITS)
MOE_UNITS = [("g", 0), ("u", 0)]
for _c in range(1, NCH):
    MOE_UNITS += [("g", _c), ("u", _c), ("d", _c - 1)]
MOE_UNITS.append(("d", NCH - 1))
MOE_NO = {u: n for n, u in enumerate(MOE_UNITS)}
M_UNITS = len(MOE_UNITS)
assert M_UNITS % RING == 0


class Progress:

    def __init__(self, name, marks):
        self.name, self.marks, self.n, self.loop, self.start = name, marks, 0, None, 0

    def step(self, key=None):
        self.n += 1
        if key is not None:
            self.marks[key] = (self.name, self.loop, self.start, self.n - self.start if self.loop else self.n)
        return 1

    def enter(self, loop):
        self.loop, self.start = loop, self.n

    def leave(self, trips):
        k = self.n - self.start
        self.marks["per", self.loop, self.name] = k
        self.n = self.start + trips * k
        self.loop = None


class Counts:

    def __init__(self, known):
        self.known = known

    def at(self, key, it=None, back=0):
        if self.known is None:
            return 1 if it is None else it + 1
        name, loop, start, m = self.known[key]
        if loop is None:
            return m
        k = self.known["per", loop, name]
        if it is None:
            return start + (NE - 1) * k + m
        return it * k + (start + m - back * k)

    def own(self, progress, it=None):
        if progress.loop is None:
            return progress.n
        if self.known is None:
            return it + 1
        return it * self.known["per", progress.loop, progress.name] + progress.n


def trunk_program(nc, known, x, cst, smalls, w_in, w_uq, w_ukv, w_out, dense_g, dense_u, dense_d, moe_g, moe_u,
                  moe_d, out):
    marks = {}
    counts = Counts(known)
    with ExitStack() as ctx:
        def sb(name, shape, dt=F32):
            return ctx.enter_context(nc.sbuf_tensor(name, shape, dt))

        def sem(name):
            return ctx.enter_context(nc.semaphore(name))

        ring = sb("ring", [P, RING, UNIT])
        xres = sb("xres", [P, TT, D])
        consts = sb("consts", [P, N_CONST])
        small = sb("small", [P, N_SMALL])
        hT = sb("hT", [P, KD, T])
        xn = sb("xn", [P, TT, D])
        cols = sb("cols", [P, TT, IN_COLS])
        scratch = sb("scratch", [P, 8 * SEG])
        uq = sb("uq", [P, 2, HA * QK])
        ukv = sb("ukv", [P, HA * (NOPE + HD)])
        mla_v = sb("mla_v", [P, TT, HA * HD])
        mla_T = sb("mla_T", [P, 2 * HA, T])
        swa_qT = sb("swa_qT", [P, HB // 2, T])
        swa_kT = sb("swa_kT", [P, T])
        stick_qT = sb("stick_qT", [P, HC // 2, T])
        stick_kT = sb("stick_kT", [P, HC // 2, T])
        stick = sb("stick", [P, HC, SEG])
        stat = sb("stat", [P, 96])
        stat_a = sb("stat_a", [P, 96])
        stat_t = sb("stat_t", [P, 20])
        top = sb("top", [P, TT, 8])
        top_at = sb("top_at", [P, TT, 8], U32)
        sel = sb("sel", [P, TT, NE])
        over = sb("over", [P, 4])
        over_i = sb("over_i", [1, 1], I32)
        rankm = sb("rankm", [P, TT, NE + 1])
        gates = sb("gates", [P, TT, NE + 1])
        ps = ctx.enter_context(nc.psum_tensor("ps", [P, 8, 512], F32))

        probsT = hT[:, :, :].rearrange("p k t -> p (k t)")[:, 0:4 * SEG].rearrange("p (h s) -> p h s", h=4)
        qk = xn[:, :, :].rearrange("p a d -> p (a d)")[:, 0:TT * 2 * HA * QK].rearrange(
            "p (a h d) -> p a h d", a=TT, h=2 * HA)
        mixed = xn
        S = scratch[:, :].rearrange("p (h s) -> p h s", h=8)
        cqT = scratch[:, 0:512].rearrange("p (c t) -> p c t", c=2)
        ckvT = scratch[:, 512:768]
        mla_sq = scratch[:, 768:768 + 1536]
        rope_t = scratch[:, 768:768 + 1024].rearrange("p (n a h d) -> p n a h d", n=4, a=TT, h=2 * HA)
        swa_sq = scratch[:, 1536:1536 + 1280]
        swa_q = scratch[:, 2048:3072].rearrange("p (a n) -> p a n", a=TT)
        junk = stick[:, :, :].rearrange("p h s -> p (h s)")
        flat = cols[:, :, :].rearrange("p a c -> p (a c)")
        sig = flat[:, 0:1024].rearrange("p (b n) -> p b n", b=2)
        gated = flat[:, 1024:1536]
        hid = flat[:, 1536:2560].rearrange("p (b n) -> p b n", b=2)
        hidT = flat[:, 2560:3584].rearrange("p (b n) -> p b n", b=2)
        xgT = scratch[:, 0:1024].rearrange("p (k s) -> p k s", k=KD)
        ysb = scratch[:, 1024:2048]
        pick = scratch[:, 2048:2304].rearrange("p (a s) -> p a s", a=TT)
        pick_g = scratch[:, 2304:2560].rearrange("p (a s) -> p a s", a=TT)
        pick_gT = scratch[:, 2560:2816].rearrange("p (a s) -> p a s", a=TT)

        def C(name):
            a, w = CONST[name]
            return consts[:, a:a + w]

        def G(name, l=None):
            a, w = SMALL[name] if l is None else SMALL[name, l]
            return small[:, a:a + w]

        ident = C("ident")

        pe_done, act_done, dve_done, unit_used = sem("pe_done"), sem("act_done"), sem("dve_done"), sem("unit_used")
        pe_p, act_p, dve_p, unit_p = (Progress(n, marks) for n in ("pe", "act", "dve", "unit"))
        at = counts.at
        x_loaded, const_loaded, small_loaded = sem("x_loaded"), sem("const_loaded"), sem("small_loaded")
        up_loaded = sem("up_loaded")
        slot_loaded = [sem(f"slot_loaded{n}") for n in range(RING)]
        result_ready, out_stored = sem("result_ready"), sem("out_stored")

        def slot_of(no):
            return ring[:, no % RING, :]

        def loaded(no, it=None):
            v = 16 * (no // RING + 1)
            return slot_loaded[no % RING], v if it is None else it * (16 * M_UNITS // RING) + v

        def cols_in_sbuf(l, n, a):
            return (dve_done if a == 0 else act_done), at(("cols_sb", l, n, a))

        def probs_in_sbuf(l, kind, h):
            return (dve_done if h % 2 else act_done), at(("pT" + kind, l, h))

        hid_d = flat[:, 0:1024].rearrange("p (b n) -> p b n", b=4)
        sig_d = flat[:, 1024:2048].rearrange("p (b n) -> p b n", b=4)
        gated_d = flat[:, 2048:2304]

        block = ctx.enter_context(nc.Block())

        def unit_source(kind, l, n, dst):
            if kind == "in":
                a, w = COL_CHUNKS[n]
                return (dst[:, 0:KD * w].rearrange("p (k n) -> p k n", k=KD),
                        w_in[l].rearrange("(k p) n -> p k n", p=P)[:, :, a:a + w])
            if kind == "out":
                return (dst.rearrange("p (k n) -> p k n", k=KD),
                        w_out[l].rearrange("(k p) n -> p k n", p=P)[:, :, n * CH:(n + 1) * CH])
            w = min(CH, FF - n * CH)
            if kind == "down":
                return (dst[:, 0:w // P * D].rearrange("p (j n) -> p j n", n=D),
                        dense_d[l // 2, n * CH:n * CH + w, :].rearrange("(j p) n -> p j n", p=P))
            src = dense_g if kind == "gate" else dense_u
            return (dst[:, 0:KD * w].rearrange("p (k n) -> p k n", k=KD),
                    src[l // 2].rearrange("(k p) n -> p k n", p=P)[:, :, n * CH:n * CH + w])

        @block.sync
        def _(sp):
            for a in range(TT):
                sp.dma_start(xres[:, a, :], x[0, a * P:(a + 1) * P, :]).then_inc(x_loaded, 16)
            sp.dma_start(consts[:], cst[:]).then_inc(const_loaded, 16)
            sp.dma_start(small[:], smalls[:]).then_inc(small_loaded, 16)

            def load_up(l):
                sp.dma_start(uq[:], w_uq[l].rearrange("(k p) n -> p k n", p=P)).then_inc(up_loaded, 16)
                sp.dma_start(ukv[:], w_ukv[l]).then_inc(up_loaded, 16)

            for no, (kind, l, n) in enumerate(UNITS):
                if no >= RING:
                    sp.wait_ge(unit_used, no - RING + 1)
                dst, src = unit_source(kind, l, n, slot_of(no))
                sp.dma_start(dst, src).then_inc(slot_loaded[no % RING], 16)
                if no == 1:
                    load_up(0)
                if no == UNIT_NO["down", 0, 0]:
                    sp.wait_ge(pe_done, at(("up_proj", 0)))
                    load_up(1)

            def expert_units(group):
                with sp.Fori(0, NE) as e:
                    for r, (kind, c) in enumerate(MOE_UNITS):
                        no = N_UNITS + group * NE * M_UNITS + r
                        sp.wait_ge(unit_used, e * M_UNITS + (no - RING + 1))
                        if kind == "d":
                            rows = moe_d[0, bass.ds(e, 1), c * CH:(c + 1) * CH, :]
                            src = rows.rearrange("o (j p) n -> p (o j) n", p=P)
                            dst = slot_of(no).rearrange("p (j n) -> p j n", n=D)
                        else:
                            columns = (moe_g if kind == "g" else moe_u)[0, bass.ds(e, 1), :, c * CH:(c + 1) * CH]
                            src = columns.rearrange("o (k p) n -> p (o k) n", p=P)
                            dst = slot_of(no).rearrange("p (k n) -> p k n", k=KD)
                        sp.dma_start(dst, src).then_inc(slot_loaded[no % RING], 16)

            expert_units(0)
            sp.wait_ge(dve_done, at("overflow"))
            more = sp.value_load(over_i[0:1, 0:1], min_val=0, max_val=1)
            with sp.If(more > 0):
                expert_units(1)
            sp.wait_ge(result_ready, 1)
            for a in range(TT):
                sp.dma_start(out[0, a * P:(a + 1) * P, :], xres[:, a, :]).then_inc(out_stored, 16)
            sp.wait_ge(out_stored, 16 * TT)

        @block.tensor
        def _(pe):
            def transposes(l, what):
                for a in range(TT):
                    pe.wait_ge(dve_done, at((what, l, a)))
                    for k in range(KD):
                        ins = pe.transpose(ps[:, k // 2, (k % 2) * T + a * P:(k % 2) * T + (a + 1) * P],
                                           xn[:, a, k * P:(k + 1) * P], ident)
                        if a == TT - 1 and k % 2 == 1:
                            ins.then_inc(pe_done, pe_p.step((what + "_T", l, k // 2)))

            def product(bank, width, unit_no, lhs, unit_view, last, key):
                for k in range(KD):
                    ins = pe.matmul(ps[:, bank, 0:width], lhs(k), unit_view(k), start=k == 0, stop=k == KD - 1)
                ins.then_inc(unit_used if last else pe_done, (unit_p if last else pe_p).step(key))

            def layer_mixers(l):
                u0 = UNIT_NO["in", l, 0]
                transposes(l, "attn_n")

                def cols_chunk(n):
                    a0, w = COL_CHUNKS[n]
                    view = slot_of(u0 + n)[:, 0:KD * w].rearrange("p (k n) -> p k n", k=KD)
                    pe.wait_ge(*loaded(u0 + n))
                    for a in range(TT):
                        if n >= 2:
                            pe.wait_ge(*cols_in_sbuf(l, n - 2, a))
                        if n == 0 and a == 0:
                            pe.wait_ge(act_done, at(("attn_n_done", l, 1)))
                            pe.wait_ge(dve_done, at(("attn_n_done", l, 3)))
                        product(4 + (n * 2 + a) % 4, w, u0 + n, lambda k: hT[:, k, a * P:(a + 1) * P],
                                lambda k: view[:, k, :], a == TT - 1, ("cols", l, n, a))

                cols_chunk(0)
                cols_chunk(1)
                pe.wait_ge(dve_done, at(("cq_n", l)))
                for c in range(3):
                    for a in range(TT):
                        ins = pe.transpose(ps[:, c // 2, (c % 2) * T + a * P:(c % 2) * T + (a + 1) * P],
                                           cols[:, a, c * P:(c + 1) * P], ident)
                ins.then_inc(pe_done, pe_p.step(("cq_T", l)))
                cols_chunk(2)
                pe.wait_ge(dve_done, at(("cqT", l)))
                pe.wait_ge(up_loaded, 32 * (l + 1))
                for a in range(TT):
                    for c in range(2):
                        ins = pe.matmul(ps[:, 2 + a, 0:HA * QK], cqT[:, c, a * P:(a + 1) * P], uq[:, c, :],
                                        start=c == 0, stop=c == 1)
                    ins = pe.matmul(ps[:, a, :], ckvT[:, a * P:(a + 1) * P], ukv[:], start=True, stop=True)
                ins.then_inc(pe_done, pe_p.step(("up_proj", l)))
                cols_chunk(3)
                pe.wait_ge(dve_done, at(("swa_n", l)))
                pe.wait_ge(dve_done, at(("kv_read", l)))
                for i in range(4):
                    for a in range(TT):
                        ins = pe.transpose(ps[:, i // 2, (i % 2) * T + a * P:(i % 2) * T + (a + 1) * P],
                                           swa_q[:, a, i * P:(i + 1) * P], ident)
                    if i % 2:
                        ins.then_inc(pe_done, pe_p.step(("swa_q_T", l, i // 2)))
                pe.wait_ge(act_done, at(("q_read", l)))
                for a in range(TT):
                    ins = pe.transpose(ps[:, 2, a * P:(a + 1) * P], cols[:, a, C_BK:C_BV], ident)
                ins.then_inc(pe_done, pe_p.step(("swa_k_T", l)))
                for a in range(TT):
                    pe.wait_ge(*cols_in_sbuf(l, 2, a))
                    pe.wait_ge(*cols_in_sbuf(l, 3, a))
                for i, c0 in ((0, C_CQ), (1, C_CK)):
                    for j in range(2):
                        for a in range(TT):
                            ins = pe.transpose(ps[:, 4 + i, j * T + a * P:j * T + (a + 1) * P],
                                               cols[:, a, c0 + j * P:c0 + (j + 1) * P], ident)
                    ins.then_inc(pe_done, pe_p.step(("stick_T", l, i)))
                pe.wait_ge(dve_done, at(("mla_n", l)))
                for j in range(HA):
                    bank = (6, 7, 3, 2)[j]
                    if bank == 2:
                        pe.wait_ge(act_done, at(("swa_kT", l)))
                    for h in range(2):
                        for a in range(TT):
                            ins = pe.transpose(ps[0:QK, bank, h * T + a * P:h * T + (a + 1) * P],
                                               qk[:, a, 2 * j + h, :], ident)
                    ins.then_inc(pe_done, pe_p.step(("mla_T", l, j)))

                pe.wait_ge(act_done, at(("stickT", l, 0)))
                pe.wait_ge(dve_done, at(("stickT", l, 1)))
                pe.wait_ge(act_done, at(("mlaT", l, 0)))
                pe.wait_ge(dve_done, at(("mlaT", l, 1)))
                for h in range(HC):
                    o, j = HD * (h % 2), h // 2
                    pe.matmul(ps[:, 4 + h, 0:T], stick_kT[o:o + HD, j, 0:P], stick_qT[o:o + HD, j, :],
                              start=True, stop=False, skip_group_check=True)
                    ins = pe.matmul(ps[:, 4 + h, T:SEG], stick_kT[o:o + HD, j, P:T], stick_qT[o:o + HD, j, P:T],
                                    start=False, stop=False, skip_group_check=True)
                    ins.then_inc(pe_done, pe_p.step(("z", l, h)))

                def scores(h, bank, q, k, key):
                    pe.matmul(ps[:, bank, 0:P], q[:, 0:P], k[:, 0:P], start=True, stop=True)
                    ins = pe.matmul(ps[:, bank, P:SEG], q[:, P:T], k[:, 0:T], start=True, stop=True)
                    ins.then_inc(pe_done, pe_p.step(key))

                pe.wait_ge(act_done, at(("mlaT", l, 2)))
                pe.wait_ge(dve_done, at(("mlaT", l, 3)))
                pe.wait_ge(dve_done, at(("swaT", l)))
                for h in range(HA):
                    scores(h, h, mla_T[0:QK, h, :], mla_T[0:QK, HA + h, :], ("sA", l, h))

                def swa_scores(h):
                    o = HD * (h // 4)
                    pe.wait_ge(dve_done, at(("sA_read", l, h) if h < 4 else ("sB_read", l, h - 4)))
                    scores(h, h % 4, swa_qT[o:o + HD, h % 4, :], swa_kT[o:o + HD, :], ("sB", l, h))

                for h in range(4):
                    swa_scores(h)

                for h in range(HC):
                    pe.wait_ge(dve_done, at(("sp", l, h)))
                    pe.matmul(ps[:, 4 + h, 0:T], C("neg_tri"), stick[:, h, 0:T], start=False, stop=False,
                              skip_group_check=True)
                    pe.matmul(ps[:, 4 + h, P:T], C("neg_ones"), stick[:, h, T:SEG], start=False, stop=False,
                              skip_group_check=True)
                    ins = pe.matmul(ps[:, 4 + h, T:SEG], C("neg_tri"), stick[:, h, T:SEG], start=False, stop=True,
                                    skip_group_check=True)
                    ins.then_inc(pe_done, pe_p.step(("cum", l, h)))

                def probs_T(h, bank, slot, key):
                    for j in range(3):
                        ins = pe.transpose(ps[:, bank, j * P:(j + 1) * P], S[:, slot, j * P:(j + 1) * P], ident)
                    ins.then_inc(pe_done, pe_p.step(key))

                def values(pT, bank, c0, v, key):
                    pe.matmul(ps[:, bank, c0:c0 + HD], pT[:, 0:P], v[0], start=True, stop=True, skip_group_check=True)
                    pe.matmul(ps[:, bank, 256 + c0:256 + c0 + HD], pT[:, P:T], v[0], start=True, stop=False,
                              skip_group_check=True)
                    ins = pe.matmul(ps[:, bank, 256 + c0:256 + c0 + HD], pT[:, T:SEG], v[1], start=False, stop=True,
                                    skip_group_check=True)
                    ins.then_inc(pe_done, pe_p.step(key))

                for h in range(HA):
                    pe.wait_ge(act_done, at(("pA", l, h)))
                    pe.wait_ge(dve_done, at(("w_read", l, h)))
                    probs_T(h, 4 + h, h, ("pA_T", l, h))
                for h in range(4, HB):
                    swa_scores(h)
                for h in range(HA):
                    pe.wait_ge(*probs_in_sbuf(l, "A", h))
                    values(probsT[:, h, :], 4, h * HD, [mla_v[:, a, h * HD:(h + 1) * HD] for a in range(TT)],
                           ("oA", l, h))
                for h in range(HC):
                    pe.wait_ge(act_done, at(("aC", l, h)))
                    values(stick[:, h, :], 5, h * HD, [cols[:, a, C_CV + h * HD:C_CV + (h + 1) * HD]
                                                      for a in range(TT)], ("oC", l, h))
                for h in range(HB):
                    bank = (6, 7, 0, 1, 3, 6, 7, 0)[h]
                    pe.wait_ge(act_done, at(("pB", l, h)))
                    if bank in (0, 1, 3) and h != 7:
                        pe.wait_ge(dve_done, at(("sB_read", l, 4 + bank)))
                    if h >= 5:
                        pe.wait_ge(*probs_in_sbuf(l, "B", {5: 0, 6: 1, 7: 2}[h]))
                    probs_T(h, bank, (4 + h) % 8, ("pB_T", l, h))
                    if h % 4 == 3:
                        for g in range(h - 3, h + 1):
                            pe.wait_ge(*probs_in_sbuf(l, "B", g))
                            if g == 0:
                                pe.wait_ge(dve_done, at(("sB_read", l, 6)))
                            kv = g // 4
                            values(probsT[:, g % 4, :], 2 if g < 4 else 1, (g % 4) * HD,
                                   [cols[:, a, C_BV + kv * HD:C_BV + (kv + 1) * HD] for a in range(TT)],
                                   ("oB", l, g))

                pe.wait_ge(dve_done, at(("oB_read", l, 1)))
                transposes(l, "mix_n")
                pe.wait_ge(act_done, at(("mix_n_done", l, 1)))
                pe.wait_ge(dve_done, at(("mix_n_done", l, 3)))
                for n in range(2):
                    no = UNIT_NO["out", l, n]
                    pe.wait_ge(*loaded(no))
                    view = slot_of(no).rearrange("p (k n) -> p k n", k=KD)
                    for a in range(TT):
                        product(4 + n * 2 + a, CH, no, lambda k: hT[:, k, a * P:(a + 1) * P],
                                lambda k: view[:, k, :], a == TT - 1, ("proj", l, n, a))
                transposes(l, "ffn_n")
                pe.wait_ge(act_done, at(("ffn_n_done", l, 1)))
                pe.wait_ge(dve_done, at(("ffn_n_done", l, 3)))

            def dense(l):
                tiles = FF // P
                pe.wait_ge(dve_done, at(("proj_add", l, 3)))

                def gate_up(f):
                    c, j = f // 4, f % 4
                    w = min(CH, FF - c * CH)
                    last = j == w // P - 1
                    if f >= 4:
                        pe.wait_ge(dve_done, at(("hidden", l, f - 4)))
                    for i, kind in enumerate(("gate", "up")):
                        no = UNIT_NO[kind, l, c]
                        if j == 0:
                            pe.wait_ge(*loaded(no))
                        view = slot_of(no)[:, 0:KD * w].rearrange("p (k n) -> p k n", k=KD)
                        for k in range(KD):
                            ins = pe.matmul(ps[:, f % 4, i * T:(i + 1) * T], view[:, k, j * P:(j + 1) * P],
                                            hT[:, k, :], start=k == 0, stop=k == KD - 1)
                        ins.then_inc(unit_used if last else pe_done, (unit_p if last else pe_p).step((kind, l, f)))

                def down(f):
                    c, j = f // 4, f % 4
                    w = min(CH, FF - c * CH)
                    no = UNIT_NO["down", l, c]
                    if j == 0:
                        pe.wait_ge(*loaded(no))
                    view = slot_of(no)[:, 0:w // P * D].rearrange("p (j n) -> p j n", n=D)
                    pe.wait_ge(dve_done, at(("hidden", l, f)))
                    for a in range(TT):
                        for n in range(2):
                            ins = pe.matmul(ps[:, 4 + 2 * a + n, :], hid_d[:, f % 4, a * P:(a + 1) * P],
                                            view[:, j, n * CH:(n + 1) * CH], start=f == 0, stop=f == tiles - 1)
                    if j == w // P - 1:
                        ins.then_inc(unit_used, unit_p.step(("down", l, f)))
                    else:
                        ins.then_inc(pe_done, pe_p.step(("down", l, f)))

                for f in range(tiles):
                    gate_up(f)
                    if f >= 1:
                        down(f - 1)
                down(tiles - 1)

            def experts_prepare():
                l = DEPTH - 1
                for a in range(TT):
                    for k in range(KD):
                        ins = pe.matmul(ps[:, 4, a * NE:(a + 1) * NE], hT[:, k, a * P:(a + 1) * P],
                                        G("router")[:, k * NE:(k + 1) * NE], start=k == 0, stop=k == KD - 1)
                ins.then_inc(pe_done, pe_p.step("logits"))
                pe.wait_ge(dve_done, at("selected"))
                pe.matmul(ps[:, 5, 0:NE], C("rank_tri"), sel[:, 0, :], start=True, stop=True)
                pe.matmul(ps[:, 5, NE:2 * NE], C("ones"), sel[:, 0, :], start=True, stop=False)
                pe.matmul(ps[:, 5, NE:2 * NE], C("rank_tri"), sel[:, 1, :], start=False, stop=True)
                pe.matmul(ps[:, 5, 2 * NE:3 * NE], C("ones"), sel[:, 0, :], start=True, stop=False)
                ins = pe.matmul(ps[:, 5, 2 * NE:3 * NE], C("ones"), sel[:, 1, :], start=False, stop=True)
                ins.then_inc(pe_done, pe_p.step("ranks"))

            def experts(group):
                g = group

                def gather(key, it=None):
                    pe.wait_ge(dve_done, at((g, key, "pick"), it))
                    for n in range(2):
                        if it is None:
                            if n == 0:
                                pe.wait_ge(dve_done, at((g, "pass")))
                        else:
                            pe.wait_ge(act_done, at((g, "hidT", NCH - 2 + n), it))
                        for k in range(4):
                            for a in range(TT):
                                ins = pe.matmul(ps[:, 6 + n, k * P:(k + 1) * P],
                                                xn[:, a, (4 * n + k) * P:(4 * n + k + 1) * P], pick[:, a, :],
                                                start=a == 0, stop=a == TT - 1)
                        ins.then_inc(pe_done, pe_p.step((g, key, "gathered", n)))

                def scatter(it=None, first_wait=None):
                    pe.wait_ge(act_done, at((g, "y_out"), it, 1)) if it is not None else pe.wait_ge(act_done, at((g, "y_out")))
                    for a in range(TT):
                        for n in range(2):
                            if 2 * a + n >= 2:
                                pe.wait_ge(dve_done, at((g, "add" if it is not None else "add_end", 2 * a + n - 2), it))
                            ins = pe.matmul(ps[:, 6 + n, :], pick_gT[:, a, :], ysb[:, n * CH:(n + 1) * CH],
                                            start=True, stop=True)
                            ins.then_inc(pe_done, pe_p.step((g, "scatter" if it is not None else "scatter_end", 2 * a + n)))

                gather("first")
                pe.wait_ge(act_done, at((g, "first", "xgT", 1)))
                for p in (pe_p, unit_p):
                    p.enter(("experts", g))
                with pe.Fori(0, NE) as e:
                    base = N_UNITS + g * NE * M_UNITS

                    def gate_or_up(kind, c):
                        no = base + MOE_NO[kind, c]
                        bank = (0 if kind == "g" else 2) + c % 2
                        pe.wait_ge(*loaded(no, e))
                        if c >= 2:
                            pe.wait_ge(dve_done, at((g, "hid", c - 2), e))
                        elif c == 1:
                            pe.wait_ge(dve_done, at((g, "hid", NCH - 2), e, 1))
                        else:
                            pe.wait_ge(dve_done, at((g, "hid", NCH - 1), e, 1))
                        view = slot_of(no).rearrange("p (k n) -> p k n", k=KD)
                        for k in range(KD):
                            ins = pe.matmul(ps[:, bank, :], xgT[:, k, :], view[:, k, :], start=k == 0,
                                            stop=k == KD - 1)
                        ins.then_inc(unit_used, unit_p.step((g, kind, c)))

                    def hidden_T(c):
                        pe.wait_ge(dve_done, at((g, "hid", c), e))
                        bank = 7 if c % 2 == 0 else 6
                        if c == 0:
                            pe.wait_ge(dve_done, at((g, "add", 3), e))
                        elif c == 1:
                            pe.wait_ge(act_done, at((g, "pick_gT"), e))
                        else:
                            pe.wait_ge(act_done, at((g, "hidT", c - 2), e))
                        for j in range(4):
                            ins = pe.transpose(ps[:, bank, j * P:(j + 1) * P], hid[:, c % 2, j * P:(j + 1) * P], ident)
                        ins.then_inc(pe_done, pe_p.step((g, "hid_T", c)))

                    def down(c):
                        no = base + MOE_NO["d", c]
                        pe.wait_ge(*loaded(no, e))
                        pe.wait_ge(act_done, at((g, "hidT", c), e))
                        if c == 0:
                            pe.wait_ge(act_done, at((g, "y_out"), e, 1))
                        view = slot_of(no).rearrange("p (j n) -> p j n", n=D)
                        for j in range(4):
                            for n in range(2):
                                ins = pe.matmul(ps[:, 4 + n, :], hidT[:, c % 2, j * P:(j + 1) * P],
                                                view[:, j, n * CH:(n + 1) * CH], start=c == 0 and j == 0,
                                                stop=c == NCH - 1 and j == 3)
                        ins.then_inc(unit_used, unit_p.step((g, "d", c)))

                    pe.wait_ge(act_done, at((g, "next", "xgT", 1), e, 1))
                    for c in range(NCH):
                        gate_or_up("g", c)
                        if c == 0:
                            scatter(e)
                        else:
                            hidden_T(c - 1)
                        gate_or_up("u", c)
                        if c == 0:
                            pe.wait_ge(dve_done, at((g, "add", 2), e))
                            for a in range(TT):
                                ins = pe.transpose(ps[:, 6, a * P:(a + 1) * P], pick_g[:, a, :], ident)
                            ins.then_inc(pe_done, pe_p.step((g, "pick_g_T")))
                        else:
                            down(c - 1)
                    hidden_T(NCH - 1)
                    gather("next", e)
                    down(NCH - 1)
                for p in (pe_p, unit_p):
                    p.leave(NE)
                pe.wait_ge(act_done, at((g, "next", "xgT", 1)))
                scatter()

            pe.wait_ge(const_loaded, 16)
            pe.wait_ge(small_loaded, 16)
            layer_mixers(0)
            dense(0)
            pe.wait_ge(dve_done, at(("ffn_add", 0)))
            layer_mixers(1)
            experts_prepare()
            experts(0)
            more = pe.value_load(over_i[0:1, 0:1], min_val=0, max_val=1)
            with pe.If(more > 0):
                experts(1)

        @block.scalar
        def _(act):
            def rstd_of(v, r, key):
                act.wait_ge(dve_done, at((key, "ms")))
                nc.scalar.activation(r, v, ACT.Ln).then_inc(act_done, act_p.step())
                act.wait_ge(act_done, counts.own(act_p))
                nc.scalar.activation(r, r, ACT.Exp, scale=-0.5).then_inc(act_done, act_p.step((key, "r0")))

            def row_stats(l, what):
                for a in range(TT):
                    if what == "attn_n" and l == 0 and a == 0:
                        act.wait_ge(x_loaded, 16 * TT)
                    if what == "attn_n" and l > 0 and a == 0:
                        act.wait_ge(dve_done, at(("ffn_add", l - 1)))
                    if what == "ffn_n" and a == 0:
                        act.wait_ge(dve_done, at(("proj_add", l, 3)))
                    if a or l or what != "attn_n":
                        act.wait_ge(act_done, counts.own(act_p))
                    nc.scalar.activation(junk[:, 0:D], xres[:, a, :], ACT.Square, scale=D ** -0.5,
                                                    accum_out=stat[:, a:a + 1]).then_inc(act_done, act_p.step((what, l, "sq", a)))
                rstd_of(stat[:, 2:4], stat[:, 4:6], (what, l))

            def transposed_out(l, what, gain):
                for b in range(2):
                    act.wait_ge(pe_done, at((what + "_T", l, b)))
                    for i in range(2):
                        k = 2 * b + i
                        nc.scalar.activation(hT[:, k, :], ps[:, b, i * T:(i + 1) * T], ACT.Copy,
                                                        scale=gain[:, k:k + 1]).then_inc(act_done, act_p.step((what + "_done", l, b) if i else None))

            def cols_out(l, n):
                a0, w = COL_CHUNKS[n]
                act.wait_ge(unit_used, at(("cols", l, n, 1)))
                nc.scalar.activation(cols[:, 1, a0:a0 + w], ps[:, 4 + (n * 2 + 1) % 4, 0:w], ACT.Copy).then_inc(act_done, act_p.step(("cols_sb", l, n, 1)))

            def layer_mixers(l):
                row_stats(l, "attn_n")
                if l == 0:
                    act.wait_ge(small_loaded, 16)
                transposed_out(l, "attn_n", G("attn_g", l))
                cols_out(l, 0)
                act.wait_ge(act_done, counts.own(act_p))
                act.wait_ge(dve_done, at(("cols_sb", l, 0, 0)))
                for a in range(TT):
                    for i, (c0, w) in enumerate(((0, QR), (C_CKV, KVR))):
                        nc.scalar.activation(junk[:, (2 * a + i) * QR:(2 * a + i) * QR + w],
                                                        cols[:, a, c0:c0 + w], ACT.Square, scale=w ** -0.5,
                                                        accum_out=stat[:, 6 + 2 * a + i:7 + 2 * a + i]).then_inc(act_done, act_p.step(("cq_sq", l, 2 * a + i)))
                rstd_of(stat[:, 10:14], stat[:, 14:18], ("cq", l))
                cols_out(l, 1)
                cols_out(l, 2)
                act.wait_ge(pe_done, at(("up_proj", l)))
                for a in range(TT):
                    nc.scalar.activation(
                        qk[:, a, 0:HA, :].rearrange("p h d -> p (h d)"), ps[:, 2 + a, 0:HA * QK], ACT.Copy).then_inc(act_done, act_p.step(("q_read", l)))
                rstd_of(stat[:, 18:34], stat[:, 34:50], ("mla", l))
                rstd_of(stat[:, 50:70], stat[:, 70:90], ("swa", l))
                cols_out(l, 3)
                act.wait_ge(pe_done, at(("swa_k_T", l)))
                nc.scalar.activation(swa_kT[:], ps[:, 2, 0:T], ACT.Copy, scale=G("swa_k_g", l)).then_inc(act_done, act_p.step(("swa_kT", l)))
                act.wait_ge(pe_done, at(("stick_T", l, 0)))
                nc.scalar.activation(stick_qT[:].rearrange("p j t -> p (j t)"), ps[:, 4, :], ACT.Copy,
                                                scale=HD ** -0.5).then_inc(act_done, act_p.step(("stickT", l, 0)))
                for j in (0, 2):
                    act.wait_ge(pe_done, at(("mla_T", l, j)))
                    nc.scalar.activation(mla_T[0:QK, 2 * j:2 * j + 2, :].rearrange("p h t -> p (h t)"),
                                                    ps[0:QK, (6, 7, 3, 2)[j], :], ACT.Copy).then_inc(act_done, act_p.step(("mlaT", l, j)))
                for h in range(HC):
                    act.wait_ge(pe_done, at(("z", l, h)))
                    if h == 0:
                        act.wait_ge(act_done, counts.own(act_p))
                    nc.scalar.activation(stick[:, h, :], ps[:, 4 + h, 0:SEG], ACT.Abs).then_inc(act_done, act_p.step())
                    act.wait_ge(act_done, counts.own(act_p))
                    nc.scalar.activation(stick[:, h, :], stick[:, h, :], ACT.Exp, scale=-1.0).then_inc(act_done, act_p.step())
                    act.wait_ge(act_done, counts.own(act_p))
                    nc.scalar.activation(stick[:, h, :], stick[:, h, :], ACT.Ln, bias=1.0).then_inc(act_done, act_p.step(("ln", l, h)))

                def exps(slot, nm, acc, key):
                    nc.scalar.activation(S[:, slot, 0:P], S[:, slot, 0:P], ACT.Exp, bias=nm[0],
                                                    accum_out=acc[0]).then_inc(act_done, act_p.step())
                    nc.scalar.activation(S[:, slot, P:SEG], S[:, slot, P:SEG], ACT.Exp, bias=nm[1],
                                                    accum_out=acc[1]).then_inc(act_done, act_p.step(key))

                def head_cols(base, h):
                    return [stat_a[:, base + 8 * (h // 4) + 4 * a + h % 4:base + 8 * (h // 4) + 4 * a + h % 4 + 1]
                            for a in range(TT)]

                act.wait_ge(dve_done, at(("nmA", l)))
                for h in range(HA):
                    exps(h, head_cols(24, h), head_cols(48, h), ("pA", l, h))
                for h in range(HC):
                    act.wait_ge(dve_done, at(("w_read", l, h)))
                    nc.scalar.activation(stick[:, h, :], stick[:, h, :], ACT.Exp).then_inc(act_done, act_p.step(("aC", l, h)))
                for h in (0, 2):
                    act.wait_ge(pe_done, at(("pA_T", l, h)))
                    nc.scalar.activation(probsT[:, h, :], ps[:, 4 + h, 0:SEG], ACT.Copy).then_inc(act_done, act_p.step(("pTA", l, h)))
                for q in range(2):
                    act.wait_ge(dve_done, at(("nmB", l, q)))
                    for h in range(4 * q, 4 * q + 4):
                        exps((4 + h) % 8, head_cols(32, h), head_cols(56, h), ("pB", l, h))
                    nc.scalar.activation(stat_a[:, 72 + 8 * q:80 + 8 * q], stat_a[:, 72 + 8 * q:80 + 8 * q],
                                                    ACT.Exp).then_inc(act_done, act_p.step(("sink_e", l, q)))
                    for h in (4 * q, 4 * q + 2):
                        act.wait_ge(pe_done, at(("pB_T", l, h)))
                        if q == 0:
                            act.wait_ge(pe_done, at(("oA", l, h)))
                        else:
                            act.wait_ge(pe_done, at(("oB", l, h - 4)))
                        nc.scalar.activation(probsT[:, h % 4, :], ps[:, (6, 7, 0, 1, 3, 6, 7, 0)[h], 0:SEG],
                                                        ACT.Copy).then_inc(act_done, act_p.step(("pTB", l, h)))
                act.wait_ge(dve_done, at(("oB_read", l, 1)))
                act.wait_ge(act_done, counts.own(act_p))
                act.wait_ge(pe_done, at(("oC", l, HC - 1)))
                for a in range(TT):
                    for i, (c0, w) in enumerate(((0, 256), (256, 512), (768, 256))):
                        if a or i:
                            act.wait_ge(act_done, counts.own(act_p))
                        nc.scalar.activation(junk[:, 0:w], mixed[:, a, c0:c0 + w], ACT.Square,
                                                        scale=w ** -0.5,
                                                        accum_out=stat[:, 3 * a + i:3 * a + i + 1]).then_inc(act_done, act_p.step(("mix_sq", l)))
                rstd_of(stat[:, 6:12], stat[:, 12:18], ("mix", l))
                act.wait_ge(pe_done, at(("oB", l, HB - 1)))
                transposed_out(l, "mix_n", G("out_g", l))
                row_stats(l, "ffn_n")
                act.wait_ge(unit_used, at(("proj", l, 1, 1)))
                transposed_out(l, "ffn_n", G("ffn_g", l))

            def dense(l):
                for f in range(FF // P):
                    last = f % 4 == 3 or f == FF // P - 1
                    act.wait_ge(unit_used if last else pe_done, at(("up", l, f)))
                    if f >= 4:
                        act.wait_ge(dve_done, at(("gated", l, f - 4)))
                    nc.scalar.activation(sig_d[:, f % 4, :], ps[:, f % 4, 0:T], ACT.Sigmoid).then_inc(act_done, act_p.step(("sig", l, f)))

            def experts(g):
                def gathered(key, it=None):
                    if it is not None:
                        act.wait_ge(unit_used, at((g, "u", NCH - 1), it))
                    else:
                        act.wait_ge(dve_done, at((g, "pass")))
                    for n in range(2):
                        act.wait_ge(pe_done, at((g, key, "gathered", n), it))
                        for k in range(4):
                            q = 4 * n + k
                            nc.scalar.activation(xgT[:, q, :], ps[:, 6 + n, k * P:(k + 1) * P], ACT.Copy,
                                                            scale=G("ffn_g", DEPTH - 1)[:, q:q + 1]).then_inc(act_done, act_p.step((g, key, "xgT", n) if k == 3 else None))

                gathered("first")
                act_p.enter(("experts", g))
                with act.Fori(0, NE) as e:
                    for c in range(NCH):
                        act.wait_ge(unit_used, at((g, "g", c), e))
                        act.wait_ge(dve_done, at((g, "hid", c - 2 if c >= 2 else NCH - 2 + (1 if c == 0 else 0)), e, 0 if c >= 2 else 1))
                        nc.scalar.activation(sig[:, c % 2, :], ps[:, c % 2, :], ACT.Sigmoid).then_inc(act_done, act_p.step((g, "sig", c)))
                        if c == 0:
                            act.wait_ge(pe_done, at((g, "pick_g_T"), e))
                            nc.scalar.activation(pick_gT.rearrange("p a s -> p (a s)"), ps[:, 6, 0:2 * P],
                                                            ACT.Copy).then_inc(act_done, act_p.step((g, "pick_gT")))
                        else:
                            hidden_out(act, g, c - 1, e)
                    hidden_out(act, g, NCH - 1, e)
                    gathered("next", e)
                    act.wait_ge(unit_used, at((g, "d", NCH - 1), e))
                    for n in range(2):
                        nc.scalar.activation(ysb[:, n * CH:(n + 1) * CH], ps[:, 4 + n, :], ACT.Copy).then_inc(act_done, act_p.step((g, "y_out")))
                act_p.leave(NE)

            def hidden_out(act, g, c, e):
                act.wait_ge(pe_done, at((g, "hid_T", c), e))
                act.wait_ge(unit_used, at((g, "d", c - 2 if c >= 2 else NCH - 2 + (1 if c == 0 else 0)), e, 0 if c >= 2 else 1))
                nc.scalar.activation(hidT[:, c % 2, :], ps[:, 7 if c % 2 == 0 else 6, :], ACT.Copy).then_inc(act_done, act_p.step((g, "hidT", c)))

            layer_mixers(0)
            dense(0)
            layer_mixers(1)
            act.wait_ge(dve_done, at("gap"))
            nc.scalar.activation(stat_a[:, 36:38], stat_a[:, 32:34], ACT.Exp, scale=-1.0).then_inc(act_done, act_p.step("first_gate"))
            experts(0)
            more = act.value_load(over_i[0:1, 0:1], min_val=0, max_val=1)
            with act.If(more > 0):
                experts(1)

        @block.vector
        def _(dve):
            def own(it=None):
                return counts.own(dve_p, it)

            def refine(v, r, t, key):
                dve.wait_ge(act_done, at((key, "r0")))
                nc.vector.scalar_tensor_tensor(t, r, -0.5, r, ALU.mult, ALU.mult).then_inc(dve_done, dve_p.step())
                dve.wait_ge(dve_done, own())
                nc.vector.tensor_tensor(t, t, v, ALU.mult).then_inc(dve_done, dve_p.step())
                dve.wait_ge(dve_done, own())
                nc.vector.scalar_tensor_tensor(r, t, 1.5, r, ALU.add, ALU.mult).then_inc(dve_done, dve_p.step())
                dve.wait_ge(dve_done, own())

            def row_norm(l, what):
                dve.wait_ge(act_done, at((what, l, "sq", 1)))
                nc.vector.tensor_scalar(stat[:, 2:4], stat[:, 0:2], EPS, None, ALU.add).then_inc(dve_done, dve_p.step(((what, l), "ms")))
                dve.wait_ge(dve_done, own())
                refine(stat[:, 2:4], stat[:, 4:6], stat[:, 90:92], (what, l))
                for a in range(TT):
                    nc.vector.tensor_scalar(xn[:, a, :], xres[:, a, :], stat[:, 4 + a:5 + a], None,
                                                       ALU.mult).then_inc(dve_done, dve_p.step((what, l, a)))

            def transposed_out(l, what, gain):
                for b in (2, 3):
                    dve.wait_ge(pe_done, at((what + "_T", l, b)))
                    for i in range(2):
                        k = 2 * b + i
                        nc.vector.tensor_scalar(hT[:, k, :], ps[:, b, i * T:(i + 1) * T], gain[:, k:k + 1],
                                                           None, ALU.mult).then_inc(dve_done, dve_p.step((what + "_done", l, b) if i else None))

            def cols_out(l, n):
                a0, w = COL_CHUNKS[n]
                dve.wait_ge(pe_done, at(("cols", l, n, 0)))
                nc.vector.tensor_copy(cols[:, 0, a0:a0 + w], ps[:, 4 + (n * 2) % 4, 0:w]).then_inc(dve_done, dve_p.step(("cols_sb", l, n, 0)))

            def layer_mixers(l):
                row_norm(l, "attn_n")
                if l == 0:
                    dve.wait_ge(small_loaded, 16)
                    dve.wait_ge(const_loaded, 16)
                transposed_out(l, "attn_n", G("attn_g", l))
                cols_out(l, 0)
                dve.wait_ge(act_done, at(("cq_sq", l, 3)))
                nc.vector.tensor_scalar(stat[:, 10:14], stat[:, 6:10], EPS, None, ALU.add).then_inc(dve_done, dve_p.step((("cq", l), "ms")))
                dve.wait_ge(dve_done, own())
                refine(stat[:, 10:14], stat[:, 14:18], stat[:, 90:94], ("cq", l))
                for a in range(TT):
                    for i, (c0, w) in enumerate(((0, QR), (C_CKV, KVR))):
                        nc.vector.tensor_scalar(cols[:, a, c0:c0 + w], cols[:, a, c0:c0 + w],
                                                           stat[:, 14 + 2 * a + i:15 + 2 * a + i], None, ALU.mult).then_inc(dve_done, dve_p.step(("cq_n", l)))
                cols_out(l, 1)
                dve.wait_ge(pe_done, at(("cq_T", l)))
                for c in range(2):
                    nc.vector.tensor_scalar(cqT[:, c, :], ps[:, 0, c * T:(c + 1) * T],
                                                       G("cq_g", l)[:, c:c + 1], None, ALU.mult).then_inc(dve_done, dve_p.step())
                nc.vector.tensor_scalar(ckvT, ps[:, 1, 0:T], G("ckv_g", l), None, ALU.mult).then_inc(dve_done, dve_p.step(("cqT", l)))
                cols_out(l, 2)
                dve.wait_ge(pe_done, at(("up_proj", l)))
                dve.wait_ge(act_done, at(("q_read", l)))
                dve.wait_ge(act_done, at(("cols_sb", l, 0, 1)))
                for a in range(TT):
                    kv = ps[:, a, :].rearrange("p (h d) -> p h d", h=HA)
                    nc.vector.tensor_copy(qk[:, a, HA:, 0:NOPE], kv[:, :, 0:NOPE]).then_inc(dve_done, dve_p.step())
                    nc.vector.tensor_copy(mla_v[:, a, :].rearrange("p (h d) -> p h d", h=HA),
                                                     kv[:, :, NOPE:]).then_inc(dve_done, dve_p.step(("kv_read", l)))
                    nc.vector.tensor_copy(
                        qk[:, a, HA:, NOPE:],
                        cols[:, a, C_KPE:C_BQ].rearrange("p (o d) -> p o d", o=1).broadcast_to([P, HA, ROPE])).then_inc(dve_done, dve_p.step())
                dve.wait_ge(dve_done, own())
                qkf = qk.rearrange("p a h d -> p (a h d)")
                qkg = qk.rearrange("p a h d -> p (a h) d")
                nc.vector.tensor_tensor(mla_sq, qkf, qkf, ALU.mult).then_inc(dve_done, dve_p.step())
                dve.wait_ge(dve_done, own())
                nc.vector.tensor_reduce(stat[:, 18:34], mla_sq.rearrange("p (g d) -> p g d", d=QK), AX.X,
                                              ALU.add).then_inc(dve_done, dve_p.step())
                dve.wait_ge(dve_done, own())
                nc.vector.tensor_scalar(stat[:, 18:34], stat[:, 18:34], 1.0 / QK, EPS, ALU.mult, ALU.add).then_inc(dve_done, dve_p.step((("mla", l), "ms")))
                dve.wait_ge(dve_done, own())
                dve.wait_ge(act_done, at(("cols_sb", l, 1, 1)))
                dve.wait_ge(act_done, at(("cols_sb", l, 2, 1)))
                swa = cols[:, :, C_BQ:C_BV]
                sq3 = swa_sq.rearrange("p (a n) -> p a n", a=TT)
                nc.vector.tensor_tensor(sq3, swa, swa, ALU.mult).then_inc(dve_done, dve_p.step())
                dve.wait_ge(dve_done, own())
                nc.vector.tensor_reduce(stat[:, 50:70], swa_sq.rearrange("p (g d) -> p g d", d=HD), AX.X,
                                              ALU.add).then_inc(dve_done, dve_p.step())
                dve.wait_ge(dve_done, own())
                nc.vector.tensor_scalar(stat[:, 50:70], stat[:, 50:70], 1.0 / HD, EPS, ALU.mult, ALU.add).then_inc(dve_done, dve_p.step((("swa", l), "ms")))
                dve.wait_ge(dve_done, own())
                refine(stat[:, 18:34], stat[:, 34:50], stat_t[:, 0:16], ("mla", l))
                nc.vector.tensor_tensor(stat[:, 34:50], stat[:, 34:50], C("mla_scale"), ALU.mult).then_inc(dve_done, dve_p.step())
                dve.wait_ge(dve_done, own())
                nc.vector.tensor_tensor(qkg, qkg,
                                              stat[:, 34:50].rearrange("p (g o) -> p g o", o=1).broadcast_to(
                                                  [P, 16, QK]), ALU.mult).then_inc(dve_done, dve_p.step())
                dve.wait_ge(dve_done, own())
                for a in range(TT):
                    for i, name in enumerate(("qn_g", "kn_g")):
                        part = qk[:, a, i * HA:(i + 1) * HA, :]
                        nc.vector.tensor_tensor(part, part, G(name, l).rearrange(
                            "p (o d) -> p o d", o=1).broadcast_to([P, HA, QK]), ALU.mult).then_inc(dve_done, dve_p.step())
                dve.wait_ge(dve_done, own())
                x1, x2 = qk[:, :, :, NOPE:NOPE + 16], qk[:, :, :, NOPE + 16:QK]
                cos = C("cos").rearrange("p (a o d) -> p a o d", a=TT, o=1).broadcast_to([P, TT, 2 * HA, 16])
                sin = C("sin").rearrange("p (a o d) -> p a o d", a=TT, o=1).broadcast_to([P, TT, 2 * HA, 16])
                for n, (u, v) in enumerate(((x1, cos), (x2, sin), (x1, sin), (x2, cos))):
                    nc.vector.tensor_tensor(rope_t[:, n], u, v, ALU.mult).then_inc(dve_done, dve_p.step())
                dve.wait_ge(dve_done, own())
                nc.vector.tensor_tensor(x1, rope_t[:, 0], rope_t[:, 1], ALU.subtract).then_inc(dve_done, dve_p.step())
                nc.vector.tensor_tensor(x2, rope_t[:, 2], rope_t[:, 3], ALU.add).then_inc(dve_done, dve_p.step(("mla_n", l)))
                refine(stat[:, 50:70], stat[:, 70:90], stat_t[:, 0:20], ("swa", l))
                nc.vector.tensor_tensor(stat[:, 70:90], stat[:, 70:90], C("swa_scale"), ALU.mult).then_inc(dve_done, dve_p.step())
                dve.wait_ge(dve_done, own())
                for a in range(TT):
                    r = stat[:, 70 + 10 * a:78 + 10 * a].rearrange("p (g i o) -> p i g o", g=2, o=1)
                    nc.vector.tensor_tensor(
                        swa_q[:, a, :].rearrange("p (i g d) -> p i g d", i=4, g=2),
                        cols[:, a, C_BQ:C_BK].rearrange("p (g i d) -> p i g d", g=2, i=4),
                        r.broadcast_to([P, 4, 2, HD]), ALU.mult).then_inc(dve_done, dve_p.step())
                    part = cols[:, a, C_BK:C_BV].rearrange("p (g d) -> p g d", d=HD)
                    r = stat[:, 78 + 10 * a:80 + 10 * a].rearrange("p (g o) -> p g o", o=1)
                    nc.vector.tensor_tensor(part, part, r.broadcast_to([P, HKV, HD]), ALU.mult).then_inc(dve_done, dve_p.step(("swa_n", l)))
                cols_out(l, 3)
                for b in range(2):
                    dve.wait_ge(pe_done, at(("swa_q_T", l, b)))
                    nc.vector.tensor_scalar(swa_qT[:, 2 * b:2 * b + 2, :].rearrange("p i t -> p (i t)"),
                                                       ps[:, b, :], G("swa_q_g", l), None, ALU.mult).then_inc(dve_done, dve_p.step(("swaT", l)))
                dve.wait_ge(pe_done, at(("stick_T", l, 1)))
                nc.vector.tensor_copy(stick_kT[:].rearrange("p j t -> p (j t)"), ps[:, 5, :]).then_inc(dve_done, dve_p.step(("stickT", l, 1)))
                for j in (1, 3):
                    dve.wait_ge(pe_done, at(("mla_T", l, j)))
                    nc.vector.tensor_copy(mla_T[0:QK, 2 * j:2 * j + 2, :].rearrange("p h t -> p (h t)"),
                                                     ps[0:QK, (6, 7, 3, 2)[j], :]).then_inc(dve_done, dve_p.step(("mlaT", l, j)))

                def head_max(slot, bank, bias, scale, at, h, key):
                    for a, (c0, c1) in enumerate(((0, P), (P, SEG))):
                        nc.vector.tensor_tensor_reduce(
                            out=S[:, slot, c0:c1], in0=ps[:, bank, c0:c1], in1=bias[:, c0:c1], scale=scale,
                            scalar=-3e38, op0=ALU.add, op1=ALU.max,
                            accum_out=stat_a[:, at + 8 * (h // 4) + 4 * a + h % 4:
                                             at + 8 * (h // 4) + 4 * a + h % 4 + 1]).then_inc(dve_done, dve_p.step(key))

                def softplus(h):
                    dve.wait_ge(act_done, at(("ln", l, h)))
                    nc.vector.scalar_tensor_tensor(stick[:, h, :], ps[:, 4 + h, 0:SEG], 0.0, stick[:, h, :],
                                                         ALU.max, ALU.add).then_inc(dve_done, dve_p.step())
                    dve.wait_ge(dve_done, own())
                    nc.vector.tensor_tensor(stick[:, h, :], stick[:, h, :], C("stick_mul"), ALU.mult).then_inc(dve_done, dve_p.step(("sp", l, h)))

                for h in range(HA):
                    dve.wait_ge(pe_done, at(("sA", l, h)))
                    head_max(h, h, C("causal"), 1.0, 0, h, ("sA_read", l, h))
                dve.wait_ge(dve_done, own())
                nc.vector.tensor_scalar(stat_a[:, 24:32], stat_a[:, 0:8], -1.0, None, ALU.mult).then_inc(dve_done, dve_p.step(("nmA", l)))
                for h in range(HC):
                    softplus(h)

                def swa_max(q):
                    for h in range(4 * q, 4 * q + 4):
                        dve.wait_ge(pe_done, at(("sB", l, h)))
                        if q:
                            dve.wait_ge(pe_done, at(("pA_T", l, h - 4)))
                        head_max((4 + h) % 8, h % 4, C("negdist"), 2.0 ** -(h + 1), 8, h, ("sB_read", l, h))
                    dve.wait_ge(dve_done, own())
                    sink = G("sinks", l)[:, 4 * q:4 * q + 4].rearrange("p (o h) -> p o h", o=1).broadcast_to([P, TT, 4])

                    def by_tile(c0):
                        return stat_a[:, c0 + 8 * q:c0 + 8 * q + 8].rearrange("p (a h) -> p a h", a=TT)
                    nc.vector.tensor_tensor(by_tile(8), by_tile(8), sink, ALU.max).then_inc(dve_done, dve_p.step())
                    dve.wait_ge(dve_done, own())
                    nc.vector.tensor_scalar(by_tile(32), by_tile(8), -1.0, None, ALU.mult).then_inc(dve_done, dve_p.step())
                    dve.wait_ge(dve_done, own())
                    nc.vector.tensor_tensor(by_tile(72), by_tile(32), sink, ALU.add).then_inc(dve_done, dve_p.step(("nmB", l, q)))

                swa_max(0)
                for h in range(HC):
                    dve.wait_ge(pe_done, at(("cum", l, h)))
                    nc.vector.tensor_tensor(stick[:, h, :], ps[:, 4 + h, 0:SEG], C("stick_add"), ALU.add).then_inc(dve_done, dve_p.step(("w_read", l, h)))
                for h in (1, 3):
                    dve.wait_ge(pe_done, at(("pA_T", l, h)))
                    nc.vector.tensor_copy(probsT[:, h, :], ps[:, 4 + h, 0:SEG]).then_inc(dve_done, dve_p.step(("pTA", l, h)))
                swa_max(1)

                def heads_out(bank, den, c0, key):
                    o = mixed[:, :, c0:c0 + 256].rearrange("p a (h d) -> p a h d", h=4)
                    i = ps[:, bank, :].rearrange("p (a h d) -> p a h d", a=TT, h=4)
                    d = den.rearrange("p (a h o) -> p a h o", a=TT, o=1).broadcast_to([P, TT, 4, HD])
                    nc.vector.tensor_tensor(o, i, d, ALU.mult).then_inc(dve_done, dve_p.step(key))

                dve.wait_ge(act_done, at(("pA", l, HA - 1)))
                nc.vector.reciprocal(stat_a[:, 0:8], stat_a[:, 48:56]).then_inc(dve_done, dve_p.step())
                dve.wait_ge(dve_done, own())
                dve.wait_ge(pe_done, at(("oA", l, HA - 1)))
                heads_out(4, stat_a[:, 0:8], 0, ("oA_read", l))
                dve.wait_ge(pe_done, at(("oC", l, HC - 1)))
                nc.vector.tensor_copy(mixed[:, :, 768:1024],
                                                 ps[:, 5, :].rearrange("p (a n) -> p a n", a=TT)).then_inc(dve_done, dve_p.step(("oC_read", l)))
                for q in range(2):
                    for h in (4 * q + 1, 4 * q + 3):
                        dve.wait_ge(pe_done, at(("pB_T", l, h)))
                        dve.wait_ge(pe_done, at(("oA", l, h) if q == 0 else ("oB", l, h - 4)))
                        nc.vector.tensor_copy(probsT[:, h % 4, :],
                                                         ps[:, (6, 7, 0, 1, 3, 6, 7, 0)[h], 0:SEG]).then_inc(dve_done, dve_p.step(("pTB", l, h)))
                    dve.wait_ge(act_done, at(("sink_e", l, q)))
                    den = stat_a[:, 8 + 8 * q:16 + 8 * q]
                    nc.vector.tensor_tensor(den, stat_a[:, 56 + 8 * q:64 + 8 * q],
                                                  stat_a[:, 72 + 8 * q:80 + 8 * q], ALU.add).then_inc(dve_done, dve_p.step())
                    dve.wait_ge(dve_done, own())
                    nc.vector.reciprocal(den, den).then_inc(dve_done, dve_p.step())
                    dve.wait_ge(dve_done, own())
                    dve.wait_ge(pe_done, at(("oB", l, 4 * q + 3)))
                    heads_out(2 if q == 0 else 1, den, 256 + 256 * q, ("oB_read", l, q))
                dve.wait_ge(act_done, at(("mix_sq", l)))
                nc.vector.tensor_scalar(stat[:, 6:12], stat[:, 0:6], EPS, None, ALU.add).then_inc(dve_done, dve_p.step((("mix", l), "ms")))
                dve.wait_ge(dve_done, own())
                refine(stat[:, 6:12], stat[:, 12:18], stat[:, 90:96], ("mix", l))
                for a in range(TT):
                    for i, (c0, w) in enumerate(((0, 256), (256, 512), (768, 256))):
                        nc.vector.tensor_scalar(mixed[:, a, c0:c0 + w], mixed[:, a, c0:c0 + w],
                                                           stat[:, 12 + 3 * a + i:13 + 3 * a + i], None, ALU.mult).then_inc(dve_done, dve_p.step(("mix_n", l, a)))
                dve.wait_ge(pe_done, at(("oB", l, HB - 1)))
                transposed_out(l, "mix_n", G("out_g", l))
                for n in range(2):
                    for a in range(TT):
                        dve.wait_ge(unit_used if a else pe_done, at(("proj", l, n, a)))
                        part = xres[:, a, n * CH:(n + 1) * CH]
                        nc.vector.tensor_tensor(part, ps[:, 4 + 2 * n + a, :], part, ALU.add).then_inc(dve_done, dve_p.step(("proj_add", l, 2 * n + a)))
                row_norm(l, "ffn_n")
                dve.wait_ge(unit_used, at(("proj", l, 1, 1)))
                transposed_out(l, "ffn_n", G("ffn_g", l))

            def dense(l):
                tiles = FF // P
                for f in range(tiles):
                    dve.wait_ge(act_done, at(("sig", l, f)))
                    nc.vector.tensor_tensor(gated_d, ps[:, f % 4, 0:T], sig_d[:, f % 4, :], ALU.mult).then_inc(dve_done, dve_p.step(("gated", l, f)))
                    dve.wait_ge(dve_done, own())
                    if f >= 4:
                        g = f - 4
                        dve.wait_ge(unit_used if g % 4 == 3 else pe_done, at(("down", l, g)))
                    nc.vector.tensor_tensor(hid_d[:, f % 4, :], ps[:, f % 4, T:2 * T], gated_d, ALU.mult).then_inc(dve_done, dve_p.step(("hidden", l, f)))
                    dve.wait_ge(dve_done, own())
                dve.wait_ge(unit_used, at(("down", l, tiles - 1)))
                for a in range(TT):
                    for n in range(2):
                        part = xres[:, a, n * CH:(n + 1) * CH]
                        nc.vector.tensor_tensor(part, ps[:, 4 + 2 * a + n, :], part, ALU.add).then_inc(dve_done, dve_p.step(("ffn_add", l)))

            def route():
                iota8 = C("iota")[:, 0:NE]
                nc.vector.memset(rankm[:], -1.0).then_inc(dve_done, dve_p.step())
                dve.wait_ge(dve_done, own())
                nc.vector.memset(gates[:], 0.0).then_inc(dve_done, dve_p.step())
                dve.wait_ge(dve_done, own())
                dve.wait_ge(pe_done, at("logits"))
                logits = stat_a[:, 0:16].rearrange("p (a n) -> p a n", a=TT)
                nc.vector.tensor_copy(stat_a[:, 0:16], ps[:, 4, 0:2 * NE]).then_inc(dve_done, dve_p.step())
                dve.wait_ge(dve_done, own())
                for a in range(TT):
                    nc.vector.max(top[:, a, :], logits[:, a, :]).then_inc(dve_done, dve_p.step())
                    dve.wait_ge(dve_done, own())
                    nc.vector.max_index(top_at[:, a, :], top[:, a, :], logits[:, a, :]).then_inc(dve_done, dve_p.step())
                    dve.wait_ge(dve_done, own())
                found = stat_a[:, 16:32].rearrange("p (a n) -> p a n", a=TT)
                nc.vector.tensor_copy(found, top_at[:]).then_inc(dve_done, dve_p.step())
                dve.wait_ge(dve_done, own())
                gap = stat_a[:, 32:34].rearrange("p (a o) -> p a o", a=TT)
                nc.vector.tensor_tensor(gap, top[:, :, 0:1], top[:, :, 1:2], ALU.subtract).then_inc(dve_done, dve_p.step("gap"))
                dve.wait_ge(dve_done, own())
                dve.wait_ge(act_done, at("first_gate"))
                g1, g2 = stat_a[:, 34:36], stat_a[:, 36:38]
                nc.vector.tensor_scalar(stat_a[:, 38:40], g2, 1.0, None, ALU.add).then_inc(dve_done, dve_p.step())
                dve.wait_ge(dve_done, own())
                nc.vector.reciprocal(g1, stat_a[:, 38:40]).then_inc(dve_done, dve_p.step())
                dve.wait_ge(dve_done, own())
                nc.vector.tensor_tensor(g2, g2, g1, ALU.mult).then_inc(dve_done, dve_p.step())
                dve.wait_ge(dve_done, own())
                one = stat_a[:, 40:72].rearrange("p (i a n) -> p i a n", i=2, a=TT)
                for a in range(TT):
                    for i in range(2):
                        nc.vector.tensor_scalar(one[:, i, a, :], iota8, found[:, a, i:i + 1], None, ALU.is_equal).then_inc(dve_done, dve_p.step())
                        dve.wait_ge(dve_done, own())
                nc.vector.tensor_tensor(sel[:], one[:, 0], one[:, 1], ALU.add).then_inc(dve_done, dve_p.step("selected"))
                dve.wait_ge(dve_done, own())
                for a in range(TT):
                    nc.vector.tensor_scalar(one[:, 0, a, :], one[:, 0, a, :], g1[:, a:a + 1], None, ALU.mult).then_inc(dve_done, dve_p.step())
                    dve.wait_ge(dve_done, own())
                    nc.vector.scalar_tensor_tensor(gates[:, a, 0:NE], one[:, 1, a, :], g2[:, a:a + 1],
                                                         one[:, 0, a, :], ALU.mult, ALU.add).then_inc(dve_done, dve_p.step())
                    dve.wait_ge(dve_done, own())
                dve.wait_ge(pe_done, at("ranks"))
                nc.vector.scalar_tensor_tensor(rankm[:, :, 0:NE],
                                                     ps[:, 5, 0:2 * NE].rearrange("p (a n) -> p a n", a=TT), 1.0,
                                                     sel[:], ALU.add, ALU.mult).then_inc(dve_done, dve_p.step())
                dve.wait_ge(dve_done, own())
                nc.vector.tensor_scalar(rankm[:, :, 0:NE], rankm[:, :, 0:NE], -1.0, None, ALU.add).then_inc(dve_done, dve_p.step())
                dve.wait_ge(dve_done, own())
                nc.vector.tensor_reduce(over[:, 0:1], ps[:, 5, 2 * NE:3 * NE], AX.X, ALU.max).then_inc(dve_done, dve_p.step())
                dve.wait_ge(dve_done, own())
                nc.vector.tensor_scalar(over[:, 1:2], over[:, 0:1], float(GROUP), None, ALU.is_gt).then_inc(dve_done, dve_p.step())
                dve.wait_ge(dve_done, own())
                nc.vector.tensor_copy(over_i[0:1, 0:1], over[0:1, 1:2]).then_inc(dve_done, dve_p.step("overflow"))
                dve.wait_ge(dve_done, own())

            def experts(g):
                slots = C("iota")[:, g * GROUP:(g + 1) * GROUP]

                def picks(key, e):
                    for a in range(TT):
                        r = rankm[:, a, 0:1] if e is None else rankm[:, a, bass.ds(e + 1, 1)]
                        w = gates[:, a, 0:1] if e is None else gates[:, a, bass.ds(e + 1, 1)]
                        nc.vector.tensor_scalar(pick[:, a, :], slots, r, None, ALU.is_equal).then_inc(dve_done, dve_p.step())
                        nc.vector.tensor_scalar(pick_g[:, a, :], slots, r, w, ALU.is_equal, ALU.mult).then_inc(dve_done, dve_p.step((g, key, "pick")))

                def add(it, key):
                    for q in range(4):
                        dve.wait_ge(pe_done, at((g, "scatter" + key, q), it))
                        a, n = q // 2, q % 2
                        part = xres[:, a, n * CH:(n + 1) * CH]
                        nc.vector.tensor_tensor(part, ps[:, 6 + n, :], part, ALU.add).then_inc(dve_done, dve_p.step((g, "add" + key, q)))

                if g:
                    dve.wait_ge(pe_done, at((0, "scatter_end", 3)))
                nc.vector.memset(ysb, 0.0).then_inc(dve_done, dve_p.step())
                nc.vector.memset(pick_gT.rearrange("p a s -> p (a s)"), 0.0).then_inc(dve_done, dve_p.step((g, "pass")))
                picks("first", None)
                dve.wait_ge(dve_done, own())
                dve_p.enter(("experts", g))
                with dve.Fori(0, NE) as e:
                    for c in range(NCH):
                        dve.wait_ge(act_done, at((g, "sig", c), e))
                        nc.vector.tensor_tensor(gated, ps[:, c % 2, :], sig[:, c % 2, :], ALU.mult).then_inc(dve_done, dve_p.step((g, "gated", c)))
                        if c == 0:
                            add(e, "")
                        dve.wait_ge(dve_done, own(e))
                        dve.wait_ge(unit_used, at((g, "u", c), e))
                        if c >= 2:
                            dve.wait_ge(pe_done, at((g, "hid_T", c - 2), e))
                        nc.vector.tensor_tensor(hid[:, c % 2, :], ps[:, 2 + c % 2, :], gated, ALU.mult).then_inc(dve_done, dve_p.step((g, "hid", c)))
                        if c == NCH - 2:
                            dve.wait_ge(pe_done, at((g, "pick_g_T"), e))
                            picks("next", e)
                        dve.wait_ge(dve_done, own(e))
                dve_p.leave(NE)
                add(None, "_end")
                dve.wait_ge(dve_done, own())

            layer_mixers(0)
            dense(0)
            layer_mixers(1)
            route()
            experts(0)
            more = dve.value_load(over_i[0:1, 0:1], min_val=0, max_val=1)
            with dve.If(more > 0):
                experts(1)
            nc.vector.memset(over[0:1, 2:3], 0.0).then_inc(result_ready, 1)

    return marks


def constants():
    c = np.zeros((P, N_CONST), np.float32)

    def put(name, value):
        a, w = CONST[name]
        c[:, a:a + w] = np.reshape(value, (-1, w))

    p = np.arange(P)[:, None]
    n = np.arange(P)[None, :]
    put("ident", p == n)
    half = ROPE // 2
    inv = (np.float32(10000.0) ** (-np.arange(half, dtype=np.float32) / np.float32(half))).astype(np.float32)
    pos = (np.arange(TT)[None, :] * P + p).astype(np.float32)
    ang = (pos[:, :, None] * inv).astype(np.float32)
    put("cos", np.cos(ang))
    put("sin", np.sin(ang))
    dist = np.concatenate([p - n, p + P - np.arange(T)[None, :]], 1)
    put("causal", np.where(dist >= 0, 0.0, NEG))
    put("negdist", np.where((dist >= 0) & (dist < P), -dist, NEG))
    before = np.concatenate([p < np.arange(T)[None, :], p < n], 1)
    put("stick_add", np.where(before, 0.0, NEG))
    put("stick_mul", before)
    put("neg_tri", -(p >= n).astype(np.float32))
    put("neg_ones", -1.0 * np.ones((P, P)))
    put("ones", np.ones((P, P)))
    put("rank_tri", p < n)
    put("iota", np.broadcast_to(np.arange(2 * GROUP), (P, 2 * GROUP)))
    swa = [HD ** -0.5 * 2.0 ** (h + 1) for h in range(HB)] + [1.0] * HKV
    put("swa_scale", np.broadcast_to(np.tile(swa, TT), (P, TT * (HB + HKV))))
    put("mla_scale", np.broadcast_to(np.tile([QK ** -0.5] * HA + [1.0] * HA, TT), (P, TT * 2 * HA)))
    return c


def small_weights(i):
    s = np.zeros((P, N_SMALL), np.float32)
    for l in range(DEPTH):
        for name, v in (("attn_g", i["attn_norm_g"][l]), ("ffn_g", i["ffn_norm_g"][l]), ("out_g", i["out_norm_g"][l]),
                        ("cq_g", i["mla_cq_norm_g"][l]), ("ckv_g", i["mla_ckv_norm_g"][l])):
            a, w = SMALL[name, l]
            s[:, a:a + w] = v.reshape(w, P).T
        for name, v in (("swa_q_g", i["swa_qn_g"][l]), ("swa_k_g", i["swa_kn_g"][l])):
            a, _ = SMALL[name, l]
            s[:, a] = np.concatenate([v, v])
        for name, v in (("qn_g", i["mla_qn_g"][l]), ("kn_g", i["mla_kn_g"][l]), ("sinks", i["swa_sinks"][l])):
            a, w = SMALL[name, l]
            s[:, a:a + w] = v[None, :]
    a, w = SMALL["router"]
    s[:, a:a + w] = i["router_w"][0].reshape(KD, P, NE).transpose(1, 0, 2).reshape(P, w)
    return s


def kernel(**inputs):
    import concourse.bacc as bacc
    from concourse.bass_utils import run_bass_kernel_spmd

    arrays = {name: np.ascontiguousarray(inputs[key]) for name, key in (
        ("x", "x"), ("w_in", "w_in"), ("w_uq", "mla_w_uq"), ("w_ukv", "mla_w_ukv"), ("w_out", "w_out"),
        ("dense_g", "dense_w_gate"), ("dense_u", "dense_w_up"), ("dense_d", "dense_w_down"),
        ("moe_g", "moe_w_gate"), ("moe_u", "moe_w_up"), ("moe_d", "moe_w_down"))}
    arrays["smalls"] = small_weights({k: np.asarray(v) for k, v in inputs.items()})
    arrays["cst"] = constants()
    known = None
    for _ in range(2):
        nc = bacc.Bacc("TRN2", target_bir_lowering=False, num_devices=1)
        aps = {n: nc.dram_tensor(n, a.shape, F32, kind="ExternalInput").ap() for n, a in arrays.items()}
        out = nc.dram_tensor("out", (1, T, D), F32, kind="ExternalOutput").ap()
        known = trunk_program(nc, known, out=out, **aps)
    r = run_bass_kernel_spmd(nc, [arrays], core_ids=[0])
    return r.results[0]["out"]
```

```python
from contextlib import ExitStack

import numpy as np

import concourse.bass as bass
from concourse import mybir

F32 = mybir.dt.float32
F32R = mybir.dt.float32r
I32 = mybir.dt.int32
U32 = mybir.dt.uint32
ALU = mybir.AluOpType
ACT = mybir.ActivationFunctionType
AX = mybir.AxisListType

P = 128
D = 1024
T = 256
TT = T // P
KD = D // P
DEPTH = 2
HD = 64
QR, KVR, NOPE, ROPE = 256, 128, 64, 32
HA, HB, HKV, HC = 4, 8, 2, 4
QK = NOPE + ROPE
C_CKV = QR
C_KPE = QR + KVR
C_BQ = C_KPE + ROPE
C_BK = C_BQ + HB * HD
C_BV = C_BK + HKV * HD
C_CQ = C_BV + HKV * HD
C_CK = C_CQ + HC * HD
C_CV = C_CK + HC * HD
IN_COLS = C_CV + HC * HD
COL_CHUNKS = [(0, C_BQ), (C_BQ, 512), (C_BQ + 512, 512), (C_BQ + 1024, 512)]
FF = 2816
NE = 8
FE = 3584
CH = 512
NCH = FE // CH
EPS = 1e-6
NEG = -1e30
SCATTER_BANKS = (1, 3, 6, 7)
SEG = 3 * P
GROUP = P

CONST = {}
_at = 0
for _name, _w in (("ident", P), ("cos", TT * 16), ("sin", TT * 16), ("causal", SEG), ("negdist", SEG),
                  ("stick_add", SEG), ("stick_mul", SEG), ("neg_tri", P), ("neg_ones", P), ("ones", P),
                  ("rank_tri", P), ("iota", 2 * GROUP), ("swa_scale", TT * (HB + HKV)), ("mla_scale", TT * 2 * HA)):
    CONST[_name] = (_at, _w)
    _at += _w
N_CONST = _at

SMALL = {}
_at = 0
for _l in range(DEPTH):
    for _name, _w in (("attn_g", KD), ("ffn_g", KD), ("out_g", KD), ("cq_g", 2), ("ckv_g", 1), ("swa_q_g", 1),
                      ("swa_k_g", 1), ("qn_g", QK), ("kn_g", QK), ("sinks", HB)):
        SMALL[_name, _l] = (_at, _w)
        _at += _w
SMALL["router"] = (_at, KD * NE)
N_SMALL = _at + KD * NE

RING = 7
UNIT = KD * CH
UNITS = []
for _l in range(DEPTH):
    UNITS += [("in", _l, n) for n in range(4)] + [("out", _l, n) for n in range(2)]
    if _l % 2 == 0:
        _last = (FF + CH - 1) // CH - 1
        UNITS += [("gate", _l, 0), ("up", _l, 0)]
        UNITS += [(w, _l, n - (w == "down")) for n in range(1, _last + 1) for w in ("gate", "up", "down")]
        UNITS.append(("down", _l, _last))
UNIT_NO = {u: n for n, u in enumerate(UNITS)}
N_UNITS = len(UNITS)
MOE_UNITS = [("g", 0), ("u", 0)]
for _c in range(1, NCH):
    MOE_UNITS += [("g", _c), ("u", _c), ("d", _c - 1)]
MOE_UNITS.append(("d", NCH - 1))
MOE_NO = {u: n for n, u in enumerate(MOE_UNITS)}
M_UNITS = len(MOE_UNITS)
assert M_UNITS % RING == 0

PIECE = 1024
SPLIT = 4
PER_UNIT = UNIT // PIECE
FF_TILES = FF // P
FF_CHUNKS = [min(CH, FF - n) for n in range(0, FF, CH)]


def pieces_of(units, widths):
    pieces, first, last = [], {}, {}
    for kind, c in units:
        first[kind, c] = len(pieces)
        pieces += [((kind, c), r) for r in range(widths[c] * KD // PIECE)]
        last[kind, c] = len(pieces) - 1
    return pieces, first, last


DENSE_UNITS = [("gate", 0), ("up", 0)]
for _c in range(1, len(FF_CHUNKS)):
    DENSE_UNITS += [("gate", _c), ("up", _c), ("down", _c - 1)]
DENSE_UNITS.append(("down", len(FF_CHUNKS) - 1))
D_PIECES, D_FIRST, D_LAST = pieces_of(DENSE_UNITS, FF_CHUNKS)
E_PIECES, E_FIRST, E_LAST = pieces_of(MOE_UNITS, [CH] * NCH)
N_E = len(E_PIECES)
assert N_E % SPLIT == 0
AT_Y_OUT, AT_ADD, AT_PICK_GT, AT_PICKS, AT_GATHERED = SPLIT - 1, 2 * SPLIT, 3 * SPLIT, 40, N_E - 1
T_LAST = N_E - 6
AT_SIG = {E_LAST["g", c] + SPLIT: c for c in range(NCH)}
AT_GATED = {E_LAST["g", c] + SPLIT + 1: c for c in range(NCH)}
AT_HID = {E_LAST["u", c] + SPLIT: c for c in range(NCH)}
AT_HIDT = {(E_LAST["g", c + 1] + SPLIT + 1 if c < NCH - 1 else T_LAST + SPLIT): c for c in range(NCH)}


class Progress:

    def __init__(self, name, marks):
        self.name, self.marks, self.n, self.loop, self.start = name, marks, 0, None, 0

    def step(self, key=None):
        self.n += 1
        if key is not None:
            self.marks[key] = (self.name, self.loop, self.start, self.n - self.start if self.loop else self.n)
        return 1

    def enter(self, loop):
        self.loop, self.start = loop, self.n

    def leave(self, trips):
        k = self.n - self.start
        self.marks["per", self.loop, self.name] = k
        self.n = self.start + trips * k
        self.loop = None


class Counts:

    def __init__(self, known):
        self.known = known

    def at(self, key, it=None, back=0):
        if self.known is None:
            return 1 if it is None else it + 1
        name, loop, start, m = self.known[key]
        if loop is None:
            return m
        k = self.known["per", loop, name]
        if it is None:
            return start + (NE - 1) * k + m
        return it * k + (start + m - back * k)

    def own(self, progress, it=None):
        if progress.loop is None:
            return progress.n
        if self.known is None:
            return it + 1
        return it * self.known["per", progress.loop, progress.name] + progress.n


def trunk_program(nc, known, x, cst, smalls, w_in, w_uq, w_ukv, w_out, dense_g, dense_u, dense_d, moe_g, moe_u,
                  moe_d, out):
    marks = {}
    counts = Counts(known)
    with ExitStack() as ctx:
        def sb(name, shape, dt=F32):
            return ctx.enter_context(nc.sbuf_tensor(name, shape, dt))

        def sem(name):
            return ctx.enter_context(nc.semaphore(name))

        ring = sb("ring", [P, RING, UNIT])
        xres = sb("xres", [P, TT, D])
        consts = sb("consts", [P, N_CONST])
        small = sb("small", [P, N_SMALL])
        hT = sb("hT", [P, KD, T])
        xn = sb("xn", [P, TT, D])
        uq = sb("uq", [P, 2, HA * QK])
        ukv = sb("ukv", [P, HA * (NOPE + HD)])
        stat = sb("stat", [P, 96])
        stat_a = sb("stat_a", [P, 96])
        stat_t = sb("stat_t", [P, 20])
        top = sb("top", [P, TT, 8])
        top_at = sb("top_at", [P, TT, 8], U32)
        sel = sb("sel", [P, TT, NE])
        over = sb("over", [P, 4])
        over_i = sb("over_i", [1, 1], I32)
        rankm = sb("rankm", [P, TT, NE + 1])
        gates = sb("gates", [P, TT, NE + 1])
        ps = ctx.enter_context(nc.psum_tensor("ps", [P, 8, 512], F32))

        with ExitStack() as stage:
            def sb_stage(name, shape, dt=F32):
                return stage.enter_context(nc.sbuf_tensor(name, shape, dt))
            cols = sb_stage("cols", [P, TT, IN_COLS])
            scratch = sb_stage("scratch", [P, 8 * SEG])
            mla_v = sb_stage("mla_v", [P, TT, HA * HD])
            mla_T = sb_stage("mla_T", [P, 2 * HA, T])
            swa_qT = sb_stage("swa_qT", [P, HB // 2, T])
            swa_kT = sb_stage("swa_kT", [P, T])
            stick_qT = sb_stage("stick_qT", [P, HC // 2, T])
            stick_kT = sb_stage("stick_kT", [P, HC // 2, T])
            stick = sb_stage("stick", [P, HC, SEG])
        with ExitStack() as stage:
            def sb_stage(name, shape, dt=F32):
                return stage.enter_context(nc.sbuf_tensor(name, shape, dt))
            d_hi = sb_stage("d_hi", [P, SPLIT, PIECE], F32R)
            d_lo = sb_stage("d_lo", [P, SPLIT, PIECE], F32R)
            hT_hi = sb_stage("hT_hi", [P, KD, T], F32R)
            hT_lo = sb_stage("hT_lo", [P, KD, T], F32R)
            hid_hi = sb_stage("hid_hi", [P, 2, 4 * T], F32R)
            hid_lo = sb_stage("hid_lo", [P, 2, 4 * T], F32R)
        with ExitStack() as stage:
            def sb_stage(name, shape, dt=F32):
                return stage.enter_context(nc.sbuf_tensor(name, shape, dt))
            e_hi = sb_stage("e_hi", [P, SPLIT, PIECE], F32R)
            e_lo = sb_stage("e_lo", [P, SPLIT, PIECE], F32R)
            xgT_hi = sb_stage("xgT_hi", [P, KD, GROUP], F32R)
            xgT_lo = sb_stage("xgT_lo", [P, KD, GROUP], F32R)
            hidT_hi = sb_stage("hidT_hi", [P, 2, CH], F32R)
            hidT_lo = sb_stage("hidT_lo", [P, 2, CH], F32R)
            gated = sb_stage("gated", [P, CH])
            ysb = sb_stage("ysb", [P, D])
            pick = sb_stage("pick", [P, TT, GROUP])
            pick_g = sb_stage("pick_g", [P, TT, GROUP])
            pick_gT = sb_stage("pick_gT", [P, TT, P])

        probsT = hT[:, :, :].rearrange("p k t -> p (k t)")[:, 0:4 * SEG].rearrange("p (h s) -> p h s", h=4)
        qk = xn[:, :, :].rearrange("p a d -> p (a d)")[:, 0:TT * 2 * HA * QK].rearrange(
            "p (a h d) -> p a h d", a=TT, h=2 * HA)
        mixed = xn
        S = scratch[:, :].rearrange("p (h s) -> p h s", h=8)
        cqT = scratch[:, 0:512].rearrange("p (c t) -> p c t", c=2)
        ckvT = scratch[:, 512:768]
        mla_sq = scratch[:, 768:768 + 1536]
        rope_t = scratch[:, 768:768 + 1024].rearrange("p (n a h d) -> p n a h d", n=4, a=TT, h=2 * HA)
        swa_sq = scratch[:, 1536:1536 + 1280]
        swa_q = scratch[:, 2048:3072].rearrange("p (a n) -> p a n", a=TT)
        junk = stick[:, :, :].rearrange("p h s -> p (h s)")
        hT_flat = hT[:, :, :].rearrange("p k t -> p (k t)")
        sig = hT_flat[:, 0:1024].rearrange("p (b n) -> p b n", b=2)
        hid = hT_flat[:, 1024:2048].rearrange("p (b n) -> p b n", b=2)
        sig_d, gated_d = hT_flat[:, 0:1024], hT_flat[:, 1024:2048]
        hidden_d = xn[:, 0, :]

        def C(name):
            a, w = CONST[name]
            return consts[:, a:a + w]

        def G(name, l=None):
            a, w = SMALL[name] if l is None else SMALL[name, l]
            return small[:, a:a + w]

        ident = C("ident")

        pe_done, act_done, dve_done, unit_used = sem("pe_done"), sem("act_done"), sem("dve_done"), sem("unit_used")
        pe_p, act_p, dve_p, unit_p = (Progress(n, marks) for n in ("pe", "act", "dve", "unit"))
        at = counts.at
        x_loaded, const_loaded, small_loaded = sem("x_loaded"), sem("const_loaded"), sem("small_loaded")
        up_loaded = sem("up_loaded")
        slot_loaded = [sem(f"slot_loaded{n}") for n in range(RING)]
        result_ready, out_stored = sem("result_ready"), sem("out_stored")

        def slot_of(no):
            return ring[:, no % RING, :]

        def loaded(no, it=None):
            v = 16 * (no // RING + 1)
            return slot_loaded[no % RING], v if it is None else it * (16 * M_UNITS // RING) + v

        def cols_in_sbuf(l, n, a):
            return (dve_done if a == 0 else act_done), at(("cols_sb", l, n, a))

        def probs_in_sbuf(l, kind, h):
            return (dve_done if h % 2 else act_done), at(("pT" + kind, l, h))

        block = ctx.enter_context(nc.Block())

        def unit_source(kind, l, n, dst):
            if kind == "in":
                a, w = COL_CHUNKS[n]
                return (dst[:, 0:KD * w].rearrange("p (k n) -> p k n", k=KD),
                        w_in[l].rearrange("(k p) n -> p k n", p=P)[:, :, a:a + w])
            if kind == "out":
                return (dst.rearrange("p (k n) -> p k n", k=KD),
                        w_out[l].rearrange("(k p) n -> p k n", p=P)[:, :, n * CH:(n + 1) * CH])
            w = min(CH, FF - n * CH)
            if kind == "down":
                return (dst[:, 0:w // P * D].rearrange("p (j n) -> p j n", n=D),
                        dense_d[l // 2, n * CH:n * CH + w, :].rearrange("(j p) n -> p j n", p=P))
            src = dense_g if kind == "gate" else dense_u
            return (dst[:, 0:KD * w].rearrange("p (k n) -> p k n", k=KD),
                    src[l // 2].rearrange("(k p) n -> p k n", p=P)[:, :, n * CH:n * CH + w])

        @block.sync
        def _(sp):
            for a in range(TT):
                sp.dma_start(xres[:, a, :], x[0, a * P:(a + 1) * P, :]).then_inc(x_loaded, 16)
            sp.dma_start(consts[:], cst[:]).then_inc(const_loaded, 16)
            sp.dma_start(small[:], smalls[:]).then_inc(small_loaded, 16)

            def load_up(l):
                sp.dma_start(uq[:], w_uq[l].rearrange("(k p) n -> p k n", p=P)).then_inc(up_loaded, 16)
                sp.dma_start(ukv[:], w_ukv[l]).then_inc(up_loaded, 16)

            def free(no):
                kind, l, n = UNITS[no - RING]
                if kind in ("in", "out"):
                    return unit_used, at((("cols" if kind == "in" else "proj"), l, n, 1))
                return dve_done, at(("rest", l, D_LAST[kind, n]))

            for no, (kind, l, n) in enumerate(UNITS):
                if no >= RING:
                    sp.wait_ge(*free(no))
                dst, src = unit_source(kind, l, n, slot_of(no))
                sp.dma_start(dst, src).then_inc(slot_loaded[no % RING], 16)
                if no == 1:
                    load_up(0)
                if no == UNIT_NO["down", 0, 0]:
                    sp.wait_ge(pe_done, at(("up_proj", 0)))
                    load_up(1)

            def expert_unit(group, r, e):
                kind, c = MOE_UNITS[r]
                no = N_UNITS + group * NE * M_UNITS + r
                which = bass.ds(e, 1)
                if kind == "d":
                    src = moe_d[0, which, c * CH:(c + 1) * CH, :].rearrange("o (j p) n -> p (o j) n", p=P)
                    dst = slot_of(no).rearrange("p (j n) -> p j n", n=D)
                else:
                    columns = (moe_g if kind == "g" else moe_u)[0, which, :, c * CH:(c + 1) * CH]
                    src = columns.rearrange("o (k p) n -> p (o k) n", p=P)
                    dst = slot_of(no).rearrange("p (k n) -> p k n", k=KD)
                sp.dma_start(dst, src).then_inc(slot_loaded[no % RING], 16)

            def expert_units(group):
                for r in range(RING):
                    if group:
                        sp.wait_ge(dve_done, at((0, "rest", E_LAST[MOE_UNITS[M_UNITS - RING + r]])))
                    else:
                        sp.wait_ge(*free(N_UNITS + r))
                    expert_unit(group, r, 0)
                with sp.Fori(0, NE - 1) as e:
                    for r in range(M_UNITS):
                        sp.wait_ge(dve_done, at((group, "rest", E_LAST[MOE_UNITS[r]]), e))
                        expert_unit(group, (r + RING) % M_UNITS, e if r + RING < M_UNITS else e + 1)
                for r in range(M_UNITS - RING):
                    sp.wait_ge(dve_done, at((group, "rest", E_LAST[MOE_UNITS[r]])))
                    expert_unit(group, r + RING, NE - 1)

            expert_units(0)
            sp.wait_ge(dve_done, at("overflow"))
            more = sp.value_load(over_i[0:1, 0:1], min_val=0, max_val=1)
            with sp.If(more > 0):
                expert_units(1)
            sp.wait_ge(result_ready, 1)
            for a in range(TT):
                sp.dma_start(out[0, a * P:(a + 1) * P, :], xres[:, a, :]).then_inc(out_stored, 16)
            sp.wait_ge(out_stored, 16 * TT)

        @block.tensor
        def _(pe):
            def transposes(l, what):
                for a in range(TT):
                    pe.wait_ge(dve_done, at((what, l, a)))
                    for k in range(KD):
                        ins = pe.transpose(ps[:, k // 2, (k % 2) * T + a * P:(k % 2) * T + (a + 1) * P],
                                           xn[:, a, k * P:(k + 1) * P], ident)
                        if a == TT - 1 and k % 2 == 1:
                            ins.then_inc(pe_done, pe_p.step((what + "_T", l, k // 2)))

            def product(bank, width, unit_no, lhs, unit_view, last, key):
                for k in range(KD):
                    ins = pe.matmul(ps[:, bank, 0:width], lhs(k), unit_view(k), start=k == 0, stop=k == KD - 1)
                ins.then_inc(unit_used if last else pe_done, (unit_p if last else pe_p).step(key))

            def layer_mixers(l):
                u0 = UNIT_NO["in", l, 0]
                transposes(l, "attn_n")

                def cols_chunk(n):
                    a0, w = COL_CHUNKS[n]
                    view = slot_of(u0 + n)[:, 0:KD * w].rearrange("p (k n) -> p k n", k=KD)
                    pe.wait_ge(*loaded(u0 + n))
                    for a in range(TT):
                        if n >= 2:
                            pe.wait_ge(*cols_in_sbuf(l, n - 2, a))
                        if n == 0 and a == 0:
                            pe.wait_ge(act_done, at(("attn_n_done", l, 1)))
                            pe.wait_ge(dve_done, at(("attn_n_done", l, 3)))
                        product(4 + (n * 2 + a) % 4, w, u0 + n, lambda k: hT[:, k, a * P:(a + 1) * P],
                                lambda k: view[:, k, :], a == TT - 1, ("cols", l, n, a))

                cols_chunk(0)
                cols_chunk(1)
                pe.wait_ge(dve_done, at(("cq_n", l)))
                for c in range(3):
                    for a in range(TT):
                        ins = pe.transpose(ps[:, c // 2, (c % 2) * T + a * P:(c % 2) * T + (a + 1) * P],
                                           cols[:, a, c * P:(c + 1) * P], ident)
                ins.then_inc(pe_done, pe_p.step(("cq_T", l)))
                cols_chunk(2)
                pe.wait_ge(dve_done, at(("cqT", l)))
                pe.wait_ge(up_loaded, 32 * (l + 1))
                for a in range(TT):
                    for c in range(2):
                        ins = pe.matmul(ps[:, 2 + a, 0:HA * QK], cqT[:, c, a * P:(a + 1) * P], uq[:, c, :],
                                        start=c == 0, stop=c == 1)
                    ins = pe.matmul(ps[:, a, :], ckvT[:, a * P:(a + 1) * P], ukv[:], start=True, stop=True)
                ins.then_inc(pe_done, pe_p.step(("up_proj", l)))
                cols_chunk(3)
                pe.wait_ge(dve_done, at(("swa_n", l)))
                pe.wait_ge(dve_done, at(("kv_read", l)))
                for i in range(4):
                    for a in range(TT):
                        ins = pe.transpose(ps[:, i // 2, (i % 2) * T + a * P:(i % 2) * T + (a + 1) * P],
                                           swa_q[:, a, i * P:(i + 1) * P], ident)
                    if i % 2:
                        ins.then_inc(pe_done, pe_p.step(("swa_q_T", l, i // 2)))
                pe.wait_ge(act_done, at(("q_read", l)))
                for a in range(TT):
                    ins = pe.transpose(ps[:, 2, a * P:(a + 1) * P], cols[:, a, C_BK:C_BV], ident)
                ins.then_inc(pe_done, pe_p.step(("swa_k_T", l)))
                for a in range(TT):
                    pe.wait_ge(*cols_in_sbuf(l, 2, a))
                    pe.wait_ge(*cols_in_sbuf(l, 3, a))
                for i, c0 in ((0, C_CQ), (1, C_CK)):
                    for j in range(2):
                        for a in range(TT):
                            ins = pe.transpose(ps[:, 4 + i, j * T + a * P:j * T + (a + 1) * P],
                                               cols[:, a, c0 + j * P:c0 + (j + 1) * P], ident)
                    ins.then_inc(pe_done, pe_p.step(("stick_T", l, i)))
                pe.wait_ge(dve_done, at(("mla_n", l)))
                for j in range(HA):
                    bank = (6, 7, 3, 2)[j]
                    if bank == 2:
                        pe.wait_ge(act_done, at(("swa_kT", l)))
                    for h in range(2):
                        for a in range(TT):
                            ins = pe.transpose(ps[0:QK, bank, h * T + a * P:h * T + (a + 1) * P],
                                               qk[:, a, 2 * j + h, :], ident)
                    ins.then_inc(pe_done, pe_p.step(("mla_T", l, j)))

                pe.wait_ge(act_done, at(("stickT", l, 0)))
                pe.wait_ge(dve_done, at(("stickT", l, 1)))
                pe.wait_ge(act_done, at(("mlaT", l, 0)))
                pe.wait_ge(dve_done, at(("mlaT", l, 1)))
                for h in range(HC):
                    o, j = HD * (h % 2), h // 2
                    pe.matmul(ps[:, 4 + h, 0:T], stick_kT[o:o + HD, j, 0:P], stick_qT[o:o + HD, j, :],
                              start=True, stop=False, skip_group_check=True)
                    ins = pe.matmul(ps[:, 4 + h, T:SEG], stick_kT[o:o + HD, j, P:T], stick_qT[o:o + HD, j, P:T],
                                    start=False, stop=False, skip_group_check=True)
                    ins.then_inc(pe_done, pe_p.step(("z", l, h)))

                def scores(h, bank, q, k, key):
                    pe.matmul(ps[:, bank, 0:P], q[:, 0:P], k[:, 0:P], start=True, stop=True)
                    ins = pe.matmul(ps[:, bank, P:SEG], q[:, P:T], k[:, 0:T], start=True, stop=True)
                    ins.then_inc(pe_done, pe_p.step(key))

                pe.wait_ge(act_done, at(("mlaT", l, 2)))
                pe.wait_ge(dve_done, at(("mlaT", l, 3)))
                pe.wait_ge(dve_done, at(("swaT", l)))
                for h in range(HA):
                    scores(h, h, mla_T[0:QK, h, :], mla_T[0:QK, HA + h, :], ("sA", l, h))

                def swa_scores(h):
                    o = HD * (h // 4)
                    pe.wait_ge(dve_done, at(("sA_read", l, h) if h < 4 else ("sB_read", l, h - 4)))
                    scores(h, h % 4, swa_qT[o:o + HD, h % 4, :], swa_kT[o:o + HD, :], ("sB", l, h))

                for h in range(4):
                    swa_scores(h)

                for h in range(HC):
                    pe.wait_ge(dve_done, at(("sp", l, h)))
                    pe.matmul(ps[:, 4 + h, 0:T], C("neg_tri"), stick[:, h, 0:T], start=False, stop=False,
                              skip_group_check=True)
                    pe.matmul(ps[:, 4 + h, P:T], C("neg_ones"), stick[:, h, T:SEG], start=False, stop=False,
                              skip_group_check=True)
                    ins = pe.matmul(ps[:, 4 + h, T:SEG], C("neg_tri"), stick[:, h, T:SEG], start=False, stop=True,
                                    skip_group_check=True)
                    ins.then_inc(pe_done, pe_p.step(("cum", l, h)))

                def probs_T(h, bank, slot, key):
                    for j in range(3):
                        ins = pe.transpose(ps[:, bank, j * P:(j + 1) * P], S[:, slot, j * P:(j + 1) * P], ident)
                    ins.then_inc(pe_done, pe_p.step(key))

                def values(pT, bank, c0, v, key):
                    pe.matmul(ps[:, bank, c0:c0 + HD], pT[:, 0:P], v[0], start=True, stop=True, skip_group_check=True)
                    pe.matmul(ps[:, bank, 256 + c0:256 + c0 + HD], pT[:, P:T], v[0], start=True, stop=False,
                              skip_group_check=True)
                    ins = pe.matmul(ps[:, bank, 256 + c0:256 + c0 + HD], pT[:, T:SEG], v[1], start=False, stop=True,
                                    skip_group_check=True)
                    ins.then_inc(pe_done, pe_p.step(key))

                for h in range(HA):
                    pe.wait_ge(act_done, at(("pA", l, h)))
                    pe.wait_ge(dve_done, at(("w_read", l, h)))
                    probs_T(h, 4 + h, h, ("pA_T", l, h))
                for h in range(4, HB):
                    swa_scores(h)
                for h in range(HA):
                    pe.wait_ge(*probs_in_sbuf(l, "A", h))
                    values(probsT[:, h, :], 4, h * HD, [mla_v[:, a, h * HD:(h + 1) * HD] for a in range(TT)],
                           ("oA", l, h))
                for h in range(HC):
                    pe.wait_ge(act_done, at(("aC", l, h)))
                    values(stick[:, h, :], 5, h * HD, [cols[:, a, C_CV + h * HD:C_CV + (h + 1) * HD]
                                                      for a in range(TT)], ("oC", l, h))
                for h in range(HB):
                    bank = (6, 7, 0, 1, 3, 6, 7, 0)[h]
                    pe.wait_ge(act_done, at(("pB", l, h)))
                    if bank in (0, 1, 3) and h != 7:
                        pe.wait_ge(dve_done, at(("sB_read", l, 4 + bank)))
                    if h >= 5:
                        pe.wait_ge(*probs_in_sbuf(l, "B", {5: 0, 6: 1, 7: 2}[h]))
                    probs_T(h, bank, (4 + h) % 8, ("pB_T", l, h))
                    if h % 4 == 3:
                        for g in range(h - 3, h + 1):
                            pe.wait_ge(*probs_in_sbuf(l, "B", g))
                            if g == 0:
                                pe.wait_ge(dve_done, at(("sB_read", l, 6)))
                            kv = g // 4
                            values(probsT[:, g % 4, :], 2 if g < 4 else 1, (g % 4) * HD,
                                   [cols[:, a, C_BV + kv * HD:C_BV + (kv + 1) * HD] for a in range(TT)],
                                   ("oB", l, g))

                pe.wait_ge(dve_done, at(("oB_read", l, 1)))
                transposes(l, "mix_n")
                pe.wait_ge(act_done, at(("mix_n_done", l, 1)))
                pe.wait_ge(dve_done, at(("mix_n_done", l, 3)))
                for n in range(2):
                    no = UNIT_NO["out", l, n]
                    pe.wait_ge(*loaded(no))
                    view = slot_of(no).rearrange("p (k n) -> p k n", k=KD)
                    for a in range(TT):
                        product(4 + n * 2 + a, CH, no, lambda k: hT[:, k, a * P:(a + 1) * P],
                                lambda k: view[:, k, :], a == TT - 1, ("proj", l, n, a))
                transposes(l, "ffn_n")
                if l % 2:
                    pe.wait_ge(act_done, at(("ffn_n_done", l, 1)))
                pe.wait_ge(dve_done, at(("ffn_n_done", l, 3)))

            def three_passes(out, hi_l, lo_l, hi_r, lo_r, start, stop):
                pe.matmul(out, hi_l, hi_r, start=start, stop=False, skip_group_check=True)
                pe.matmul(out, hi_l, lo_r, start=False, stop=False, skip_group_check=True)
                return pe.matmul(out, lo_l, hi_r, start=False, stop=stop, skip_group_check=True)

            def dense(l):
                pe.wait_ge(dve_done, at(("proj_add", l, 3)))
                for q, ((kind, c), r) in enumerate(D_PIECES):
                    w, slot = FF_CHUNKS[c], q % SPLIT
                    if q == D_FIRST[kind, c]:
                        if kind == "gate" and c:
                            pe.wait_ge(dve_done, at(("gated", l, c - 1)))
                        if kind == "up" and c:
                            pe.wait_ge(dve_done, at(("hidden", l, c - 1)))
                        if kind == "down":
                            pe.wait_ge(dve_done, at(("hid_lo", l, c)))
                    pe.wait_ge(dve_done, at(("rest", l, q)))
                    if kind == "down":
                        for a in range(TT):
                            tokens = slice(r * T + a * P, r * T + (a + 1) * P)
                            for n in range(2):
                                dims = slice(n * CH, (n + 1) * CH)
                                ins = three_passes(ps[:, 4 + 2 * a + n, :], hid_hi[:, c % 2, tokens],
                                                   hid_lo[:, c % 2, tokens], d_hi[:, slot, dims], d_lo[:, slot, dims],
                                                   c == 0 and r == 0, q == len(D_PIECES) - 1)
                    else:
                        ks = PIECE // w
                        for j in range(w // P):
                            bank = (0 if kind == "gate" else 2) + j // 2
                            for i in range(ks):
                                k, at_w = r * ks + i, slice(i * w + j * P, i * w + (j + 1) * P)
                                ins = three_passes(ps[:, bank, (j % 2) * T:(j % 2 + 1) * T], d_hi[:, slot, at_w],
                                                   d_lo[:, slot, at_w], hT_hi[:, k, :], hT_lo[:, k, :],
                                                   k == 0 and j % 2 == 0, k == KD - 1 and j % 2 == 1)
                    ins.then_inc(pe_done, pe_p.step(("piece", l, q)))

            def experts_prepare():
                l = DEPTH - 1
                for a in range(TT):
                    for k in range(KD):
                        ins = pe.matmul(ps[:, 4, a * NE:(a + 1) * NE], hT[:, k, a * P:(a + 1) * P],
                                        G("router")[:, k * NE:(k + 1) * NE], start=k == 0, stop=k == KD - 1)
                ins.then_inc(pe_done, pe_p.step("logits"))
                pe.wait_ge(dve_done, at("selected"))
                pe.matmul(ps[:, 5, 0:NE], C("rank_tri"), sel[:, 0, :], start=True, stop=True)
                pe.matmul(ps[:, 5, NE:2 * NE], C("ones"), sel[:, 0, :], start=True, stop=False)
                pe.matmul(ps[:, 5, NE:2 * NE], C("rank_tri"), sel[:, 1, :], start=False, stop=True)
                pe.matmul(ps[:, 5, 2 * NE:3 * NE], C("ones"), sel[:, 0, :], start=True, stop=False)
                ins = pe.matmul(ps[:, 5, 2 * NE:3 * NE], C("ones"), sel[:, 1, :], start=False, stop=True)
                ins.then_inc(pe_done, pe_p.step("ranks"))

            def experts(group):
                g = group

                def gather(key, it=None):
                    pe.wait_ge(dve_done, at((g, key, "pick"), it))
                    for n in range(2):
                        if it is not None:
                            pe.wait_ge(dve_done, at((g, "hidT_lo", NCH - 2 + n), it))
                        for k in range(4):
                            for a in range(TT):
                                ins = pe.matmul(ps[:, 6 + n, k * P:(k + 1) * P],
                                                xn[:, a, (4 * n + k) * P:(4 * n + k + 1) * P], pick[:, a, :],
                                                start=a == 0, stop=a == TT - 1)
                        ins.then_inc(pe_done, pe_p.step((g, key, "gathered", n)))

                def scatter(key, it=None):
                    pe.wait_ge(act_done, at((g, "y_out" + key), it))
                    for q, bank in enumerate(SCATTER_BANKS):
                        a, n = q // 2, q % 2
                        ins = pe.matmul(ps[:, bank, :], pick_gT[:, a, :], ysb[:, n * CH:(n + 1) * CH],
                                        start=True, stop=True)
                        ins.then_inc(pe_done, pe_p.step((g, "scatter" + key, q)))

                gather("first")
                pe.wait_ge(dve_done, at((g, "first", "xgT_lo")))
                pe_p.enter(("experts", g))
                with pe.Fori(0, NE) as e:
                    def hidden_T(c):
                        pe.wait_ge(dve_done, at((g, "hid", c), e))
                        bank = 7 if c % 2 == 0 else 6
                        if c == 0:
                            pe.wait_ge(dve_done, at((g, "add", 3), e))
                        elif c == 1:
                            pe.wait_ge(act_done, at((g, "pick_gT"), e))
                        else:
                            pe.wait_ge(dve_done, at((g, "hidT_lo", c - 2), e))
                        for j in range(4):
                            ins = pe.transpose(ps[:, bank, j * P:(j + 1) * P], hid[:, c % 2, j * P:(j + 1) * P], ident)
                        ins.then_inc(pe_done, pe_p.step((g, "hid_T", c)))

                    def bank_free(kind, c):
                        if kind == "d":
                            pe.wait_ge(dve_done, at((g, "hidT_lo", c), e))
                        elif kind == "g":
                            if c == 0:
                                pe.wait_ge(dve_done, at((g, "next", "xgT_lo"), e, 1))
                            elif c == 1:
                                pe.wait_ge(dve_done, at((g, "add", 0), e))
                            else:
                                pe.wait_ge(dve_done, at((g, "gated", c - 2), e))
                        elif c == 1:
                            pe.wait_ge(dve_done, at((g, "add", 1), e))
                        elif c:
                            pe.wait_ge(dve_done, at((g, "hid", c - 2), e))

                    for q, ((kind, c), r) in enumerate(E_PIECES):
                        slot = q % SPLIT
                        if r == 0:
                            bank_free(kind, c)
                        pe.wait_ge(dve_done, at((g, "rest", q), e))
                        if kind == "d":
                            rows = slice(r * P, (r + 1) * P)
                            for n in range(2):
                                dims = slice(n * CH, (n + 1) * CH)
                                ins = three_passes(ps[:, 4 + n, :], hidT_hi[:, c % 2, rows], hidT_lo[:, c % 2, rows],
                                                   e_hi[:, slot, dims], e_lo[:, slot, dims], c == 0 and r == 0,
                                                   c == NCH - 1 and r == PER_UNIT - 1)
                        else:
                            for i in range(PIECE // CH):
                                k, part = r * (PIECE // CH) + i, slice(i * CH, (i + 1) * CH)
                                ins = three_passes(ps[:, (0 if kind == "g" else 2) + c % 2, :], xgT_hi[:, k, :],
                                                   xgT_lo[:, k, :], e_hi[:, slot, part], e_lo[:, slot, part], k == 0,
                                                   k == KD - 1)
                        ins.then_inc(pe_done, pe_p.step((g, "piece", q)))
                        if q == E_LAST["g", 0]:
                            scatter("", e)
                        elif q == E_LAST["u", 0]:
                            pe.wait_ge(dve_done, at((g, "add", 2), e))
                            for a in range(TT):
                                ins = pe.transpose(ps[:, 6, a * P:(a + 1) * P], pick_g[:, a, :], ident)
                            ins.then_inc(pe_done, pe_p.step((g, "pick_g_T")))
                        elif q == E_LAST[kind, c] and kind == "g":
                            hidden_T(c - 1)
                        elif q == T_LAST:
                            hidden_T(NCH - 1)
                        elif q == E_LAST["d", NCH - 2]:
                            gather("next", e)
                pe_p.leave(NE)
                pe.wait_ge(dve_done, at((g, "next", "xgT_lo")))
                scatter("_end")

            pe.wait_ge(const_loaded, 16)
            pe.wait_ge(small_loaded, 16)
            layer_mixers(0)
            dense(0)
            pe.wait_ge(dve_done, at(("ffn_add", 0)))
            layer_mixers(1)
            experts_prepare()
            experts(0)
            more = pe.value_load(over_i[0:1, 0:1], min_val=0, max_val=1)
            with pe.If(more > 0):
                experts(1)

        @block.scalar
        def _(act):
            def rstd_of(v, r, key):
                act.wait_ge(dve_done, at((key, "ms")))
                nc.scalar.activation(r, v, ACT.Ln).then_inc(act_done, act_p.step())
                act.wait_ge(act_done, counts.own(act_p))
                nc.scalar.activation(r, r, ACT.Exp, scale=-0.5).then_inc(act_done, act_p.step((key, "r0")))

            def row_stats(l, what):
                for a in range(TT):
                    if what == "attn_n" and l == 0 and a == 0:
                        act.wait_ge(x_loaded, 16 * TT)
                    if what == "attn_n" and l > 0 and a == 0:
                        act.wait_ge(dve_done, at(("ffn_add", l - 1)))
                    if what == "ffn_n" and a == 0:
                        act.wait_ge(dve_done, at(("proj_add", l, 3)))
                    if a or l or what != "attn_n":
                        act.wait_ge(act_done, counts.own(act_p))
                    unread = junk[:, 0:D] if what == "attn_n" else hT_flat[:, 0:D]
                    nc.scalar.activation(unread, xres[:, a, :], ACT.Square, scale=D ** -0.5,
                                                    accum_out=stat[:, a:a + 1]).then_inc(act_done, act_p.step((what, l, "sq", a)))
                rstd_of(stat[:, 2:4], stat[:, 4:6], (what, l))

            def transposed_out(l, what, gain):
                for b in range(2):
                    act.wait_ge(pe_done, at((what + "_T", l, b)))
                    for i in range(2):
                        k = 2 * b + i
                        nc.scalar.activation(hT[:, k, :], ps[:, b, i * T:(i + 1) * T], ACT.Copy,
                                                        scale=gain[:, k:k + 1]).then_inc(act_done, act_p.step((what + "_done", l, b) if i else None))

            def cols_out(l, n):
                a0, w = COL_CHUNKS[n]
                act.wait_ge(unit_used, at(("cols", l, n, 1)))
                nc.scalar.activation(cols[:, 1, a0:a0 + w], ps[:, 4 + (n * 2 + 1) % 4, 0:w], ACT.Copy).then_inc(act_done, act_p.step(("cols_sb", l, n, 1)))

            def layer_mixers(l):
                row_stats(l, "attn_n")
                if l == 0:
                    act.wait_ge(small_loaded, 16)
                transposed_out(l, "attn_n", G("attn_g", l))
                cols_out(l, 0)
                act.wait_ge(act_done, counts.own(act_p))
                act.wait_ge(dve_done, at(("cols_sb", l, 0, 0)))
                for a in range(TT):
                    for i, (c0, w) in enumerate(((0, QR), (C_CKV, KVR))):
                        nc.scalar.activation(junk[:, (2 * a + i) * QR:(2 * a + i) * QR + w],
                                                        cols[:, a, c0:c0 + w], ACT.Square, scale=w ** -0.5,
                                                        accum_out=stat[:, 6 + 2 * a + i:7 + 2 * a + i]).then_inc(act_done, act_p.step(("cq_sq", l, 2 * a + i)))
                rstd_of(stat[:, 10:14], stat[:, 14:18], ("cq", l))
                cols_out(l, 1)
                cols_out(l, 2)
                act.wait_ge(pe_done, at(("up_proj", l)))
                for a in range(TT):
                    nc.scalar.activation(
                        qk[:, a, 0:HA, :].rearrange("p h d -> p (h d)"), ps[:, 2 + a, 0:HA * QK], ACT.Copy).then_inc(act_done, act_p.step(("q_read", l)))
                rstd_of(stat[:, 18:34], stat[:, 34:50], ("mla", l))
                rstd_of(stat[:, 50:70], stat[:, 70:90], ("swa", l))
                cols_out(l, 3)
                act.wait_ge(pe_done, at(("swa_k_T", l)))
                nc.scalar.activation(swa_kT[:], ps[:, 2, 0:T], ACT.Copy, scale=G("swa_k_g", l)).then_inc(act_done, act_p.step(("swa_kT", l)))
                act.wait_ge(pe_done, at(("stick_T", l, 0)))
                nc.scalar.activation(stick_qT[:].rearrange("p j t -> p (j t)"), ps[:, 4, :], ACT.Copy,
                                                scale=HD ** -0.5).then_inc(act_done, act_p.step(("stickT", l, 0)))
                for j in (0, 2):
                    act.wait_ge(pe_done, at(("mla_T", l, j)))
                    nc.scalar.activation(mla_T[0:QK, 2 * j:2 * j + 2, :].rearrange("p h t -> p (h t)"),
                                                    ps[0:QK, (6, 7, 3, 2)[j], :], ACT.Copy).then_inc(act_done, act_p.step(("mlaT", l, j)))
                for h in range(HC):
                    act.wait_ge(pe_done, at(("z", l, h)))
                    if h == 0:
                        act.wait_ge(act_done, counts.own(act_p))
                    nc.scalar.activation(stick[:, h, :], ps[:, 4 + h, 0:SEG], ACT.Abs).then_inc(act_done, act_p.step())
                    act.wait_ge(act_done, counts.own(act_p))
                    nc.scalar.activation(stick[:, h, :], stick[:, h, :], ACT.Exp, scale=-1.0).then_inc(act_done, act_p.step())
                    act.wait_ge(act_done, counts.own(act_p))
                    nc.scalar.activation(stick[:, h, :], stick[:, h, :], ACT.Ln, bias=1.0).then_inc(act_done, act_p.step(("ln", l, h)))

                def exps(slot, nm, acc, key):
                    nc.scalar.activation(S[:, slot, 0:P], S[:, slot, 0:P], ACT.Exp, bias=nm[0],
                                                    accum_out=acc[0]).then_inc(act_done, act_p.step())
                    nc.scalar.activation(S[:, slot, P:SEG], S[:, slot, P:SEG], ACT.Exp, bias=nm[1],
                                                    accum_out=acc[1]).then_inc(act_done, act_p.step(key))

                def head_cols(base, h):
                    return [stat_a[:, base + 8 * (h // 4) + 4 * a + h % 4:base + 8 * (h // 4) + 4 * a + h % 4 + 1]
                            for a in range(TT)]

                act.wait_ge(dve_done, at(("nmA", l)))
                for h in range(HA):
                    exps(h, head_cols(24, h), head_cols(48, h), ("pA", l, h))
                for h in range(HC):
                    act.wait_ge(dve_done, at(("w_read", l, h)))
                    nc.scalar.activation(stick[:, h, :], stick[:, h, :], ACT.Exp).then_inc(act_done, act_p.step(("aC", l, h)))
                for h in (0, 2):
                    act.wait_ge(pe_done, at(("pA_T", l, h)))
                    nc.scalar.activation(probsT[:, h, :], ps[:, 4 + h, 0:SEG], ACT.Copy).then_inc(act_done, act_p.step(("pTA", l, h)))
                for q in range(2):
                    act.wait_ge(dve_done, at(("nmB", l, q)))
                    for h in range(4 * q, 4 * q + 4):
                        exps((4 + h) % 8, head_cols(32, h), head_cols(56, h), ("pB", l, h))
                    nc.scalar.activation(stat_a[:, 72 + 8 * q:80 + 8 * q], stat_a[:, 72 + 8 * q:80 + 8 * q],
                                                    ACT.Exp).then_inc(act_done, act_p.step(("sink_e", l, q)))
                    for h in (4 * q, 4 * q + 2):
                        act.wait_ge(pe_done, at(("pB_T", l, h)))
                        if q == 0:
                            act.wait_ge(pe_done, at(("oA", l, h)))
                        else:
                            act.wait_ge(pe_done, at(("oB", l, h - 4)))
                        nc.scalar.activation(probsT[:, h % 4, :], ps[:, (6, 7, 0, 1, 3, 6, 7, 0)[h], 0:SEG],
                                                        ACT.Copy).then_inc(act_done, act_p.step(("pTB", l, h)))
                act.wait_ge(dve_done, at(("oB_read", l, 1)))
                act.wait_ge(act_done, counts.own(act_p))
                act.wait_ge(pe_done, at(("oC", l, HC - 1)))
                for a in range(TT):
                    for i, (c0, w) in enumerate(((0, 256), (256, 512), (768, 256))):
                        if a or i:
                            act.wait_ge(act_done, counts.own(act_p))
                        nc.scalar.activation(junk[:, 0:w], mixed[:, a, c0:c0 + w], ACT.Square,
                                                        scale=w ** -0.5,
                                                        accum_out=stat[:, 3 * a + i:3 * a + i + 1]).then_inc(act_done, act_p.step(("mix_sq", l)))
                rstd_of(stat[:, 6:12], stat[:, 12:18], ("mix", l))
                act.wait_ge(pe_done, at(("oB", l, HB - 1)))
                transposed_out(l, "mix_n", G("out_g", l))
                if l % 2 == 0:
                    for q in range(SPLIT):
                        lead(l, q)
                row_stats(l, "ffn_n")
                if l % 2:
                    act.wait_ge(unit_used, at(("proj", l, 1, 1)))
                    transposed_out(l, "ffn_n", G("ffn_g", l))
                    return
                for b in range(4):
                    act.wait_ge(pe_done, at(("ffn_n_T", l, b)))
                    for k in (2 * b, 2 * b + 1):
                        nc.scalar.activation(hT_hi[:, k, :], ps[:, b, (k % 2) * T:(k % 2 + 1) * T], ACT.Copy,
                                             scale=G("ffn_g", l)[:, k:k + 1]).then_inc(act_done, act_p.step(("hT_hi", l, b)))

            def lead(l, q):
                (kind, c), r = D_PIECES[q]
                no = UNIT_NO[kind, l, c]
                if r == 0:
                    act.wait_ge(*loaded(no))
                if q >= SPLIT:
                    act.wait_ge(pe_done, at(("piece", l, q - SPLIT)))
                nc.scalar.activation(d_hi[:, q % SPLIT, :], slot_of(no)[:, r * PIECE:(r + 1) * PIECE],
                                     ACT.Copy).then_inc(act_done, act_p.step(("lead", l, q)))

            def dense(l):
                chunks = range(len(FF_CHUNKS))
                for q in range(SPLIT, len(D_PIECES)):
                    lead(l, q)
                    for c in chunks:
                        w = FF_CHUNKS[c] // P * T
                        if q == D_LAST["gate", c] + SPLIT:
                            nc.scalar.activation(sig_d[:, 0:w], ps[:, 0:w // 512, :].rearrange("p b n -> p (b n)"),
                                                 ACT.Sigmoid).then_inc(act_done, act_p.step(("sig", l, c)))
                        if q == D_LAST["up", c] + SPLIT + 1:
                            act.wait_ge(dve_done, at(("hidden", l, c)))
                            nc.scalar.activation(hid_hi[:, c % 2, 0:w], hidden_d[:, 0:w],
                                                 ACT.Copy).then_inc(act_done, act_p.step(("hid_hi", l, c)))

            def experts(g):
                def gathered(key, it=None):
                    for n in range(2):
                        act.wait_ge(pe_done, at((g, key, "gathered", n), it))
                        for k in range(4 * n, 4 * n + 4):
                            nc.scalar.activation(xgT_hi[:, k, :], ps[:, 6 + n, (k % 4) * P:(k % 4 + 1) * P], ACT.Copy,
                                                 scale=G("ffn_g", DEPTH - 1)[:, k:k + 1]).then_inc(act_done, act_p.step((g, key, "xgT_hi", n)))

                def y_out(key):
                    nc.scalar.activation(ysb[:], ps[:, 4:6, :].rearrange("p b n -> p (b n)"), ACT.Copy).then_inc(act_done, act_p.step((g, "y_out" + key)))

                act.wait_ge(dve_done, at((g, "pass")))
                gathered("first")
                act_p.enter(("experts", g))
                with act.Fori(0, NE) as e:
                    for q, ((kind, c), r) in enumerate(E_PIECES):
                        no = N_UNITS + g * NE * M_UNITS + MOE_NO[kind, c]
                        if r == 0:
                            act.wait_ge(*loaded(no, e))
                        act.wait_ge(pe_done, at((g, "piece", q - SPLIT), e) if q >= SPLIT
                                    else at((g, "piece", q - SPLIT + N_E), e, 1))
                        nc.scalar.activation(e_hi[:, q % SPLIT, :], slot_of(no)[:, r * PIECE:(r + 1) * PIECE],
                                             ACT.Copy).then_inc(act_done, act_p.step((g, "lead", q)))
                        if q == AT_Y_OUT:
                            y_out("")
                        if q in AT_SIG:
                            n = AT_SIG[q]
                            nc.scalar.activation(sig[:, n % 2, :], ps[:, n % 2, :], ACT.Sigmoid).then_inc(act_done, act_p.step((g, "sig", n)))
                        if q == AT_PICK_GT:
                            act.wait_ge(pe_done, at((g, "pick_g_T"), e))
                            nc.scalar.activation(pick_gT[:].rearrange("p a s -> p (a s)"), ps[:, 6, 0:2 * P],
                                                 ACT.Copy).then_inc(act_done, act_p.step((g, "pick_gT")))
                        if q in AT_HIDT:
                            n = AT_HIDT[q]
                            act.wait_ge(pe_done, at((g, "hid_T", n), e))
                            nc.scalar.activation(hidT_hi[:, n % 2, :], ps[:, 7 if n % 2 == 0 else 6, :],
                                                 ACT.Copy).then_inc(act_done, act_p.step((g, "hidT_hi", n)))
                        if q == AT_GATHERED:
                            gathered("next", e)
                act_p.leave(NE)
                act.wait_ge(pe_done, at((g, "piece", N_E - 1)))
                y_out("_end")

            layer_mixers(0)
            dense(0)
            layer_mixers(1)
            act.wait_ge(dve_done, at("gap"))
            nc.scalar.activation(stat_a[:, 36:38], stat_a[:, 32:34], ACT.Exp, scale=-1.0).then_inc(act_done, act_p.step("first_gate"))
            experts(0)
            more = act.value_load(over_i[0:1, 0:1], min_val=0, max_val=1)
            with act.If(more > 0):
                experts(1)

        @block.vector
        def _(dve):
            def own(it=None):
                return counts.own(dve_p, it)

            def refine(v, r, t, key):
                dve.wait_ge(act_done, at((key, "r0")))
                nc.vector.scalar_tensor_tensor(t, r, -0.5, r, ALU.mult, ALU.mult).then_inc(dve_done, dve_p.step())
                dve.wait_ge(dve_done, own())
                nc.vector.tensor_tensor(t, t, v, ALU.mult).then_inc(dve_done, dve_p.step())
                dve.wait_ge(dve_done, own())
                nc.vector.scalar_tensor_tensor(r, t, 1.5, r, ALU.add, ALU.mult).then_inc(dve_done, dve_p.step())
                dve.wait_ge(dve_done, own())

            def row_norm(l, what):
                dve.wait_ge(act_done, at((what, l, "sq", 1)))
                nc.vector.tensor_scalar(stat[:, 2:4], stat[:, 0:2], EPS, None, ALU.add).then_inc(dve_done, dve_p.step(((what, l), "ms")))
                dve.wait_ge(dve_done, own())
                refine(stat[:, 2:4], stat[:, 4:6], stat[:, 90:92], (what, l))
                for a in range(TT):
                    nc.vector.tensor_scalar(xn[:, a, :], xres[:, a, :], stat[:, 4 + a:5 + a], None,
                                                       ALU.mult).then_inc(dve_done, dve_p.step((what, l, a)))

            def transposed_out(l, what, gain):
                for b in (2, 3):
                    dve.wait_ge(pe_done, at((what + "_T", l, b)))
                    for i in range(2):
                        k = 2 * b + i
                        nc.vector.tensor_scalar(hT[:, k, :], ps[:, b, i * T:(i + 1) * T], gain[:, k:k + 1],
                                                           None, ALU.mult).then_inc(dve_done, dve_p.step((what + "_done", l, b) if i else None))

            def cols_out(l, n):
                a0, w = COL_CHUNKS[n]
                dve.wait_ge(pe_done, at(("cols", l, n, 0)))
                nc.vector.tensor_copy(cols[:, 0, a0:a0 + w], ps[:, 4 + (n * 2) % 4, 0:w]).then_inc(dve_done, dve_p.step(("cols_sb", l, n, 0)))

            def layer_mixers(l):
                row_norm(l, "attn_n")
                if l == 0:
                    dve.wait_ge(small_loaded, 16)
                    dve.wait_ge(const_loaded, 16)
                transposed_out(l, "attn_n", G("attn_g", l))
                cols_out(l, 0)
                dve.wait_ge(act_done, at(("cq_sq", l, 3)))
                nc.vector.tensor_scalar(stat[:, 10:14], stat[:, 6:10], EPS, None, ALU.add).then_inc(dve_done, dve_p.step((("cq", l), "ms")))
                dve.wait_ge(dve_done, own())
                refine(stat[:, 10:14], stat[:, 14:18], stat[:, 90:94], ("cq", l))
                for a in range(TT):
                    for i, (c0, w) in enumerate(((0, QR), (C_CKV, KVR))):
                        nc.vector.tensor_scalar(cols[:, a, c0:c0 + w], cols[:, a, c0:c0 + w],
                                                           stat[:, 14 + 2 * a + i:15 + 2 * a + i], None, ALU.mult).then_inc(dve_done, dve_p.step(("cq_n", l)))
                cols_out(l, 1)
                dve.wait_ge(pe_done, at(("cq_T", l)))
                for c in range(2):
                    nc.vector.tensor_scalar(cqT[:, c, :], ps[:, 0, c * T:(c + 1) * T],
                                                       G("cq_g", l)[:, c:c + 1], None, ALU.mult).then_inc(dve_done, dve_p.step())
                nc.vector.tensor_scalar(ckvT, ps[:, 1, 0:T], G("ckv_g", l), None, ALU.mult).then_inc(dve_done, dve_p.step(("cqT", l)))
                cols_out(l, 2)
                dve.wait_ge(pe_done, at(("up_proj", l)))
                dve.wait_ge(act_done, at(("q_read", l)))
                dve.wait_ge(act_done, at(("cols_sb", l, 0, 1)))
                for a in range(TT):
                    kv = ps[:, a, :].rearrange("p (h d) -> p h d", h=HA)
                    nc.vector.tensor_copy(qk[:, a, HA:, 0:NOPE], kv[:, :, 0:NOPE]).then_inc(dve_done, dve_p.step())
                    nc.vector.tensor_copy(mla_v[:, a, :].rearrange("p (h d) -> p h d", h=HA),
                                                     kv[:, :, NOPE:]).then_inc(dve_done, dve_p.step(("kv_read", l)))
                    nc.vector.tensor_copy(
                        qk[:, a, HA:, NOPE:],
                        cols[:, a, C_KPE:C_BQ].rearrange("p (o d) -> p o d", o=1).broadcast_to([P, HA, ROPE])).then_inc(dve_done, dve_p.step())
                dve.wait_ge(dve_done, own())
                qkf = qk.rearrange("p a h d -> p (a h d)")
                qkg = qk.rearrange("p a h d -> p (a h) d")
                nc.vector.tensor_tensor(mla_sq, qkf, qkf, ALU.mult).then_inc(dve_done, dve_p.step())
                dve.wait_ge(dve_done, own())
                nc.vector.tensor_reduce(stat[:, 18:34], mla_sq.rearrange("p (g d) -> p g d", d=QK), AX.X,
                                              ALU.add).then_inc(dve_done, dve_p.step())
                dve.wait_ge(dve_done, own())
                nc.vector.tensor_scalar(stat[:, 18:34], stat[:, 18:34], 1.0 / QK, EPS, ALU.mult, ALU.add).then_inc(dve_done, dve_p.step((("mla", l), "ms")))
                dve.wait_ge(dve_done, own())
                dve.wait_ge(act_done, at(("cols_sb", l, 1, 1)))
                dve.wait_ge(act_done, at(("cols_sb", l, 2, 1)))
                swa = cols[:, :, C_BQ:C_BV]
                sq3 = swa_sq.rearrange("p (a n) -> p a n", a=TT)
                nc.vector.tensor_tensor(sq3, swa, swa, ALU.mult).then_inc(dve_done, dve_p.step())
                dve.wait_ge(dve_done, own())
                nc.vector.tensor_reduce(stat[:, 50:70], swa_sq.rearrange("p (g d) -> p g d", d=HD), AX.X,
                                              ALU.add).then_inc(dve_done, dve_p.step())
                dve.wait_ge(dve_done, own())
                nc.vector.tensor_scalar(stat[:, 50:70], stat[:, 50:70], 1.0 / HD, EPS, ALU.mult, ALU.add).then_inc(dve_done, dve_p.step((("swa", l), "ms")))
                dve.wait_ge(dve_done, own())
                refine(stat[:, 18:34], stat[:, 34:50], stat_t[:, 0:16], ("mla", l))
                nc.vector.tensor_tensor(stat[:, 34:50], stat[:, 34:50], C("mla_scale"), ALU.mult).then_inc(dve_done, dve_p.step())
                dve.wait_ge(dve_done, own())
                nc.vector.tensor_tensor(qkg, qkg,
                                              stat[:, 34:50].rearrange("p (g o) -> p g o", o=1).broadcast_to(
                                                  [P, 16, QK]), ALU.mult).then_inc(dve_done, dve_p.step())
                dve.wait_ge(dve_done, own())
                for a in range(TT):
                    for i, name in enumerate(("qn_g", "kn_g")):
                        part = qk[:, a, i * HA:(i + 1) * HA, :]
                        nc.vector.tensor_tensor(part, part, G(name, l).rearrange(
                            "p (o d) -> p o d", o=1).broadcast_to([P, HA, QK]), ALU.mult).then_inc(dve_done, dve_p.step())
                dve.wait_ge(dve_done, own())
                x1, x2 = qk[:, :, :, NOPE:NOPE + 16], qk[:, :, :, NOPE + 16:QK]
                cos = C("cos").rearrange("p (a o d) -> p a o d", a=TT, o=1).broadcast_to([P, TT, 2 * HA, 16])
                sin = C("sin").rearrange("p (a o d) -> p a o d", a=TT, o=1).broadcast_to([P, TT, 2 * HA, 16])
                for n, (u, v) in enumerate(((x1, cos), (x2, sin), (x1, sin), (x2, cos))):
                    nc.vector.tensor_tensor(rope_t[:, n], u, v, ALU.mult).then_inc(dve_done, dve_p.step())
                dve.wait_ge(dve_done, own())
                nc.vector.tensor_tensor(x1, rope_t[:, 0], rope_t[:, 1], ALU.subtract).then_inc(dve_done, dve_p.step())
                nc.vector.tensor_tensor(x2, rope_t[:, 2], rope_t[:, 3], ALU.add).then_inc(dve_done, dve_p.step(("mla_n", l)))
                refine(stat[:, 50:70], stat[:, 70:90], stat_t[:, 0:20], ("swa", l))
                nc.vector.tensor_tensor(stat[:, 70:90], stat[:, 70:90], C("swa_scale"), ALU.mult).then_inc(dve_done, dve_p.step())
                dve.wait_ge(dve_done, own())
                for a in range(TT):
                    r = stat[:, 70 + 10 * a:78 + 10 * a].rearrange("p (g i o) -> p i g o", g=2, o=1)
                    nc.vector.tensor_tensor(
                        swa_q[:, a, :].rearrange("p (i g d) -> p i g d", i=4, g=2),
                        cols[:, a, C_BQ:C_BK].rearrange("p (g i d) -> p i g d", g=2, i=4),
                        r.broadcast_to([P, 4, 2, HD]), ALU.mult).then_inc(dve_done, dve_p.step())
                    part = cols[:, a, C_BK:C_BV].rearrange("p (g d) -> p g d", d=HD)
                    r = stat[:, 78 + 10 * a:80 + 10 * a].rearrange("p (g o) -> p g o", o=1)
                    nc.vector.tensor_tensor(part, part, r.broadcast_to([P, HKV, HD]), ALU.mult).then_inc(dve_done, dve_p.step(("swa_n", l)))
                cols_out(l, 3)
                for b in range(2):
                    dve.wait_ge(pe_done, at(("swa_q_T", l, b)))
                    nc.vector.tensor_scalar(swa_qT[:, 2 * b:2 * b + 2, :].rearrange("p i t -> p (i t)"),
                                                       ps[:, b, :], G("swa_q_g", l), None, ALU.mult).then_inc(dve_done, dve_p.step(("swaT", l)))
                dve.wait_ge(pe_done, at(("stick_T", l, 1)))
                nc.vector.tensor_copy(stick_kT[:].rearrange("p j t -> p (j t)"), ps[:, 5, :]).then_inc(dve_done, dve_p.step(("stickT", l, 1)))
                for j in (1, 3):
                    dve.wait_ge(pe_done, at(("mla_T", l, j)))
                    nc.vector.tensor_copy(mla_T[0:QK, 2 * j:2 * j + 2, :].rearrange("p h t -> p (h t)"),
                                                     ps[0:QK, (6, 7, 3, 2)[j], :]).then_inc(dve_done, dve_p.step(("mlaT", l, j)))

                def head_max(slot, bank, bias, scale, at, h, key):
                    for a, (c0, c1) in enumerate(((0, P), (P, SEG))):
                        nc.vector.tensor_tensor_reduce(
                            out=S[:, slot, c0:c1], in0=ps[:, bank, c0:c1], in1=bias[:, c0:c1], scale=scale,
                            scalar=-3e38, op0=ALU.add, op1=ALU.max,
                            accum_out=stat_a[:, at + 8 * (h // 4) + 4 * a + h % 4:
                                             at + 8 * (h // 4) + 4 * a + h % 4 + 1]).then_inc(dve_done, dve_p.step(key))

                def softplus(h):
                    dve.wait_ge(act_done, at(("ln", l, h)))
                    nc.vector.scalar_tensor_tensor(stick[:, h, :], ps[:, 4 + h, 0:SEG], 0.0, stick[:, h, :],
                                                         ALU.max, ALU.add).then_inc(dve_done, dve_p.step())
                    dve.wait_ge(dve_done, own())
                    nc.vector.tensor_tensor(stick[:, h, :], stick[:, h, :], C("stick_mul"), ALU.mult).then_inc(dve_done, dve_p.step(("sp", l, h)))

                for h in range(HA):
                    dve.wait_ge(pe_done, at(("sA", l, h)))
                    head_max(h, h, C("causal"), 1.0, 0, h, ("sA_read", l, h))
                dve.wait_ge(dve_done, own())
                nc.vector.tensor_scalar(stat_a[:, 24:32], stat_a[:, 0:8], -1.0, None, ALU.mult).then_inc(dve_done, dve_p.step(("nmA", l)))
                for h in range(HC):
                    softplus(h)

                def swa_max(q):
                    for h in range(4 * q, 4 * q + 4):
                        dve.wait_ge(pe_done, at(("sB", l, h)))
                        if q:
                            dve.wait_ge(pe_done, at(("pA_T", l, h - 4)))
                        head_max((4 + h) % 8, h % 4, C("negdist"), 2.0 ** -(h + 1), 8, h, ("sB_read", l, h))
                    dve.wait_ge(dve_done, own())
                    sink = G("sinks", l)[:, 4 * q:4 * q + 4].rearrange("p (o h) -> p o h", o=1).broadcast_to([P, TT, 4])

                    def by_tile(c0):
                        return stat_a[:, c0 + 8 * q:c0 + 8 * q + 8].rearrange("p (a h) -> p a h", a=TT)
                    nc.vector.tensor_tensor(by_tile(8), by_tile(8), sink, ALU.max).then_inc(dve_done, dve_p.step())
                    dve.wait_ge(dve_done, own())
                    nc.vector.tensor_scalar(by_tile(32), by_tile(8), -1.0, None, ALU.mult).then_inc(dve_done, dve_p.step())
                    dve.wait_ge(dve_done, own())
                    nc.vector.tensor_tensor(by_tile(72), by_tile(32), sink, ALU.add).then_inc(dve_done, dve_p.step(("nmB", l, q)))

                swa_max(0)
                for h in range(HC):
                    dve.wait_ge(pe_done, at(("cum", l, h)))
                    nc.vector.tensor_tensor(stick[:, h, :], ps[:, 4 + h, 0:SEG], C("stick_add"), ALU.add).then_inc(dve_done, dve_p.step(("w_read", l, h)))
                for h in (1, 3):
                    dve.wait_ge(pe_done, at(("pA_T", l, h)))
                    nc.vector.tensor_copy(probsT[:, h, :], ps[:, 4 + h, 0:SEG]).then_inc(dve_done, dve_p.step(("pTA", l, h)))
                swa_max(1)

                def heads_out(bank, den, c0, key):
                    o = mixed[:, :, c0:c0 + 256].rearrange("p a (h d) -> p a h d", h=4)
                    i = ps[:, bank, :].rearrange("p (a h d) -> p a h d", a=TT, h=4)
                    d = den.rearrange("p (a h o) -> p a h o", a=TT, o=1).broadcast_to([P, TT, 4, HD])
                    nc.vector.tensor_tensor(o, i, d, ALU.mult).then_inc(dve_done, dve_p.step(key))

                dve.wait_ge(act_done, at(("pA", l, HA - 1)))
                nc.vector.reciprocal(stat_a[:, 0:8], stat_a[:, 48:56]).then_inc(dve_done, dve_p.step())
                dve.wait_ge(dve_done, own())
                dve.wait_ge(pe_done, at(("oA", l, HA - 1)))
                heads_out(4, stat_a[:, 0:8], 0, ("oA_read", l))
                dve.wait_ge(pe_done, at(("oC", l, HC - 1)))
                nc.vector.tensor_copy(mixed[:, :, 768:1024],
                                                 ps[:, 5, :].rearrange("p (a n) -> p a n", a=TT)).then_inc(dve_done, dve_p.step(("oC_read", l)))
                for q in range(2):
                    for h in (4 * q + 1, 4 * q + 3):
                        dve.wait_ge(pe_done, at(("pB_T", l, h)))
                        dve.wait_ge(pe_done, at(("oA", l, h) if q == 0 else ("oB", l, h - 4)))
                        nc.vector.tensor_copy(probsT[:, h % 4, :],
                                                         ps[:, (6, 7, 0, 1, 3, 6, 7, 0)[h], 0:SEG]).then_inc(dve_done, dve_p.step(("pTB", l, h)))
                    dve.wait_ge(act_done, at(("sink_e", l, q)))
                    den = stat_a[:, 8 + 8 * q:16 + 8 * q]
                    nc.vector.tensor_tensor(den, stat_a[:, 56 + 8 * q:64 + 8 * q],
                                                  stat_a[:, 72 + 8 * q:80 + 8 * q], ALU.add).then_inc(dve_done, dve_p.step())
                    dve.wait_ge(dve_done, own())
                    nc.vector.reciprocal(den, den).then_inc(dve_done, dve_p.step())
                    dve.wait_ge(dve_done, own())
                    dve.wait_ge(pe_done, at(("oB", l, 4 * q + 3)))
                    heads_out(2 if q == 0 else 1, den, 256 + 256 * q, ("oB_read", l, q))
                dve.wait_ge(act_done, at(("mix_sq", l)))
                nc.vector.tensor_scalar(stat[:, 6:12], stat[:, 0:6], EPS, None, ALU.add).then_inc(dve_done, dve_p.step((("mix", l), "ms")))
                dve.wait_ge(dve_done, own())
                refine(stat[:, 6:12], stat[:, 12:18], stat[:, 90:96], ("mix", l))
                for a in range(TT):
                    for i, (c0, w) in enumerate(((0, 256), (256, 512), (768, 256))):
                        nc.vector.tensor_scalar(mixed[:, a, c0:c0 + w], mixed[:, a, c0:c0 + w],
                                                           stat[:, 12 + 3 * a + i:13 + 3 * a + i], None, ALU.mult).then_inc(dve_done, dve_p.step(("mix_n", l, a)))
                dve.wait_ge(pe_done, at(("oB", l, HB - 1)))
                transposed_out(l, "mix_n", G("out_g", l))
                if l % 2 == 0:
                    for q in range(SPLIT):
                        rest(l, q)
                for n in range(2):
                    for a in range(TT):
                        dve.wait_ge(unit_used if a else pe_done, at(("proj", l, n, a)))
                        part = xres[:, a, n * CH:(n + 1) * CH]
                        nc.vector.tensor_tensor(part, ps[:, 4 + 2 * n + a, :], part, ALU.add).then_inc(dve_done, dve_p.step(("proj_add", l, 2 * n + a)))
                row_norm(l, "ffn_n")
                dve.wait_ge(unit_used, at(("proj", l, 1, 1)))
                if l % 2:
                    transposed_out(l, "ffn_n", G("ffn_g", l))
                    return
                for k in range(KD):
                    dve.wait_ge(act_done, at(("hT_hi", l, k // 2)))
                    nc.vector.scalar_tensor_tensor(hT_lo[:, k, :], ps[:, k // 2, (k % 2) * T:(k % 2 + 1) * T],
                                                   G("ffn_g", l)[:, k:k + 1], hT_hi[:, k, :].bitcast(F32),
                                                   ALU.mult, ALU.subtract).then_inc(dve_done, dve_p.step(("ffn_n_done", l, k // 2)))

            def rest(l, q):
                (kind, c), r = D_PIECES[q]
                dve.wait_ge(act_done, at(("lead", l, q)))
                nc.vector.tensor_tensor(d_lo[:, q % SPLIT, :], slot_of(UNIT_NO[kind, l, c])[:, r * PIECE:(r + 1) * PIECE],
                                        d_hi[:, q % SPLIT, :].bitcast(F32), ALU.subtract).then_inc(dve_done, dve_p.step(("rest", l, q)))

            def dense(l):
                for q in range(SPLIT, len(D_PIECES) + 2):
                    if q < len(D_PIECES):
                        rest(l, q)
                    for c in range(len(FF_CHUNKS)):
                        w = FF_CHUNKS[c] // P * T
                        if q == D_LAST["gate", c] + SPLIT + 1:
                            dve.wait_ge(act_done, at(("sig", l, c)))
                            nc.vector.tensor_tensor(gated_d[:, 0:w], ps[:, 0:w // 512, :].rearrange("p b n -> p (b n)"),
                                                    sig_d[:, 0:w], ALU.mult).then_inc(dve_done, dve_p.step(("gated", l, c)))
                        if q == D_LAST["up", c] + SPLIT:
                            dve.wait_ge(dve_done, own())
                            nc.vector.tensor_tensor(hidden_d[:, 0:w], ps[:, 2:2 + w // 512, :].rearrange("p b n -> p (b n)"),
                                                    gated_d[:, 0:w], ALU.mult).then_inc(dve_done, dve_p.step(("hidden", l, c)))
                        if q == D_LAST["up", c] + SPLIT + 2:
                            dve.wait_ge(act_done, at(("hid_hi", l, c)))
                            nc.vector.tensor_tensor(hid_lo[:, c % 2, 0:w], hidden_d[:, 0:w],
                                                    hid_hi[:, c % 2, 0:w].bitcast(F32), ALU.subtract).then_inc(dve_done, dve_p.step(("hid_lo", l, c)))
                dve.wait_ge(pe_done, at(("piece", l, len(D_PIECES) - 1)))
                for a in range(TT):
                    for n in range(2):
                        part = xres[:, a, n * CH:(n + 1) * CH]
                        nc.vector.tensor_tensor(part, ps[:, 4 + 2 * a + n, :], part, ALU.add).then_inc(dve_done, dve_p.step(("ffn_add", l)))

            def route():
                iota8 = C("iota")[:, 0:NE]
                nc.vector.memset(rankm[:], -1.0).then_inc(dve_done, dve_p.step())
                dve.wait_ge(dve_done, own())
                nc.vector.memset(gates[:], 0.0).then_inc(dve_done, dve_p.step())
                dve.wait_ge(dve_done, own())
                dve.wait_ge(pe_done, at("logits"))
                logits = stat_a[:, 0:16].rearrange("p (a n) -> p a n", a=TT)
                nc.vector.tensor_copy(stat_a[:, 0:16], ps[:, 4, 0:2 * NE]).then_inc(dve_done, dve_p.step())
                dve.wait_ge(dve_done, own())
                for a in range(TT):
                    nc.vector.max(top[:, a, :], logits[:, a, :]).then_inc(dve_done, dve_p.step())
                    dve.wait_ge(dve_done, own())
                    nc.vector.max_index(top_at[:, a, :], top[:, a, :], logits[:, a, :]).then_inc(dve_done, dve_p.step())
                    dve.wait_ge(dve_done, own())
                found = stat_a[:, 16:32].rearrange("p (a n) -> p a n", a=TT)
                nc.vector.tensor_copy(found, top_at[:]).then_inc(dve_done, dve_p.step())
                dve.wait_ge(dve_done, own())
                gap = stat_a[:, 32:34].rearrange("p (a o) -> p a o", a=TT)
                nc.vector.tensor_tensor(gap, top[:, :, 0:1], top[:, :, 1:2], ALU.subtract).then_inc(dve_done, dve_p.step("gap"))
                dve.wait_ge(dve_done, own())
                dve.wait_ge(act_done, at("first_gate"))
                g1, g2 = stat_a[:, 34:36], stat_a[:, 36:38]
                nc.vector.tensor_scalar(stat_a[:, 38:40], g2, 1.0, None, ALU.add).then_inc(dve_done, dve_p.step())
                dve.wait_ge(dve_done, own())
                nc.vector.reciprocal(g1, stat_a[:, 38:40]).then_inc(dve_done, dve_p.step())
                dve.wait_ge(dve_done, own())
                nc.vector.tensor_tensor(g2, g2, g1, ALU.mult).then_inc(dve_done, dve_p.step())
                dve.wait_ge(dve_done, own())
                one = stat_a[:, 40:72].rearrange("p (i a n) -> p i a n", i=2, a=TT)
                for a in range(TT):
                    for i in range(2):
                        nc.vector.tensor_scalar(one[:, i, a, :], iota8, found[:, a, i:i + 1], None, ALU.is_equal).then_inc(dve_done, dve_p.step())
                        dve.wait_ge(dve_done, own())
                nc.vector.tensor_tensor(sel[:], one[:, 0], one[:, 1], ALU.add).then_inc(dve_done, dve_p.step("selected"))
                dve.wait_ge(dve_done, own())
                for a in range(TT):
                    nc.vector.tensor_scalar(one[:, 0, a, :], one[:, 0, a, :], g1[:, a:a + 1], None, ALU.mult).then_inc(dve_done, dve_p.step())
                    dve.wait_ge(dve_done, own())
                    nc.vector.scalar_tensor_tensor(gates[:, a, 0:NE], one[:, 1, a, :], g2[:, a:a + 1],
                                                         one[:, 0, a, :], ALU.mult, ALU.add).then_inc(dve_done, dve_p.step())
                    dve.wait_ge(dve_done, own())
                dve.wait_ge(pe_done, at("ranks"))
                nc.vector.scalar_tensor_tensor(rankm[:, :, 0:NE],
                                                     ps[:, 5, 0:2 * NE].rearrange("p (a n) -> p a n", a=TT), 1.0,
                                                     sel[:], ALU.add, ALU.mult).then_inc(dve_done, dve_p.step())
                dve.wait_ge(dve_done, own())
                nc.vector.tensor_scalar(rankm[:, :, 0:NE], rankm[:, :, 0:NE], -1.0, None, ALU.add).then_inc(dve_done, dve_p.step())
                dve.wait_ge(dve_done, own())
                nc.vector.tensor_reduce(over[:, 0:1], ps[:, 5, 2 * NE:3 * NE], AX.X, ALU.max).then_inc(dve_done, dve_p.step())
                dve.wait_ge(dve_done, own())
                nc.vector.tensor_scalar(over[:, 1:2], over[:, 0:1], float(GROUP), None, ALU.is_gt).then_inc(dve_done, dve_p.step())
                dve.wait_ge(dve_done, own())
                nc.vector.tensor_copy(over_i[0:1, 0:1], over[0:1, 1:2]).then_inc(dve_done, dve_p.step("overflow"))
                dve.wait_ge(dve_done, own())

            def experts(g):
                slots = C("iota")[:, g * GROUP:(g + 1) * GROUP]

                def picks(key, e):
                    for a in range(TT):
                        r = rankm[:, a, 0:1] if e is None else rankm[:, a, bass.ds(e + 1, 1)]
                        w = gates[:, a, 0:1] if e is None else gates[:, a, bass.ds(e + 1, 1)]
                        nc.vector.tensor_scalar(pick[:, a, :], slots, r, None, ALU.is_equal).then_inc(dve_done, dve_p.step())
                        nc.vector.tensor_scalar(pick_g[:, a, :], slots, r, w, ALU.is_equal, ALU.mult).then_inc(dve_done, dve_p.step((g, key, "pick")))

                def add(it, key):
                    for q, bank in enumerate(SCATTER_BANKS):
                        dve.wait_ge(pe_done, at((g, "scatter" + key, q), it))
                        a, n = q // 2, q % 2
                        part = xres[:, a, n * CH:(n + 1) * CH]
                        nc.vector.tensor_tensor(part, ps[:, bank, :], part, ALU.add).then_inc(dve_done, dve_p.step((g, "add" + key, q)))

                def gathered_rest(key, it=None):
                    for n in range(2):
                        dve.wait_ge(act_done, at((g, key, "xgT_hi", n), it))
                        for k in range(4 * n, 4 * n + 4):
                            nc.vector.scalar_tensor_tensor(xgT_lo[:, k, :], ps[:, 6 + n, (k % 4) * P:(k % 4 + 1) * P],
                                                           G("ffn_g", DEPTH - 1)[:, k:k + 1],
                                                           xgT_hi[:, k, :].bitcast(F32), ALU.mult,
                                                           ALU.subtract).then_inc(dve_done, dve_p.step((g, key, "xgT_lo")))

                if g:
                    dve.wait_ge(pe_done, at((0, "scatter_end", 3)))
                    dve.wait_ge(act_done, at((0, "y_out_end")))
                nc.vector.memset(ps[:, 4:6, :].rearrange("p b n -> p (b n)"), 0.0).then_inc(dve_done, dve_p.step())
                nc.vector.memset(pick_gT[:].rearrange("p a s -> p (a s)"), 0.0).then_inc(dve_done, dve_p.step((g, "pass")))
                picks("first", None)
                gathered_rest("first")
                dve_p.enter(("experts", g))
                with dve.Fori(0, NE) as e:
                    for q, ((kind, c), r) in enumerate(E_PIECES):
                        no = N_UNITS + g * NE * M_UNITS + MOE_NO[kind, c]
                        dve.wait_ge(act_done, at((g, "lead", q), e))
                        nc.vector.tensor_tensor(e_lo[:, q % SPLIT, :], slot_of(no)[:, r * PIECE:(r + 1) * PIECE],
                                                e_hi[:, q % SPLIT, :].bitcast(F32), ALU.subtract).then_inc(dve_done, dve_p.step((g, "rest", q)))
                        if q in AT_HIDT:
                            n = AT_HIDT[q]
                            dve.wait_ge(act_done, at((g, "hidT_hi", n), e))
                            nc.vector.tensor_tensor(hidT_lo[:, n % 2, :], ps[:, 7 if n % 2 == 0 else 6, :],
                                                    hidT_hi[:, n % 2, :].bitcast(F32), ALU.subtract).then_inc(dve_done, dve_p.step((g, "hidT_lo", n)))
                        if q in AT_GATED:
                            n = AT_GATED[q]
                            dve.wait_ge(act_done, at((g, "sig", n), e))
                            nc.vector.tensor_tensor(gated[:], ps[:, n % 2, :], sig[:, n % 2, :], ALU.mult).then_inc(dve_done, dve_p.step((g, "gated", n)))
                        if q in AT_HID:
                            n = AT_HID[q]
                            dve.wait_ge(dve_done, at((g, "gated", n), e))
                            nc.vector.tensor_tensor(hid[:, n % 2, :], ps[:, 2 + n % 2, :], gated[:], ALU.mult).then_inc(dve_done, dve_p.step((g, "hid", n)))
                        if q == AT_ADD:
                            add(e, "")
                        if q == AT_PICKS:
                            picks("next", e)
                        if q == AT_GATHERED:
                            gathered_rest("next", e)
                dve_p.leave(NE)
                add(None, "_end")
                dve.wait_ge(dve_done, own())

            layer_mixers(0)
            dense(0)
            layer_mixers(1)
            route()
            experts(0)
            more = dve.value_load(over_i[0:1, 0:1], min_val=0, max_val=1)
            with dve.If(more > 0):
                experts(1)
            nc.vector.memset(over[0:1, 2:3], 0.0).then_inc(result_ready, 1)

    return marks


def constants():
    c = np.zeros((P, N_CONST), np.float32)

    def put(name, value):
        a, w = CONST[name]
        c[:, a:a + w] = np.reshape(value, (-1, w))

    p = np.arange(P)[:, None]
    n = np.arange(P)[None, :]
    put("ident", p == n)
    half = ROPE // 2
    inv = (np.float32(10000.0) ** (-np.arange(half, dtype=np.float32) / np.float32(half))).astype(np.float32)
    pos = (np.arange(TT)[None, :] * P + p).astype(np.float32)
    ang = (pos[:, :, None] * inv).astype(np.float32)
    put("cos", np.cos(ang))
    put("sin", np.sin(ang))
    dist = np.concatenate([p - n, p + P - np.arange(T)[None, :]], 1)
    put("causal", np.where(dist >= 0, 0.0, NEG))
    put("negdist", np.where((dist >= 0) & (dist < P), -dist, NEG))
    before = np.concatenate([p < np.arange(T)[None, :], p < n], 1)
    put("stick_add", np.where(before, 0.0, NEG))
    put("stick_mul", before)
    put("neg_tri", -(p >= n).astype(np.float32))
    put("neg_ones", -1.0 * np.ones((P, P)))
    put("ones", np.ones((P, P)))
    put("rank_tri", p < n)
    put("iota", np.broadcast_to(np.arange(2 * GROUP), (P, 2 * GROUP)))
    swa = [HD ** -0.5 * 2.0 ** (h + 1) for h in range(HB)] + [1.0] * HKV
    put("swa_scale", np.broadcast_to(np.tile(swa, TT), (P, TT * (HB + HKV))))
    put("mla_scale", np.broadcast_to(np.tile([QK ** -0.5] * HA + [1.0] * HA, TT), (P, TT * 2 * HA)))
    return c


def small_weights(i):
    s = np.zeros((P, N_SMALL), np.float32)
    for l in range(DEPTH):
        for name, v in (("attn_g", i["attn_norm_g"][l]), ("ffn_g", i["ffn_norm_g"][l]), ("out_g", i["out_norm_g"][l]),
                        ("cq_g", i["mla_cq_norm_g"][l]), ("ckv_g", i["mla_ckv_norm_g"][l])):
            a, w = SMALL[name, l]
            s[:, a:a + w] = v.reshape(w, P).T
        for name, v in (("swa_q_g", i["swa_qn_g"][l]), ("swa_k_g", i["swa_kn_g"][l])):
            a, _ = SMALL[name, l]
            s[:, a] = np.concatenate([v, v])
        for name, v in (("qn_g", i["mla_qn_g"][l]), ("kn_g", i["mla_kn_g"][l]), ("sinks", i["swa_sinks"][l])):
            a, w = SMALL[name, l]
            s[:, a:a + w] = v[None, :]
    a, w = SMALL["router"]
    s[:, a:a + w] = i["router_w"][0].reshape(KD, P, NE).transpose(1, 0, 2).reshape(P, w)
    return s


def kernel(**inputs):
    import concourse.bacc as bacc
    from concourse.bass_utils import run_bass_kernel_spmd

    arrays = {name: np.ascontiguousarray(inputs[key]) for name, key in (
        ("x", "x"), ("w_in", "w_in"), ("w_uq", "mla_w_uq"), ("w_ukv", "mla_w_ukv"), ("w_out", "w_out"),
        ("dense_g", "dense_w_gate"), ("dense_u", "dense_w_up"), ("dense_d", "dense_w_down"),
        ("moe_g", "moe_w_gate"), ("moe_u", "moe_w_up"), ("moe_d", "moe_w_down"))}
    arrays["smalls"] = small_weights({k: np.asarray(v) for k, v in inputs.items()})
    arrays["cst"] = constants()
    known = None
    for _ in range(2):
        nc = bacc.Bacc("TRN2", target_bir_lowering=False, num_devices=1, dynamic_dma_scratch_size=1024)
        aps = {n: nc.dram_tensor(n, a.shape, F32, kind="ExternalInput").ap() for n, a in arrays.items()}
        out = nc.dram_tensor("out", (1, T, D), F32, kind="ExternalOutput").ap()
        known = trunk_program(nc, known, out=out, **aps)
    r = run_bass_kernel_spmd(nc, [arrays], core_ids=[0])
    return r.results[0]["out"]
```

```python
from contextlib import ExitStack

import numpy as np

import concourse.bass as bass
from concourse import mybir

F32 = mybir.dt.float32
F32R = mybir.dt.float32r
I32 = mybir.dt.int32
U32 = mybir.dt.uint32
ALU = mybir.AluOpType
ACT = mybir.ActivationFunctionType
AX = mybir.AxisListType

P = 128
D = 1024
T = 256
TT = T // P
KD = D // P
DEPTH = 2
HD = 64
QR, KVR, NOPE, ROPE = 256, 128, 64, 32
HA, HB, HKV, HC = 4, 8, 2, 4
QK = NOPE + ROPE
C_CKV = QR
C_KPE = QR + KVR
C_BQ = C_KPE + ROPE
C_BK = C_BQ + HB * HD
C_BV = C_BK + HKV * HD
C_CQ = C_BV + HKV * HD
C_CK = C_CQ + HC * HD
C_CV = C_CK + HC * HD
IN_COLS = C_CV + HC * HD
COL_CHUNKS = [(0, C_BQ), (C_BQ, 512), (C_BQ + 512, 512), (C_BQ + 1024, 512)]
FF = 2816
NE = 8
FE = 3584
CH = 512
NCH = FE // CH
EPS = 1e-6
NEG = -1e30
SCATTER_BANKS = (1, 3, 6, 7)
SEG = 3 * P
GROUP = P

CONST = {}
_at = 0
for _name, _w in (("ident", P), ("cos", TT * 16), ("sin", TT * 16), ("causal", SEG), ("negdist", SEG),
                  ("stick_add", SEG), ("stick_mul", SEG), ("neg_tri", P), ("neg_ones", P), ("ones", P),
                  ("rank_tri", P), ("iota", 2 * GROUP), ("swa_scale", TT * (HB + HKV)), ("mla_scale", TT * 2 * HA)):
    CONST[_name] = (_at, _w)
    _at += _w
N_CONST = _at

SMALL = {}
_at = 0
for _l in range(DEPTH):
    for _name, _w in (("attn_g", KD), ("ffn_g", KD), ("out_g", KD), ("cq_g", 2), ("ckv_g", 1), ("swa_q_g", 1),
                      ("swa_k_g", 1), ("qn_g", QK), ("kn_g", QK), ("sinks", HB)):
        SMALL[_name, _l] = (_at, _w)
        _at += _w
SMALL["router"] = (_at, KD * NE)
N_SMALL = _at + KD * NE

RING = 7
UNIT = KD * CH
UNITS = []
for _l in range(DEPTH):
    UNITS += [("in", _l, n) for n in range(4)] + [("out", _l, n) for n in range(2)]
    if _l % 2 == 0:
        _last = (FF + CH - 1) // CH - 1
        UNITS += [("gate", _l, 0), ("up", _l, 0)]
        UNITS += [(w, _l, n - (w == "down")) for n in range(1, _last + 1) for w in ("gate", "up", "down")]
        UNITS.append(("down", _l, _last))
UNIT_NO = {u: n for n, u in enumerate(UNITS)}
N_UNITS = len(UNITS)
MOE_UNITS = [("g", 0), ("u", 0)]
for _c in range(1, NCH):
    MOE_UNITS += [("g", _c), ("u", _c), ("d", _c - 1)]
MOE_UNITS.append(("d", NCH - 1))
MOE_NO = {u: n for n, u in enumerate(MOE_UNITS)}
M_UNITS = len(MOE_UNITS)
T_BANK = [7 if c % 2 == 0 else 6 for c in range(NCH - 1)] + [0]
assert M_UNITS % RING == 0

PIECE = 1024
SPLIT = 4
PER_UNIT = UNIT // PIECE
FF_TILES = FF // P
FF_CHUNKS = [min(CH, FF - n) for n in range(0, FF, CH)]


def pieces_of(units, widths):
    pieces, first, last = [], {}, {}
    for kind, c in units:
        first[kind, c] = len(pieces)
        pieces += [((kind, c), r) for r in range(widths[c] * KD // PIECE)]
        last[kind, c] = len(pieces) - 1
    return pieces, first, last


DENSE_UNITS = [("gate", 0), ("up", 0)]
for _c in range(1, len(FF_CHUNKS)):
    DENSE_UNITS += [("gate", _c), ("up", _c), ("down", _c - 1)]
DENSE_UNITS.append(("down", len(FF_CHUNKS) - 1))
L_PIECES, L_FIRST, L_LAST = [], [], []
for _l in range(DEPTH):
    _pieces = pieces_of([("out", 0), ("out", 1)] + (DENSE_UNITS if _l % 2 == 0 else []),
                        [CH, CH] + FF_CHUNKS[2:])
    for _list, _part in zip((L_PIECES, L_FIRST, L_LAST), _pieces):
        _list.append(_part)
N_OUT = 2 * PER_UNIT
IN_SPLIT = 3
UP_AT = 10
IN_PIECES = [(n, r) for n in range(len(COL_CHUNKS)) for r in range(KD // 2)]
E_PIECES, E_FIRST, E_LAST = pieces_of(MOE_UNITS, [CH] * NCH)
N_E = len(E_PIECES)
assert N_E % SPLIT == 0
AT_Y_OUT, AT_ADD, AT_PICK_GT, AT_PICKS, AT_GATHERED = SPLIT - 1, 2 * SPLIT - 1, 4 * SPLIT + 1, 47, N_E - 1
T_LAST = N_E - 6
AT_SIG = {E_LAST["g", c] + SPLIT: c for c in range(NCH)}
AT_GATED = {E_LAST["g", c] + SPLIT + 1: c for c in range(NCH)}
AT_HID = {E_LAST["u", c] + SPLIT: c for c in range(NCH)}
AT_HIDT = {(E_LAST["g", c + 1] + SPLIT + 1 if c < NCH - 1 else T_LAST + SPLIT): c for c in range(NCH)}


class Progress:

    def __init__(self, name, marks):
        self.name, self.marks, self.n, self.loop, self.start = name, marks, 0, None, 0

    def step(self, key=None):
        self.n += 1
        if key is not None:
            self.marks[key] = (self.name, self.loop, self.start, self.n - self.start if self.loop else self.n)
        return 1

    def enter(self, loop):
        self.loop, self.start = loop, self.n

    def leave(self, trips):
        k = self.n - self.start
        self.marks["per", self.loop, self.name] = k
        self.n = self.start + trips * k
        self.loop = None


class Counts:

    def __init__(self, known):
        self.known = known

    def at(self, key, it=None, back=0):
        if self.known is None:
            return 1 if it is None else it + 1
        name, loop, start, m = self.known[key]
        if loop is None:
            return m
        k = self.known["per", loop, name]
        if it is None:
            return start + (NE - 1) * k + m
        assert start + m - back * k > 0
        return it * k + (start + m - back * k)

    def own(self, progress, it=None):
        if progress.loop is None:
            return progress.n
        if self.known is None:
            return it + 1
        return it * self.known["per", progress.loop, progress.name] + progress.n


def trunk_program(nc, known, x, cst, smalls, w_in, w_uq, w_ukv, w_out, dense_g, dense_u, dense_d, moe_g, moe_u,
                  moe_d, out):
    marks = {}
    counts = Counts(known)
    with ExitStack() as ctx:
        def sb(name, shape, dt=F32):
            return ctx.enter_context(nc.sbuf_tensor(name, shape, dt))

        def sem(name):
            return ctx.enter_context(nc.semaphore(name))

        ring = sb("ring", [P, RING, UNIT])
        xres = sb("xres", [P, TT, D])
        consts = sb("consts", [P, N_CONST])
        small = sb("small", [P, N_SMALL])
        with ExitStack() as stage:
            in_hT_hi = stage.enter_context(nc.sbuf_tensor("in_hT_hi", [P, KD, T], F32R))
        hT = sb("hT", [P, KD, T])
        xn = sb("xn", [P, TT, D])
        uq = sb("uq", [P, 2, HA * QK])
        ukv = sb("ukv", [P, HA * (NOPE + HD)])
        stat = sb("stat", [P, 96])
        stat_a = sb("stat_a", [P, 96])
        stat_t = sb("stat_t", [P, 20])
        top = sb("top", [P, TT, 8])
        top_at = sb("top_at", [P, TT, 8], U32)
        sel = sb("sel", [P, TT, NE])
        over = sb("over", [P, 4])
        over_i = sb("over_i", [1, 1], I32)
        rankm = sb("rankm", [P, TT, NE + 1])
        gates = sb("gates", [P, TT, NE + 1])
        ps = ctx.enter_context(nc.psum_tensor("ps", [P, 8, 512], F32))

        with ExitStack() as stage:
            def sb_stage(name, shape, dt=F32):
                return stage.enter_context(nc.sbuf_tensor(name, shape, dt))
            cols = sb_stage("cols", [P, TT, IN_COLS])
            scratch = sb_stage("scratch", [P, 8 * SEG])
            mla_v = sb_stage("mla_v", [P, TT, HA * HD])
            with ExitStack() as projection:
                in_hT_lo, in_hi, in_lo = (projection.enter_context(nc.sbuf_tensor(n, shape, F32R)) for n, shape in (
                    ("in_hT_lo", [P, KD, T]), ("in_hi", [P, IN_SPLIT, PIECE]), ("in_lo", [P, IN_SPLIT, PIECE])))
            mla_T = sb_stage("mla_T", [P, 2 * HA, T])
            swa_qT = sb_stage("swa_qT", [P, HB // 2, T])
            swa_kT = sb_stage("swa_kT", [P, T])
            stick_qT = sb_stage("stick_qT", [P, HC // 2, T])
            stick_kT = sb_stage("stick_kT", [P, HC // 2, T])
            stick = sb_stage("stick", [P, HC, SEG])
        with ExitStack() as stage:
            def sb_stage(name, shape, dt=F32):
                return stage.enter_context(nc.sbuf_tensor(name, shape, dt))
            d_hi = sb_stage("d_hi", [P, SPLIT, PIECE], F32R)
            d_lo = sb_stage("d_lo", [P, SPLIT, PIECE], F32R)
            hT_hi = sb_stage("hT_hi", [P, KD, T], F32R)
            hT_lo = sb_stage("hT_lo", [P, KD, T], F32R)
            hid_hi = sb_stage("hid_hi", [P, 2, 4 * T], F32R)
            hid_lo = sb_stage("hid_lo", [P, 2, 4 * T], F32R)
        with ExitStack() as stage:
            def sb_stage(name, shape, dt=F32):
                return stage.enter_context(nc.sbuf_tensor(name, shape, dt))
            e_hi = sb_stage("e_hi", [P, SPLIT, PIECE], F32R)
            e_lo = sb_stage("e_lo", [P, SPLIT, PIECE], F32R)
            xgT_hi = sb_stage("xgT_hi", [P, KD, GROUP], F32R)
            xgT_lo = sb_stage("xgT_lo", [P, KD, GROUP], F32R)
            hidT_hi = sb_stage("hidT_hi", [P, 2, CH], F32R)
            hidT_lo = sb_stage("hidT_lo", [P, 2, CH], F32R)
            pick = sb_stage("pick", [P, TT, GROUP], F32R)
            xn_hi = sb_stage("xn_hi", [P, TT, D], F32R)
            xn_lo = sb_stage("xn_lo", [P, TT, D], F32R)
            pick_g = sb_stage("pick_g", [P, TT, GROUP])
            pick_gT = sb_stage("pick_gT", [P, TT, P])

        probsT = hT[:, :, :].rearrange("p k t -> p (k t)")[:, 0:4 * SEG].rearrange("p (h s) -> p h s", h=4)
        qk = xn[:, :, :].rearrange("p a d -> p (a d)")[:, 0:TT * 2 * HA * QK].rearrange(
            "p (a h d) -> p a h d", a=TT, h=2 * HA)
        mixed = xn
        S = scratch[:, :].rearrange("p (h s) -> p h s", h=8)
        cqT = scratch[:, 0:512].rearrange("p (c t) -> p c t", c=2)
        ckvT = scratch[:, 512:768]
        mla_sq = scratch[:, 768:768 + 1536]
        rope_t = scratch[:, 768:768 + 1024].rearrange("p (n a h d) -> p n a h d", n=4, a=TT, h=2 * HA)
        swa_sq = [scratch[:, c0:c0 + 640] for c0 in (0, 1792)]
        swa_q = scratch[:, 2048:3072].rearrange("p (a n) -> p a n", a=TT)
        junk = stick[:, :, :].rearrange("p h s -> p (h s)")
        junk_x = xn[:, 0, :]
        hT_flat = hT[:, :, :].rearrange("p k t -> p (k t)")
        sig = hT_flat[:, 0:1024].rearrange("p (b n) -> p b n", b=2)
        hid = hT_flat[:, 1024:2048].rearrange("p (b n) -> p b n", b=2)
        ysb, gated = xn[:, 0, :], xn[:, 1, 0:CH]
        sig_d, gated_d = hT_flat[:, 0:1024], hT_flat[:, 1024:2048]
        hidden_d = xn[:, 0, :]

        def C(name):
            a, w = CONST[name]
            return consts[:, a:a + w]

        def G(name, l=None):
            a, w = SMALL[name] if l is None else SMALL[name, l]
            return small[:, a:a + w]

        ident = C("ident")

        pe_done, act_done, dve_done = sem("pe_done"), sem("act_done"), sem("dve_done")
        pe_p, act_p, dve_p = (Progress(n, marks) for n in ("pe", "act", "dve"))
        at = counts.at
        x_loaded, ident_loaded, const_loaded, small_loaded = (sem(n) for n in (
            "x_loaded", "ident_loaded", "const_loaded", "small_loaded"))
        up_loaded = sem("up_loaded")
        slot_loaded = [sem(f"slot_loaded{n}") for n in range(RING)]
        result_ready, out_stored = sem("result_ready"), sem("out_stored")

        def slot_of(no):
            return ring[:, no % RING, :]

        def loaded(no, it=None):
            v = 16 * (no // RING + 1)
            return slot_loaded[no % RING], v if it is None else it * (16 * M_UNITS // RING) + v

        def cols_in_sbuf(l, n, a):
            return (dve_done if a == 0 else act_done), at(("cols_sb", l, n, a))

        def probs_in_sbuf(l, kind, h):
            return (dve_done if h % 2 else act_done), at(("pT" + kind, l, h))

        block = ctx.enter_context(nc.Block())

        def unit_source(kind, l, n, dst):
            if kind == "in":
                a, w = COL_CHUNKS[n]
                return (dst[:, 0:KD * w].rearrange("p (k n) -> p k n", k=KD),
                        w_in[l].rearrange("(k p) n -> p k n", p=P)[:, :, a:a + w])
            if kind == "out":
                return (dst.rearrange("p (k n) -> p k n", k=KD),
                        w_out[l].rearrange("(k p) n -> p k n", p=P)[:, :, n * CH:(n + 1) * CH])
            w = min(CH, FF - n * CH)
            if kind == "down":
                return (dst[:, 0:w // P * D].rearrange("p (j n) -> p j n", n=D),
                        dense_d[l // 2, n * CH:n * CH + w, :].rearrange("(j p) n -> p j n", p=P))
            src = dense_g if kind == "gate" else dense_u
            return (dst[:, 0:KD * w].rearrange("p (k n) -> p k n", k=KD),
                    src[l // 2].rearrange("(k p) n -> p k n", p=P)[:, :, n * CH:n * CH + w])

        @block.sync
        def _(sp):
            for a in range(TT):
                sp.dma_start(xres[:, a, :], x[0, a * P:(a + 1) * P, :]).then_inc(x_loaded, 16)
            sp.dma_start(ident, cst[:, 0:P]).then_inc(ident_loaded, 16)
            sp.dma_start(small[:], smalls[:]).then_inc(small_loaded, 16)

            def load_up(l):
                sp.dma_start(uq[:], w_uq[l].rearrange("(k p) n -> p k n", p=P)).then_inc(up_loaded, 16)
                sp.dma_start(ukv[:], w_ukv[l]).then_inc(up_loaded, 16)

            def free(no):
                kind, l, n = UNITS[no - RING]
                if kind == "in":
                    return dve_done, at(("in_rest", l, IN_PIECES.index((n, KD // 2 - 1))))
                return dve_done, at(("rest", l, L_LAST[l][kind, n]))

            for no, (kind, l, n) in enumerate(UNITS):
                if no >= RING:
                    sp.wait_ge(*free(no))
                dst, src = unit_source(kind, l, n, slot_of(no))
                sp.dma_start(dst, src).then_inc(slot_loaded[no % RING], 16)
                if no == 1:
                    sp.dma_start(consts[:, P:], cst[:, P:]).then_inc(const_loaded, 16)
                    load_up(0)
                if no == UNIT_NO["down", 0, 0]:
                    sp.wait_ge(pe_done, at(("up_proj", 0)))
                    load_up(1)

            def expert_unit(group, r, e):
                kind, c = MOE_UNITS[r]
                no = N_UNITS + group * NE * M_UNITS + r
                which = bass.ds(e, 1)
                if kind == "d":
                    src = moe_d[0, which, c * CH:(c + 1) * CH, :].rearrange("o (j p) n -> p (o j) n", p=P)
                    dst = slot_of(no).rearrange("p (j n) -> p j n", n=D)
                else:
                    columns = (moe_g if kind == "g" else moe_u)[0, which, :, c * CH:(c + 1) * CH]
                    src = columns.rearrange("o (k p) n -> p (o k) n", p=P)
                    dst = slot_of(no).rearrange("p (k n) -> p k n", k=KD)
                sp.dma_start(dst, src).then_inc(slot_loaded[no % RING], 16)

            def expert_units(group):
                for r in range(RING):
                    if group:
                        sp.wait_ge(dve_done, at((0, "rest", E_LAST[MOE_UNITS[M_UNITS - RING + r]])))
                    else:
                        sp.wait_ge(*free(N_UNITS + r))
                    expert_unit(group, r, 0)
                with sp.Fori(0, NE - 1) as e:
                    for r in range(M_UNITS):
                        sp.wait_ge(dve_done, at((group, "rest", E_LAST[MOE_UNITS[r]]), e))
                        expert_unit(group, (r + RING) % M_UNITS, e if r + RING < M_UNITS else e + 1)
                for r in range(M_UNITS - RING):
                    sp.wait_ge(dve_done, at((group, "rest", E_LAST[MOE_UNITS[r]])))
                    expert_unit(group, r + RING, NE - 1)

            expert_units(0)
            sp.wait_ge(dve_done, at("overflow"))
            more = sp.value_load(over_i[0:1, 0:1], min_val=0, max_val=1)
            with sp.If(more > 0):
                expert_units(1)
            sp.wait_ge(result_ready, 1)
            for a in range(TT):
                sp.dma_start(out[0, a * P:(a + 1) * P, :], xres[:, a, :]).then_inc(out_stored, 16)
            sp.wait_ge(out_stored, 16 * TT)

        @block.tensor
        def _(pe):
            more = []

            def stay_warm(bank, times):
                for _ in range(times):
                    pe.matmul(ps[:, bank, :], ident, consts[:, 0:512], start=True, stop=True)

            def transposes(l, what):
                b0 = 4 if what == "ffn_n" else 0
                if what != "attn_n" or l:
                    stay_warm(0, {"mix_n": 4, "ffn_n": 4, "attn_n": 4}[what])
                for a in range(TT):
                    pe.wait_ge(act_done if a else dve_done, at((what, l, a)))
                for k in range(KD):
                    for a in range(TT):
                        ins = pe.transpose(ps[:, b0 + k // 2, (k % 2) * T + a * P:(k % 2) * T + (a + 1) * P],
                                           xn[:, a, k * P:(k + 1) * P], ident)
                    if k % 2 == 1:
                        ins.then_inc(pe_done, pe_p.step((what + "_T", l, k // 2)))

            def three_passes(out, hi_l, lo_l, hi_r, lo_r, start, stop):
                pe.matmul(out, hi_l, hi_r, start=start, stop=False, skip_group_check=True)
                pe.matmul(out, hi_l, lo_r, start=False, stop=False, skip_group_check=True)
                return pe.matmul(out, lo_l, hi_r, start=False, stop=stop, skip_group_check=True)

            def layer_mixers(l):
                transposes(l, "attn_n")

                def up_projection():
                    pe.wait_ge(dve_done, at(("cqT", l)))
                    pe.wait_ge(up_loaded, 32 * (l + 1))
                    for a in range(TT):
                        for c in range(2):
                            ins = pe.matmul(ps[:, 2 + a, 0:HA * QK], cqT[:, c, a * P:(a + 1) * P], uq[:, c, :],
                                            start=c == 0, stop=c == 1)
                        ins = pe.matmul(ps[:, a, :], ckvT[:, a * P:(a + 1) * P], ukv[:], start=True, stop=True)
                    ins.then_inc(pe_done, pe_p.step(("up_proj", l)))

                def cols_chunk(n):
                    w = COL_CHUNKS[n][1]
                    for a in range(TT):
                        if n >= 2:
                            pe.wait_ge(*cols_in_sbuf(l, n - 2, a))
                    for r in range(KD // 2):
                        q = n * (KD // 2) + r
                        if n == 0:
                            pe.wait_ge(dve_done, at(("attn_n_done", l, r)))
                        if q == UP_AT:
                            up_projection()
                        pe.wait_ge(dve_done, at(("in_rest", l, q)))
                        for a in range(TT):
                            for k in (2 * r, 2 * r + 1):
                                part, tokens = slice(k % 2 * w, (k % 2 + 1) * w), slice(a * P, (a + 1) * P)
                                ins = three_passes(ps[:, 4 + (n * 2 + a) % 4, 0:w], in_hT_hi[:, k, tokens],
                                                   in_hT_lo[:, k, tokens], in_hi[:, q % IN_SPLIT, part],
                                                   in_lo[:, q % IN_SPLIT, part], k == 0, k == KD - 1)
                        ins.then_inc(pe_done, pe_p.step(("in_piece", l, q)))

                cols_chunk(0)
                cols_chunk(1)
                pe.wait_ge(dve_done, at(("cq_n", l)))
                for c in range(3):
                    for a in range(TT):
                        ins = pe.transpose(ps[:, c // 2, (c % 2) * T + a * P:(c % 2) * T + (a + 1) * P],
                                           cols[:, a, c * P:(c + 1) * P], ident)
                ins.then_inc(pe_done, pe_p.step(("cq_T", l)))
                cols_chunk(2)
                cols_chunk(3)
                pe.wait_ge(dve_done, at(("mla_n", l)))
                for j in range(HA):
                    for h in range(2):
                        for a in range(TT):
                            ins = pe.transpose(ps[0:QK, j, h * T + a * P:h * T + (a + 1) * P],
                                               qk[:, a, 2 * j + h, :], ident)
                    ins.then_inc(pe_done, pe_p.step(("mla_T", l, j)))
                for a in range(TT):
                    pe.wait_ge(*cols_in_sbuf(l, 2, a))
                pe.wait_ge(const_loaded, 16)
                stay_warm(4, 2)
                pe.wait_ge(dve_done, at(("swa_n", l)))
                for i in range(4):
                    for a in range(TT):
                        ins = pe.transpose(ps[:, 4 + i // 2, (i % 2) * T + a * P:(i % 2) * T + (a + 1) * P],
                                           swa_q[:, a, i * P:(i + 1) * P], ident)
                    if i % 2:
                        ins.then_inc(pe_done, pe_p.step(("swa_q_T", l, i // 2)))
                pe.wait_ge(act_done, at(("mlaT", l, 0)))
                for a in range(TT):
                    ins = pe.transpose(ps[:, 0, a * P:(a + 1) * P], cols[:, a, C_BK:C_BV], ident)
                ins.then_inc(pe_done, pe_p.step(("swa_k_T", l)))
                for a in range(TT):
                    pe.wait_ge(*cols_in_sbuf(l, 3, a))
                for i, c0 in ((0, C_CQ), (1, C_CK)):
                    for j in range(2):
                        for a in range(TT):
                            ins = pe.transpose(ps[:, 6 + i, j * T + a * P:j * T + (a + 1) * P],
                                               cols[:, a, c0 + j * P:c0 + (j + 1) * P], ident)
                    ins.then_inc(pe_done, pe_p.step(("stick_T", l, i)))

                pe.wait_ge(act_done, at(("stickT", l, 0)))
                pe.wait_ge(dve_done, at(("stickT", l, 1)))
                pe.wait_ge(act_done, at(("mlaT", l, 1)))
                stay_warm(1, 1)
                pe.wait_ge(dve_done, at(("stickT", l, 1)))
                for h in range(HC):
                    o, j = HD * (h % 2), h // 2
                    pe.matmul(ps[:, 4 + h, 0:T], stick_kT[o:o + HD, j, 0:P], stick_qT[o:o + HD, j, :],
                              start=True, stop=False, skip_group_check=True)
                    ins = pe.matmul(ps[:, 4 + h, T:SEG], stick_kT[o:o + HD, j, P:T], stick_qT[o:o + HD, j, P:T],
                                    start=False, stop=False, skip_group_check=True)
                    ins.then_inc(pe_done, pe_p.step(("z", l, h)))

                def scores(h, bank, q, k, key):
                    pe.matmul(ps[:, bank, 0:P], q[:, 0:P], k[:, 0:P], start=True, stop=True)
                    ins = pe.matmul(ps[:, bank, P:SEG], q[:, P:T], k[:, 0:T], start=True, stop=True)
                    ins.then_inc(pe_done, pe_p.step(key))

                pe.wait_ge(act_done, at(("swa_kT", l)))
                for h in range(HA):
                    scores(h, h, mla_T[0:QK, h, :], mla_T[0:QK, HA + h, :], ("sA", l, h))

                def swa_scores(h):
                    o = HD * (h // 4)
                    pe.wait_ge(dve_done, at(("sA_read", l, h) if h < 4 else ("sB_read", l, h - 4)))
                    scores(h, h % 4, swa_qT[o:o + HD, h % 4, :], swa_kT[o:o + HD, :], ("sB", l, h))

                for h in range(4):
                    swa_scores(h)

                pe.wait_ge(const_loaded, 16)
                for h in range(HC):
                    pe.wait_ge(dve_done, at(("sp", l, h)))
                    pe.matmul(ps[:, 4 + h, 0:T], C("neg_tri"), stick[:, h, 0:T], start=False, stop=False,
                              skip_group_check=True)
                    pe.matmul(ps[:, 4 + h, P:T], C("neg_ones"), stick[:, h, T:SEG], start=False, stop=False,
                              skip_group_check=True)
                    ins = pe.matmul(ps[:, 4 + h, T:SEG], C("neg_tri"), stick[:, h, T:SEG], start=False, stop=True,
                                    skip_group_check=True)
                    ins.then_inc(pe_done, pe_p.step(("cum", l, h)))

                def probs_T(h, bank, slot, key):
                    for j in range(3):
                        ins = pe.transpose(ps[:, bank, j * P:(j + 1) * P], S[:, slot, j * P:(j + 1) * P], ident)
                    ins.then_inc(pe_done, pe_p.step(key))

                def values(pT, bank, c0, v, key):
                    pe.matmul(ps[:, bank, c0:c0 + HD], pT[:, 0:P], v[0], start=True, stop=True, skip_group_check=True)
                    pe.matmul(ps[:, bank, 256 + c0:256 + c0 + HD], pT[:, P:T], v[0], start=True, stop=False,
                              skip_group_check=True)
                    ins = pe.matmul(ps[:, bank, 256 + c0:256 + c0 + HD], pT[:, T:SEG], v[1], start=False, stop=True,
                                    skip_group_check=True)
                    ins.then_inc(pe_done, pe_p.step(key))

                pe.wait_ge(dve_done, at(("sB_read", l, 0)))
                stay_warm(0, 2)
                for h in range(HA):
                    pe.wait_ge(act_done, at(("pA", l, h)))
                    pe.wait_ge(dve_done, at(("w_read", l, h)))
                    probs_T(h, 4 + h, h, ("pA_T", l, h))
                for h in range(4, HB):
                    swa_scores(h)
                for h in range(HA):
                    pe.wait_ge(*probs_in_sbuf(l, "A", h))
                    values(probsT[:, h, :], 4, h * HD, [mla_v[:, a, h * HD:(h + 1) * HD] for a in range(TT)],
                           ("oA", l, h))
                for h in range(HC):
                    pe.wait_ge(act_done, at(("aC", l, h)))
                    values(stick[:, h, :], 5, h * HD, [cols[:, a, C_CV + h * HD:C_CV + (h + 1) * HD]
                                                      for a in range(TT)], ("oC", l, h))
                for h in range(HB):
                    bank = (6, 7, 0, 1, 3, 6, 7, 0)[h]
                    pe.wait_ge(act_done, at(("pB", l, h)))
                    if bank in (0, 1, 3) and h != 7:
                        pe.wait_ge(dve_done, at(("sB_read", l, 4 + bank)))
                    if h >= 5:
                        pe.wait_ge(*probs_in_sbuf(l, "B", {5: 0, 6: 1, 7: 2}[h]))
                    probs_T(h, bank, (4 + h) % 8, ("pB_T", l, h))
                    if h % 4 == 3:
                        for g in range(h - 3, h + 1):
                            pe.wait_ge(*probs_in_sbuf(l, "B", g))
                            if g == 0:
                                pe.wait_ge(dve_done, at(("sB_read", l, 6)))
                            kv = g // 4
                            values(probsT[:, g % 4, :], 2 if g < 4 else 1, (g % 4) * HD,
                                   [cols[:, a, C_BV + kv * HD:C_BV + (kv + 1) * HD] for a in range(TT)],
                                   ("oB", l, g))

                pe.wait_ge(dve_done, at(("oB_read", l, 1)))
                transposes(l, "mix_n")
                for q in range(N_OUT):
                    (_, n), r = L_PIECES[l][q]
                    if n == 0:
                        pe.wait_ge(dve_done, at(("mix_n_done", l, r)))
                    pe.wait_ge(dve_done, at(("rest", l, q)))
                    for a in range(TT):
                        for k in (2 * r, 2 * r + 1):
                            part, tokens = slice(k % 2 * CH, (k % 2 + 1) * CH), slice(a * P, (a + 1) * P)
                            ins = three_passes(ps[:, 4 + n * 2 + a, :], hT_hi[:, k, tokens], hT_lo[:, k, tokens],
                                               d_hi[:, q % SPLIT, part], d_lo[:, q % SPLIT, part], k == 0,
                                               k == KD - 1)
                    ins.then_inc(pe_done, pe_p.step(("piece", l, q)))
                transposes(l, "ffn_n")

            def dense(l):
                pe.wait_ge(dve_done, at(("proj_add", l, 3)))
                for q in range(N_OUT, len(L_PIECES[l])):
                    (kind, c), r = L_PIECES[l][q]
                    w, slot = FF_CHUNKS[c], q % SPLIT
                    if q == L_FIRST[l][kind, c]:
                        if kind == "gate" and c:
                            pe.wait_ge(dve_done, at(("gated", l, c - 1)))
                        if kind == "up" and c:
                            pe.wait_ge(dve_done, at(("hidden", l, c - 1)))
                        if kind == "down":
                            pe.wait_ge(dve_done, at(("hid_lo", l, c)))
                    if kind == "gate" and c == 0:
                        pe.wait_ge(dve_done, at(("ffn_n_done", l, r)))
                    pe.wait_ge(dve_done, at(("rest", l, q)))
                    if kind == "down":
                        for a in range(TT):
                            tokens = slice(r * T + a * P, r * T + (a + 1) * P)
                            for n in range(2):
                                dims = slice(n * CH, (n + 1) * CH)
                                ins = three_passes(ps[:, 4 + 2 * a + n, :], hid_hi[:, c % 2, tokens],
                                                   hid_lo[:, c % 2, tokens], d_hi[:, slot, dims], d_lo[:, slot, dims],
                                                   c == 0 and r == 0, q == len(L_PIECES[l]) - 1)
                    else:
                        ks = PIECE // w
                        for j in range(w // P):
                            bank = (0 if kind == "gate" else 2) + j // 2
                            for i in range(ks):
                                k, at_w = r * ks + i, slice(i * w + j * P, i * w + (j + 1) * P)
                                ins = three_passes(ps[:, bank, (j % 2) * T:(j % 2 + 1) * T], d_hi[:, slot, at_w],
                                                   d_lo[:, slot, at_w], hT_hi[:, k, :], hT_lo[:, k, :],
                                                   k == 0 and j % 2 == 0, k == KD - 1 and j % 2 == 1)
                    ins.then_inc(pe_done, pe_p.step(("piece", l, q)))

            def experts_prepare():
                l = DEPTH - 1
                pe.wait_ge(small_loaded, 16)
                for i, k in enumerate((0, 1, 4, 5, 2, 3, 6, 7)):
                    if k % 2 == 0:
                        pe.wait_ge(act_done if k < 4 else dve_done, at(("ffn_n_done", l, k // 2)))
                    for a in range(TT):
                        ins = pe.matmul(ps[:, a, 0:NE], hT[:, k, a * P:(a + 1) * P],
                                        G("router")[:, k * NE:(k + 1) * NE], start=i == 0, stop=i == KD - 1)
                ins.then_inc(pe_done, pe_p.step("logits"))
                stay_warm(3, 3)
                pe.wait_ge(dve_done, at("selected"))
                pe.matmul(ps[:, 2, 0:NE], C("rank_tri"), sel[:, 0, :], start=True, stop=True)
                pe.matmul(ps[:, 2, NE:2 * NE], C("ones"), sel[:, 0, :], start=True, stop=False)
                pe.matmul(ps[:, 2, NE:2 * NE], C("rank_tri"), sel[:, 1, :], start=False, stop=True)
                pe.matmul(ps[:, 2, 2 * NE:3 * NE], C("ones"), sel[:, 0, :], start=True, stop=False)
                ins = pe.matmul(ps[:, 2, 2 * NE:3 * NE], C("ones"), sel[:, 1, :], start=False, stop=True)
                ins.then_inc(pe_done, pe_p.step("ranks"))

            def experts(group):
                g = group

                def gather(key, it=None):
                    pe.wait_ge(dve_done, at((g, key, "pick"), it))
                    for n in range(2):
                        if it is not None:
                            pe.wait_ge(dve_done, at((g, "hidT_lo", NCH - 2 - n), it))
                        for k in range(4):
                            for a in range(TT):
                                dims = slice((4 * n + k) * P, (4 * n + k + 1) * P)
                                pe.matmul(ps[:, 6 + n, k * P:(k + 1) * P], xn_hi[:, a, dims], pick[:, a, :],
                                          start=a == 0, stop=False, skip_group_check=True)
                                ins = pe.matmul(ps[:, 6 + n, k * P:(k + 1) * P], xn_lo[:, a, dims], pick[:, a, :],
                                                start=False, stop=a == TT - 1, skip_group_check=True)
                        ins.then_inc(pe_done, pe_p.step((g, key, "gathered", n)))

                def scatter(key, it=None):
                    pe.wait_ge(act_done, at((g, "y_out" + key), it))
                    for q, bank in enumerate(SCATTER_BANKS):
                        a, n = q // 2, q % 2
                        ins = pe.matmul(ps[:, bank, :], pick_gT[:, a, :], ysb[:, n * CH:(n + 1) * CH],
                                        start=True, stop=True)
                        ins.then_inc(pe_done, pe_p.step((g, "scatter" + key, q)))

                if g == 0:
                    stay_warm(6, 3)
                gather("first")
                if g == 0:
                    more.append(pe.value_load(over_i[0:1, 0:1], min_val=0, max_val=1))
                pe.wait_ge(dve_done, at((g, "first", "xgT_lo")))
                pe_p.enter(("experts", g))
                with pe.Fori(0, NE) as e:
                    def hidden_T(c):
                        pe.wait_ge(dve_done, at((g, "hid", c), e))
                        bank = T_BANK[c]
                        if c == 0:
                            pe.wait_ge(dve_done, at((g, "add", 3), e))
                        elif c == 1:
                            pe.wait_ge(act_done, at((g, "pick_gT"), e))
                        elif c < NCH - 1:
                            pe.wait_ge(dve_done, at((g, "hidT_lo", c - 2), e))
                        for j in range(4):
                            ins = pe.transpose(ps[:, bank, j * P:(j + 1) * P], hid[:, c % 2, j * P:(j + 1) * P], ident)
                        ins.then_inc(pe_done, pe_p.step((g, "hid_T", c)))

                    def bank_free(kind, c):
                        if kind == "d":
                            pe.wait_ge(dve_done, at((g, "hidT_lo", c), e))
                        elif kind == "g":
                            if c == 0:
                                pe.wait_ge(dve_done, at((g, "next", "xgT_lo"), e, 1))
                            elif c == 1:
                                pe.wait_ge(dve_done, at((g, "add", 0), e))
                            else:
                                pe.wait_ge(dve_done, at((g, "gated", c - 2), e))
                        elif c == 1:
                            pe.wait_ge(dve_done, at((g, "add", 1), e))
                        elif c:
                            pe.wait_ge(dve_done, at((g, "hid", c - 2), e))

                    for q, ((kind, c), r) in enumerate(E_PIECES):
                        slot = q % SPLIT
                        if r == 0:
                            bank_free(kind, c)
                        pe.wait_ge(dve_done, at((g, "rest", q), e))
                        if kind == "d":
                            rows = slice(r * P, (r + 1) * P)
                            for n in range(2):
                                dims = slice(n * CH, (n + 1) * CH)
                                ins = three_passes(ps[:, 4 + n, :], hidT_hi[:, c % 2, rows], hidT_lo[:, c % 2, rows],
                                                   e_hi[:, slot, dims], e_lo[:, slot, dims], c == 0 and r == 0,
                                                   c == NCH - 1 and r == PER_UNIT - 1)
                        else:
                            for i in range(PIECE // CH):
                                k, part = r * (PIECE // CH) + i, slice(i * CH, (i + 1) * CH)
                                ins = three_passes(ps[:, (0 if kind == "g" else 2) + c % 2, :], xgT_hi[:, k, :],
                                                   xgT_lo[:, k, :], e_hi[:, slot, part], e_lo[:, slot, part], k == 0,
                                                   k == KD - 1)
                        ins.then_inc(pe_done, pe_p.step((g, "piece", q)))
                        if q == E_LAST["g", 0]:
                            scatter("", e)
                        elif q == E_LAST["g", 1]:
                            hidden_T(0)
                            pe.wait_ge(dve_done, at((g, "add", 2), e))
                            for a in range(TT):
                                ins = pe.transpose(ps[:, 6, a * P:(a + 1) * P], pick_g[:, a, :], ident)
                            ins.then_inc(pe_done, pe_p.step((g, "pick_g_T")))
                        elif q == E_LAST[kind, c] and kind == "g":
                            hidden_T(c - 1)
                        elif q == T_LAST:
                            hidden_T(NCH - 1)
                        elif q == E_LAST["d", NCH - 2]:
                            gather("next", e)
                pe_p.leave(NE)
                pe.wait_ge(dve_done, at((g, "next", "xgT_lo")))
                scatter("_end")

            pe.wait_ge(ident_loaded, 16)
            layer_mixers(0)
            dense(0)
            pe.wait_ge(dve_done, at(("ffn_add", 0, 1)))
            layer_mixers(1)
            experts_prepare()
            experts(0)
            with pe.If(more[0] > 0):
                experts(1)

        @block.scalar
        def _(act):
            more = []

            def rstd_of(v, r, key):
                act.wait_ge(dve_done, at((key, "ms")))
                nc.scalar.activation(r, v, ACT.Ln).then_inc(act_done, act_p.step())
                act.wait_ge(act_done, counts.own(act_p))
                nc.scalar.activation(r, r, ACT.Exp, scale=-0.5).then_inc(act_done, act_p.step((key, "r0")))

            def row_stats(l, what):
                for a in range(TT):
                    if what == "attn_n" and l == 0 and a == 0:
                        act.wait_ge(x_loaded, 16 * TT)
                    if what == "attn_n" and l > 0:
                        act.wait_ge(dve_done, at(("ffn_add", l - 1, a)))
                    if what == "ffn_n":
                        act.wait_ge(dve_done, at(("proj_add", l, 2 + a)))
                    if a or l or what != "attn_n":
                        act.wait_ge(act_done, counts.own(act_p))
                    nc.scalar.activation(junk_x, xres[:, a, :], ACT.Square, scale=D ** -0.5,
                                         accum_out=stat[:, a:a + 1]).then_inc(act_done, act_p.step((what, l, "sq", a)))
                rstd_of(stat[:, 2:4], stat[:, 4:6], (what, l))
                act.wait_ge(dve_done, at(((what, l), "r")))
                nc.scalar.activation(xn[:, 1, :], xres[:, 1, :], ACT.Copy,
                                     scale=stat[:, 5:6]).then_inc(act_done, act_p.step((what, l, 1)))

            def transposed_out(l, what, gain):
                for b in range(2):
                    act.wait_ge(pe_done, at((what + "_T", l, b)))
                    for i in range(2):
                        k = 2 * b + i
                        nc.scalar.activation(hT[:, k, :], ps[:, 4 + b, i * T:(i + 1) * T], ACT.Copy,
                                                        scale=gain[:, k:k + 1]).then_inc(act_done, act_p.step((what + "_done", l, b) if i else None))

            def transposed_hi(l, what, gain, hi, with_lead=None):
                b0 = 4 if what == "ffn_n" else 0
                for b in range(4):
                    if with_lead:
                        with_lead(b)
                    act.wait_ge(pe_done, at((what + "_T", l, b)))
                    for k in (2 * b, 2 * b + 1):
                        nc.scalar.activation(hi[:, k, :], ps[:, b0 + b, (k % 2) * T:(k % 2 + 1) * T], ACT.Copy,
                                             scale=gain[:, k:k + 1]).then_inc(act_done, act_p.step((what + "_hi", l, b)))

            def in_lead(l, pieces):
                for q in pieces:
                    n, r = IN_PIECES[q]
                    no, w = UNIT_NO["in", l, n], 2 * COL_CHUNKS[n][1]
                    if r == 0:
                        act.wait_ge(*loaded(no))
                    if q >= IN_SPLIT:
                        act.wait_ge(pe_done, at(("in_piece", l, q - IN_SPLIT)))
                    nc.scalar.activation(in_hi[:, q % IN_SPLIT, 0:w], slot_of(no)[:, r * w:(r + 1) * w],
                                         ACT.Copy).then_inc(act_done, act_p.step(("in_lead", l, q)))

            def cols_out(l, n):
                a0, w = COL_CHUNKS[n]
                act.wait_ge(pe_done, at(("in_piece", l, 4 * n + 3)))
                nc.scalar.activation(cols[:, 1, a0:a0 + w], ps[:, 4 + (n * 2 + 1) % 4, 0:w], ACT.Copy).then_inc(act_done, act_p.step(("cols_sb", l, n, 1)))

            def layer_mixers(l):
                nc.scalar.preload_act_table_set("natural_log_exp_and_others")
                row_stats(l, "attn_n")
                if l == 0:
                    act.wait_ge(small_loaded, 16)
                transposed_hi(l, "attn_n", G("attn_g", l), in_hT_hi, lambda b: in_lead(l, [b]))
                in_lead(l, range(4, 7))
                cols_out(l, 0)
                act.wait_ge(act_done, counts.own(act_p))
                act.wait_ge(dve_done, at(("cols_sb", l, 0, 0)))
                for a in range(TT):
                    for i, (c0, w) in enumerate(((0, QR), (C_CKV, KVR))):
                        nc.scalar.activation(junk_x[:, (2 * a + i) * QR:(2 * a + i) * QR + w],
                                                        cols[:, a, c0:c0 + w], ACT.Square, scale=w ** -0.5,
                                                        accum_out=stat[:, 6 + 2 * a + i:7 + 2 * a + i]).then_inc(act_done, act_p.step(("cq_sq", l, 2 * a + i)))
                rstd_of(stat[:, 10:14], stat[:, 14:18], ("cq", l))
                in_lead(l, range(7, 11))
                cols_out(l, 1)
                in_lead(l, range(11, 13))
                act.wait_ge(pe_done, at(("up_proj", l)))
                for a in range(TT):
                    nc.scalar.activation(
                        qk[:, a, 0:HA, :].rearrange("p h d -> p (h d)"), ps[:, 2 + a, 0:HA * QK], ACT.Copy).then_inc(act_done, act_p.step(("q_read", l)))
                in_lead(l, range(13, 14))
                act.wait_ge(act_done, counts.own(act_p))
                for a in range(TT):
                    act.wait_ge(dve_done, at(("kv_in", l, a)))
                    for h in range(2 * HA):
                        at_s = 18 + 2 * HA * a + h
                        nc.scalar.activation(mla_sq[:, QK * (at_s - 18):QK * (at_s - 17)], qk[:, a, h, :], ACT.Square,
                                             scale=QK ** -0.5, accum_out=stat[:, at_s:at_s + 1]).then_inc(act_done, act_p.step(("mla_sq", l, a)))
                rstd_of(stat[:, 18:34], stat[:, 34:50], ("mla", l))
                in_lead(l, range(14, 15))
                cols_out(l, 2)
                in_lead(l, range(15, 16))
                act.wait_ge(act_done, counts.own(act_p))
                act.wait_ge(dve_done, at(("cols_sb", l, 2, 0)))
                for a in range(TT):
                    for h in range(HB + HKV):
                        at_s = 50 + (HB + HKV) * a + h
                        nc.scalar.activation(swa_sq[a][:, h * HD:(h + 1) * HD],
                                             cols[:, a, C_BQ + h * HD:C_BQ + (h + 1) * HD], ACT.Square,
                                             scale=HD ** -0.5, accum_out=stat[:, at_s:at_s + 1]).then_inc(act_done, act_p.step(("swa_sq", l)))
                rstd_of(stat[:, 50:70], stat[:, 70:90], ("swa", l))
                cols_out(l, 3)
                for j in range(HA):
                    act.wait_ge(pe_done, at(("mla_T", l, j)))
                    nc.scalar.activation(mla_T[0:QK, 2 * j:2 * j + 2, :].rearrange("p h t -> p (h t)"),
                                         ps[0:QK, j, :], ACT.Copy).then_inc(act_done, act_p.step(("mlaT", l, j)))
                act.wait_ge(pe_done, at(("swa_k_T", l)))
                nc.scalar.activation(swa_kT[:], ps[:, 0, 0:T], ACT.Copy, scale=G("swa_k_g", l)).then_inc(act_done, act_p.step(("swa_kT", l)))
                act.wait_ge(pe_done, at(("stick_T", l, 0)))
                nc.scalar.activation(stick_qT[:].rearrange("p j t -> p (j t)"), ps[:, 6, :], ACT.Copy,
                                                scale=HD ** -0.5).then_inc(act_done, act_p.step(("stickT", l, 0)))
                for h in range(HC):
                    act.wait_ge(pe_done, at(("z", l, h)))
                    if h == 0:
                        act.wait_ge(act_done, counts.own(act_p))
                    nc.scalar.activation(stick[:, h, :], ps[:, 4 + h, 0:SEG], ACT.Abs).then_inc(act_done, act_p.step())
                    act.wait_ge(act_done, counts.own(act_p))
                    nc.scalar.activation(stick[:, h, :], stick[:, h, :], ACT.Exp, scale=-1.0).then_inc(act_done, act_p.step())
                    act.wait_ge(act_done, counts.own(act_p))
                    nc.scalar.activation(stick[:, h, :], stick[:, h, :], ACT.Ln, bias=1.0).then_inc(act_done, act_p.step(("ln", l, h)))

                def exps(slot, nm, acc, key):
                    nc.scalar.activation(S[:, slot, 0:P], S[:, slot, 0:P], ACT.Exp, bias=nm[0],
                                                    accum_out=acc[0]).then_inc(act_done, act_p.step())
                    nc.scalar.activation(S[:, slot, P:SEG], S[:, slot, P:SEG], ACT.Exp, bias=nm[1],
                                                    accum_out=acc[1]).then_inc(act_done, act_p.step(key))

                def mean_squares(mixers):
                    act.wait_ge(dve_done, at(("oC_read", l) if 0 in mixers else ("oB_read", l, 1)))
                    act.wait_ge(act_done, counts.own(act_p))
                    act.wait_ge(pe_done, at(("oC", l, HC - 1)))
                    for a in range(TT):
                        for i in mixers:
                            c0, w = ((0, 256), (256, 512), (768, 256))[i]
                            nc.scalar.activation(junk[:, 0:w], mixed[:, a, c0:c0 + w], ACT.Square,
                                                 scale=w ** -0.5,
                                                 accum_out=stat[:, 3 * a + i:3 * a + i + 1]).then_inc(act_done, act_p.step(("mix_sq", l)))
                            act.wait_ge(act_done, counts.own(act_p))

                def head_cols(base, h):
                    return [stat_a[:, base + 8 * (h // 4) + 4 * a + h % 4:base + 8 * (h // 4) + 4 * a + h % 4 + 1]
                            for a in range(TT)]

                act.wait_ge(dve_done, at(("nmA", l)))
                for h in range(HA):
                    exps(h, head_cols(24, h), head_cols(48, h), ("pA", l, h))
                for h in range(HC):
                    act.wait_ge(dve_done, at(("w_read", l, h)))
                    nc.scalar.activation(stick[:, h, :], stick[:, h, :], ACT.Exp).then_inc(act_done, act_p.step(("aC", l, h)))
                for h in (0, 2):
                    act.wait_ge(pe_done, at(("pA_T", l, h)))
                    nc.scalar.activation(probsT[:, h, :], ps[:, 4 + h, 0:SEG], ACT.Copy).then_inc(act_done, act_p.step(("pTA", l, h)))
                for q in range(2):
                    act.wait_ge(dve_done, at(("nmB", l, q)))
                    for h in range(4 * q, 4 * q + 4):
                        exps((4 + h) % 8, head_cols(32, h), head_cols(56, h), ("pB", l, h))
                    nc.scalar.activation(stat_a[:, 72 + 8 * q:80 + 8 * q], stat_a[:, 72 + 8 * q:80 + 8 * q],
                                                    ACT.Exp).then_inc(act_done, act_p.step(("sink_e", l, q)))
                for h in (0, 2, 4, 6):
                    act.wait_ge(pe_done, at(("pB_T", l, h)))
                    act.wait_ge(pe_done, at(("oA", l, h) if h < 4 else ("oB", l, h - 4)))
                    nc.scalar.activation(probsT[:, h % 4, :], ps[:, (6, 7, 0, 1, 3, 6, 7, 0)[h], 0:SEG],
                                         ACT.Copy).then_inc(act_done, act_p.step(("pTB", l, h)))
                mean_squares((0, 2))
                mean_squares((1,))
                rstd_of(stat[:, 6:12], stat[:, 12:18], ("mix", l))
                act.wait_ge(dve_done, at((("mix", l), "r")))
                for i, (c0, w) in enumerate(((0, 256), (256, 512), (768, 256))):
                    nc.scalar.activation(mixed[:, 1, c0:c0 + w], mixed[:, 1, c0:c0 + w], ACT.Copy,
                                         scale=stat[:, 15 + i:16 + i]).then_inc(act_done, act_p.step(("mix_n", l, 1)))
                act.wait_ge(pe_done, at(("oB", l, HB - 1)))
                transposed_hi(l, "mix_n", G("out_g", l), hT_hi, lambda b: lead(l, b))
                for q in range(SPLIT, N_OUT + (SPLIT - 1 if l % 2 == 0 else 0)):
                    lead(l, q)
                row_stats(l, "ffn_n")
                if l % 2 == 0:
                    lead(l, N_OUT + SPLIT - 1)
                if l % 2:
                    transposed_out(l, "ffn_n", G("ffn_g", l))
                else:
                    transposed_hi(l, "ffn_n", G("ffn_g", l), hT_hi)

            def lead(l, q):
                (kind, c), r = L_PIECES[l][q]
                no = UNIT_NO[kind, l, c]
                if r == 0:
                    act.wait_ge(*loaded(no))
                if q >= SPLIT:
                    act.wait_ge(pe_done, at(("piece", l, q - SPLIT)))
                nc.scalar.activation(d_hi[:, q % SPLIT, :], slot_of(no)[:, r * PIECE:(r + 1) * PIECE],
                                     ACT.Copy).then_inc(act_done, act_p.step(("lead", l, q)))

            def dense(l):
                chunks = range(len(FF_CHUNKS))
                for q in range(N_OUT + SPLIT, len(L_PIECES[l])):
                    lead(l, q)
                    for c in chunks:
                        w = FF_CHUNKS[c] // P * T
                        if q == L_LAST[l]["gate", c] + SPLIT:
                            nc.scalar.activation(sig_d[:, 0:w], ps[:, 0:w // 512, :].rearrange("p b n -> p (b n)"),
                                                 ACT.Sigmoid).then_inc(act_done, act_p.step(("sig", l, c)))
                        if q == L_LAST[l]["up", c] + SPLIT + 1:
                            act.wait_ge(dve_done, at(("hidden", l, c)))
                            nc.scalar.activation(hid_hi[:, c % 2, 0:w], hidden_d[:, 0:w],
                                                 ACT.Copy).then_inc(act_done, act_p.step(("hid_hi", l, c)))

            def experts(g):
                def gathered(key, it=None):
                    for n in range(2):
                        act.wait_ge(pe_done, at((g, key, "gathered", n), it))
                        for k in range(4 * n, 4 * n + 4):
                            nc.scalar.activation(xgT_hi[:, k, :], ps[:, 6 + n, (k % 4) * P:(k % 4 + 1) * P], ACT.Copy,
                                                 scale=G("ffn_g", DEPTH - 1)[:, k:k + 1]).then_inc(act_done, act_p.step((g, key, "xgT_hi", n)))

                def y_out(key):
                    nc.scalar.activation(ysb, ps[:, 4:6, :].rearrange("p b n -> p (b n)"), ACT.Copy).then_inc(act_done, act_p.step((g, "y_out" + key)))

                nc.scalar.preload_act_table(ACT.Sigmoid)
                act.wait_ge(dve_done, at((g, "pass")))
                if g == 0:
                    act.wait_ge(dve_done, at("overflow"))
                    more.append(act.value_load(over_i[0:1, 0:1], min_val=0, max_val=1))
                gathered("first")
                act_p.enter(("experts", g))
                with act.Fori(0, NE) as e:
                    for q, ((kind, c), r) in enumerate(E_PIECES):
                        no = N_UNITS + g * NE * M_UNITS + MOE_NO[kind, c]
                        if r == 0:
                            act.wait_ge(*loaded(no, e))
                        act.wait_ge(pe_done, at((g, "piece", q - SPLIT), e) if q >= SPLIT
                                    else at((g, "piece", q - SPLIT + N_E), e, 1))
                        nc.scalar.activation(e_hi[:, q % SPLIT, :], slot_of(no)[:, r * PIECE:(r + 1) * PIECE],
                                             ACT.Copy).then_inc(act_done, act_p.step((g, "lead", q)))
                        if q == AT_Y_OUT:
                            y_out("")
                        if q in AT_SIG:
                            n = AT_SIG[q]
                            nc.scalar.activation(sig[:, n % 2, :], ps[:, n % 2, :], ACT.Sigmoid).then_inc(act_done, act_p.step((g, "sig", n)))
                        if q == AT_PICK_GT:
                            act.wait_ge(pe_done, at((g, "pick_g_T"), e))
                            nc.scalar.activation(pick_gT[:].rearrange("p a s -> p (a s)"), ps[:, 6, 0:2 * P],
                                                 ACT.Copy).then_inc(act_done, act_p.step((g, "pick_gT")))
                        if q in AT_HIDT:
                            n = AT_HIDT[q]
                            act.wait_ge(pe_done, at((g, "hid_T", n), e))
                            nc.scalar.activation(hidT_hi[:, n % 2, :], ps[:, T_BANK[n], :],
                                                 ACT.Copy).then_inc(act_done, act_p.step((g, "hidT_hi", n)))
                        if q == AT_GATHERED:
                            gathered("next", e)
                act_p.leave(NE)
                act.wait_ge(pe_done, at((g, "piece", N_E - 1)))
                y_out("_end")

            layer_mixers(0)
            dense(0)
            layer_mixers(1)
            for a in range(TT):
                nc.scalar.activation(xn_hi[:, a, :], xn[:, a, :], ACT.Copy).then_inc(act_done, act_p.step("xn_hi"))
            act.wait_ge(dve_done, at("gap"))
            nc.scalar.activation(stat_a[:, 36:38], stat_a[:, 32:34], ACT.Exp, scale=-1.0).then_inc(act_done, act_p.step("first_gate"))
            experts(0)
            with act.If(more[0] > 0):
                experts(1)

        @block.vector
        def _(dve):
            more = []

            def own(it=None):
                return counts.own(dve_p, it)

            def refine(v, r, t, key):
                dve.wait_ge(act_done, at((key, "r0")))
                nc.vector.scalar_tensor_tensor(t, r, -0.5, r, ALU.mult, ALU.mult).then_inc(dve_done, dve_p.step())
                dve.wait_ge(dve_done, own())
                nc.vector.tensor_tensor(t, t, v, ALU.mult).then_inc(dve_done, dve_p.step())
                dve.wait_ge(dve_done, own())
                nc.vector.scalar_tensor_tensor(r, t, 1.5, r, ALU.add, ALU.mult).then_inc(dve_done, dve_p.step((key, "r")))
                dve.wait_ge(dve_done, own())

            def row_norm(l, what):
                dve.wait_ge(act_done, at((what, l, "sq", 1)))
                nc.vector.tensor_scalar(stat[:, 2:4], stat[:, 0:2], EPS, None, ALU.add).then_inc(dve_done, dve_p.step(((what, l), "ms")))
                dve.wait_ge(dve_done, own())
                refine(stat[:, 2:4], stat[:, 4:6], stat[:, 90:92], (what, l))
                nc.vector.tensor_scalar(xn[:, 0, :], xres[:, 0, :], stat[:, 4:5], None,
                                        ALU.mult).then_inc(dve_done, dve_p.step((what, l, 0)))

            def transposed_out(l, what, gain):
                for b in (2, 3):
                    dve.wait_ge(pe_done, at((what + "_T", l, b)))
                    for i in range(2):
                        k = 2 * b + i
                        nc.vector.tensor_scalar(hT[:, k, :], ps[:, 4 + b, i * T:(i + 1) * T], gain[:, k:k + 1],
                                                           None, ALU.mult).then_inc(dve_done, dve_p.step((what + "_done", l, b) if i else None))

            def transposed_lo(l, what, gain, hi, lo, with_rest=None):
                b0 = 4 if what == "ffn_n" else 0
                for k in range(KD):
                    if with_rest and k % 2 == 0:
                        with_rest(k // 2)
                    dve.wait_ge(act_done, at((what + "_hi", l, k // 2)))
                    nc.vector.scalar_tensor_tensor(lo[:, k, :], ps[:, b0 + k // 2, (k % 2) * T:(k % 2 + 1) * T],
                                                   gain[:, k:k + 1], hi[:, k, :].bitcast(F32), ALU.mult,
                                                   ALU.subtract).then_inc(dve_done, dve_p.step((what + "_done", l, k // 2)))

            def in_rest(l, pieces):
                for q in pieces:
                    n, r = IN_PIECES[q]
                    w = 2 * COL_CHUNKS[n][1]
                    dve.wait_ge(act_done, at(("in_lead", l, q)))
                    nc.vector.tensor_tensor(in_lo[:, q % IN_SPLIT, 0:w], slot_of(UNIT_NO["in", l, n])[:, r * w:(r + 1) * w],
                                            in_hi[:, q % IN_SPLIT, 0:w].bitcast(F32),
                                            ALU.subtract).then_inc(dve_done, dve_p.step(("in_rest", l, q)))

            def cols_out(l, n):
                a0, w = COL_CHUNKS[n]
                dve.wait_ge(pe_done, at(("in_piece", l, 4 * n + 3)))
                nc.vector.tensor_copy(cols[:, 0, a0:a0 + w], ps[:, 4 + (n * 2) % 4, 0:w]).then_inc(dve_done, dve_p.step(("cols_sb", l, n, 0)))

            def layer_mixers(l):
                row_norm(l, "attn_n")
                if l == 0:
                    dve.wait_ge(small_loaded, 16)
                transposed_lo(l, "attn_n", G("attn_g", l), in_hT_hi, in_hT_lo, lambda b: in_rest(l, [b]))
                in_rest(l, range(4, 7))
                cols_out(l, 0)
                dve.wait_ge(act_done, at(("cq_sq", l, 3)))
                nc.vector.tensor_scalar(stat[:, 10:14], stat[:, 6:10], EPS, None, ALU.add).then_inc(dve_done, dve_p.step((("cq", l), "ms")))
                dve.wait_ge(dve_done, own())
                refine(stat[:, 10:14], stat[:, 14:18], stat[:, 90:94], ("cq", l))
                for a in range(TT):
                    for i, (c0, w) in enumerate(((0, QR), (C_CKV, KVR))):
                        nc.vector.tensor_scalar(cols[:, a, c0:c0 + w], cols[:, a, c0:c0 + w],
                                                           stat[:, 14 + 2 * a + i:15 + 2 * a + i], None, ALU.mult).then_inc(dve_done, dve_p.step(("cq_n", l)))
                in_rest(l, range(7, 11))
                cols_out(l, 1)
                dve.wait_ge(pe_done, at(("cq_T", l)))
                for c in range(2):
                    nc.vector.tensor_scalar(cqT[:, c, :], ps[:, 0, c * T:(c + 1) * T],
                                                       G("cq_g", l)[:, c:c + 1], None, ALU.mult).then_inc(dve_done, dve_p.step())
                nc.vector.tensor_scalar(ckvT, ps[:, 1, 0:T], G("ckv_g", l), None, ALU.mult).then_inc(dve_done, dve_p.step(("cqT", l)))
                in_rest(l, range(11, 13))
                dve.wait_ge(pe_done, at(("up_proj", l)))
                dve.wait_ge(act_done, at(("q_read", l)))
                dve.wait_ge(act_done, at(("cols_sb", l, 0, 1)))
                for a in range(TT):
                    kv = ps[:, a, :].rearrange("p (h d) -> p h d", h=HA)
                    nc.vector.tensor_copy(qk[:, a, HA:, 0:NOPE], kv[:, :, 0:NOPE]).then_inc(dve_done, dve_p.step())
                    nc.vector.tensor_copy(mla_v[:, a, :].rearrange("p (h d) -> p h d", h=HA),
                                                     kv[:, :, NOPE:]).then_inc(dve_done, dve_p.step(("kv_read", l)))
                    nc.vector.tensor_copy(
                        qk[:, a, HA:, NOPE:],
                        cols[:, a, C_KPE:C_BQ].rearrange("p (o d) -> p o d", o=1).broadcast_to([P, HA, ROPE])).then_inc(dve_done, dve_p.step(("kv_in", l, a)))
                in_rest(l, range(13, 14))
                dve.wait_ge(dve_done, own())
                for a in range(TT):
                    dve.wait_ge(act_done, at(("mla_sq", l, a)))
                    if a == TT - 1:
                        nc.vector.tensor_scalar(stat[:, 18:34], stat[:, 18:34], EPS, None, ALU.add).then_inc(dve_done, dve_p.step((("mla", l), "ms")))
                    for i, name in enumerate(("qn_g", "kn_g")):
                        part = qk[:, a, i * HA:(i + 1) * HA, :]
                        nc.vector.tensor_tensor(part, part, G(name, l).rearrange(
                            "p (o d) -> p o d", o=1).broadcast_to([P, HA, QK]), ALU.mult).then_inc(dve_done, dve_p.step())
                in_rest(l, range(14, 15))
                cols_out(l, 2)
                dve.wait_ge(dve_done, own())
                dve.wait_ge(const_loaded, 16)
                x1, x2 = qk[:, :, :, NOPE:NOPE + 16], qk[:, :, :, NOPE + 16:QK]
                cos = C("cos").rearrange("p (a o d) -> p a o d", a=TT, o=1).broadcast_to([P, TT, 2 * HA, 16])
                sin = C("sin").rearrange("p (a o d) -> p a o d", a=TT, o=1).broadcast_to([P, TT, 2 * HA, 16])
                for n, (u, v) in enumerate(((x1, cos), (x2, sin), (x1, sin), (x2, cos))):
                    nc.vector.tensor_tensor(rope_t[:, n], u, v, ALU.mult).then_inc(dve_done, dve_p.step())
                dve.wait_ge(dve_done, own())
                nc.vector.tensor_tensor(x1, rope_t[:, 0], rope_t[:, 1], ALU.subtract).then_inc(dve_done, dve_p.step())
                nc.vector.tensor_tensor(x2, rope_t[:, 2], rope_t[:, 3], ALU.add).then_inc(dve_done, dve_p.step())
                in_rest(l, range(15, 16))
                refine(stat[:, 18:34], stat[:, 34:50], stat_t[:, 0:16], ("mla", l))
                nc.vector.tensor_tensor(stat[:, 34:50], stat[:, 34:50], C("mla_scale"), ALU.mult).then_inc(dve_done, dve_p.step())
                dve.wait_ge(dve_done, own())
                qkg = qk.rearrange("p a h d -> p (a h) d")
                nc.vector.tensor_tensor(qkg, qkg,
                                              stat[:, 34:50].rearrange("p (g o) -> p g o", o=1).broadcast_to(
                                                  [P, 16, QK]), ALU.mult).then_inc(dve_done, dve_p.step(("mla_n", l)))
                dve.wait_ge(act_done, at(("swa_sq", l)))
                nc.vector.tensor_scalar(stat[:, 50:70], stat[:, 50:70], EPS, None, ALU.add).then_inc(dve_done, dve_p.step((("swa", l), "ms")))
                dve.wait_ge(dve_done, own())
                refine(stat[:, 50:70], stat[:, 70:90], stat_t[:, 0:20], ("swa", l))
                nc.vector.tensor_tensor(stat[:, 70:90], stat[:, 70:90], C("swa_scale"), ALU.mult).then_inc(dve_done, dve_p.step())
                dve.wait_ge(dve_done, own())
                for a in range(TT):
                    r = stat[:, 70 + 10 * a:78 + 10 * a].rearrange("p (g i o) -> p i g o", g=2, o=1)
                    nc.vector.tensor_tensor(
                        swa_q[:, a, :].rearrange("p (i g d) -> p i g d", i=4, g=2),
                        cols[:, a, C_BQ:C_BK].rearrange("p (g i d) -> p i g d", g=2, i=4),
                        r.broadcast_to([P, 4, 2, HD]), ALU.mult).then_inc(dve_done, dve_p.step())
                    part = cols[:, a, C_BK:C_BV].rearrange("p (g d) -> p g d", d=HD)
                    r = stat[:, 78 + 10 * a:80 + 10 * a].rearrange("p (g o) -> p g o", o=1)
                    nc.vector.tensor_tensor(part, part, r.broadcast_to([P, HKV, HD]), ALU.mult).then_inc(dve_done, dve_p.step(("swa_n", l)))
                cols_out(l, 3)
                for b in range(2):
                    dve.wait_ge(pe_done, at(("swa_q_T", l, b)))
                    nc.vector.tensor_scalar(swa_qT[:, 2 * b:2 * b + 2, :].rearrange("p i t -> p (i t)"),
                                                       ps[:, 4 + b, :], G("swa_q_g", l), None, ALU.mult).then_inc(dve_done, dve_p.step(("swaT", l)))
                dve.wait_ge(pe_done, at(("stick_T", l, 1)))
                nc.vector.tensor_copy(stick_kT[:].rearrange("p j t -> p (j t)"), ps[:, 7, :]).then_inc(dve_done, dve_p.step(("stickT", l, 1)))

                def head_max(slot, bank, bias, scale, at, h, key):
                    for a, (c0, c1) in enumerate(((0, P), (P, SEG))):
                        nc.vector.tensor_tensor_reduce(
                            out=S[:, slot, c0:c1], in0=ps[:, bank, c0:c1], in1=bias[:, c0:c1], scale=scale,
                            scalar=-3e38, op0=ALU.add, op1=ALU.max,
                            accum_out=stat_a[:, at + 8 * (h // 4) + 4 * a + h % 4:
                                             at + 8 * (h // 4) + 4 * a + h % 4 + 1]).then_inc(dve_done, dve_p.step(key))

                def softplus(h):
                    dve.wait_ge(act_done, at(("ln", l, h)))
                    nc.vector.scalar_tensor_tensor(stick[:, h, :], ps[:, 4 + h, 0:SEG], 0.0, stick[:, h, :],
                                                         ALU.max, ALU.add).then_inc(dve_done, dve_p.step())
                    dve.wait_ge(dve_done, own())
                    nc.vector.tensor_tensor(stick[:, h, :], stick[:, h, :], C("stick_mul"), ALU.mult).then_inc(dve_done, dve_p.step(("sp", l, h)))

                for h in range(HA):
                    dve.wait_ge(pe_done, at(("sA", l, h)))
                    head_max(h, h, C("causal"), 1.0, 0, h, ("sA_read", l, h))
                dve.wait_ge(dve_done, own())
                nc.vector.tensor_scalar(stat_a[:, 24:32], stat_a[:, 0:8], -1.0, None, ALU.mult).then_inc(dve_done, dve_p.step(("nmA", l)))
                for h in range(HC):
                    softplus(h)

                def swa_max(q):
                    for h in range(4 * q, 4 * q + 4):
                        dve.wait_ge(pe_done, at(("sB", l, h)))
                        if q:
                            dve.wait_ge(pe_done, at(("pA_T", l, h - 4)))
                        head_max((4 + h) % 8, h % 4, C("negdist"), 2.0 ** -(h + 1), 8, h, ("sB_read", l, h))
                    dve.wait_ge(dve_done, own())
                    sink = G("sinks", l)[:, 4 * q:4 * q + 4].rearrange("p (o h) -> p o h", o=1).broadcast_to([P, TT, 4])

                    def by_tile(c0):
                        return stat_a[:, c0 + 8 * q:c0 + 8 * q + 8].rearrange("p (a h) -> p a h", a=TT)
                    nc.vector.tensor_tensor(by_tile(8), by_tile(8), sink, ALU.max).then_inc(dve_done, dve_p.step())
                    dve.wait_ge(dve_done, own())
                    nc.vector.tensor_scalar(by_tile(32), by_tile(8), -1.0, None, ALU.mult).then_inc(dve_done, dve_p.step())
                    dve.wait_ge(dve_done, own())
                    nc.vector.tensor_tensor(by_tile(72), by_tile(32), sink, ALU.add).then_inc(dve_done, dve_p.step(("nmB", l, q)))

                swa_max(0)
                for h in range(HC):
                    dve.wait_ge(pe_done, at(("cum", l, h)))
                    nc.vector.tensor_tensor(stick[:, h, :], ps[:, 4 + h, 0:SEG], C("stick_add"), ALU.add).then_inc(dve_done, dve_p.step(("w_read", l, h)))
                for h in (1, 3):
                    dve.wait_ge(pe_done, at(("pA_T", l, h)))
                    nc.vector.tensor_copy(probsT[:, h, :], ps[:, 4 + h, 0:SEG]).then_inc(dve_done, dve_p.step(("pTA", l, h)))
                swa_max(1)

                def heads_out(bank, den, c0, key):
                    o = mixed[:, :, c0:c0 + 256].rearrange("p a (h d) -> p a h d", h=4)
                    i = ps[:, bank, :].rearrange("p (a h d) -> p a h d", a=TT, h=4)
                    d = den.rearrange("p (a h o) -> p a h o", a=TT, o=1).broadcast_to([P, TT, 4, HD])
                    nc.vector.tensor_tensor(o, i, d, ALU.mult).then_inc(dve_done, dve_p.step(key))

                dve.wait_ge(act_done, at(("pA", l, HA - 1)))
                nc.vector.reciprocal(stat_a[:, 0:8], stat_a[:, 48:56]).then_inc(dve_done, dve_p.step())
                dve.wait_ge(dve_done, own())
                dve.wait_ge(pe_done, at(("oA", l, HA - 1)))
                heads_out(4, stat_a[:, 0:8], 0, ("oA_read", l))
                dve.wait_ge(pe_done, at(("oC", l, HC - 1)))
                nc.vector.tensor_copy(mixed[:, :, 768:1024],
                                                 ps[:, 5, :].rearrange("p (a n) -> p a n", a=TT)).then_inc(dve_done, dve_p.step(("oC_read", l)))
                for q in range(2):
                    for h in (4 * q + 1, 4 * q + 3):
                        dve.wait_ge(pe_done, at(("pB_T", l, h)))
                        dve.wait_ge(pe_done, at(("oA", l, h) if q == 0 else ("oB", l, h - 4)))
                        nc.vector.tensor_copy(probsT[:, h % 4, :],
                                                         ps[:, (6, 7, 0, 1, 3, 6, 7, 0)[h], 0:SEG]).then_inc(dve_done, dve_p.step(("pTB", l, h)))
                    dve.wait_ge(act_done, at(("sink_e", l, q)))
                    den = stat_a[:, 8 + 8 * q:16 + 8 * q]
                    nc.vector.tensor_tensor(den, stat_a[:, 56 + 8 * q:64 + 8 * q],
                                                  stat_a[:, 72 + 8 * q:80 + 8 * q], ALU.add).then_inc(dve_done, dve_p.step())
                    dve.wait_ge(dve_done, own())
                    nc.vector.reciprocal(den, den).then_inc(dve_done, dve_p.step())
                    dve.wait_ge(dve_done, own())
                    dve.wait_ge(pe_done, at(("oB", l, 4 * q + 3)))
                    heads_out(2 if q == 0 else 1, den, 256 + 256 * q, ("oB_read", l, q))
                dve.wait_ge(act_done, at(("mix_sq", l)))
                nc.vector.tensor_scalar(stat[:, 6:12], stat[:, 0:6], EPS, None, ALU.add).then_inc(dve_done, dve_p.step((("mix", l), "ms")))
                dve.wait_ge(dve_done, own())
                refine(stat[:, 6:12], stat[:, 12:18], stat[:, 90:96], ("mix", l))
                for i, (c0, w) in enumerate(((0, 256), (256, 512), (768, 256))):
                    nc.vector.tensor_scalar(mixed[:, 0, c0:c0 + w], mixed[:, 0, c0:c0 + w], stat[:, 12 + i:13 + i],
                                            None, ALU.mult).then_inc(dve_done, dve_p.step(("mix_n", l, 0)))
                dve.wait_ge(pe_done, at(("oB", l, HB - 1)))
                transposed_lo(l, "mix_n", G("out_g", l), hT_hi, hT_lo, lambda b: rest(l, b))
                for n in range(2):
                    for q in range(SPLIT * (n + 1), SPLIT * (n + 2) - n):
                        if q < len(L_PIECES[l]):
                            rest(l, q)
                    dve.wait_ge(pe_done, at(("piece", l, L_LAST[l]["out", n])))
                    for a in range(TT):
                        part = xres[:, a, n * CH:(n + 1) * CH]
                        nc.vector.tensor_tensor(part, ps[:, 4 + 2 * n + a, :], part, ALU.add).then_inc(dve_done, dve_p.step(("proj_add", l, 2 * n + a)))
                row_norm(l, "ffn_n")
                if l % 2 == 0:
                    rest(l, N_OUT + SPLIT - 1)
                if l % 2:
                    transposed_out(l, "ffn_n", G("ffn_g", l))
                else:
                    transposed_lo(l, "ffn_n", G("ffn_g", l), hT_hi, hT_lo)

            def rest(l, q):
                (kind, c), r = L_PIECES[l][q]
                dve.wait_ge(act_done, at(("lead", l, q)))
                nc.vector.tensor_tensor(d_lo[:, q % SPLIT, :], slot_of(UNIT_NO[kind, l, c])[:, r * PIECE:(r + 1) * PIECE],
                                        d_hi[:, q % SPLIT, :].bitcast(F32), ALU.subtract).then_inc(dve_done, dve_p.step(("rest", l, q)))

            def dense(l):
                for q in range(N_OUT + SPLIT, len(L_PIECES[l]) + 2):
                    if q < len(L_PIECES[l]):
                        rest(l, q)
                    for c in range(len(FF_CHUNKS)):
                        w = FF_CHUNKS[c] // P * T
                        if q == L_LAST[l]["gate", c] + SPLIT + 1:
                            dve.wait_ge(act_done, at(("sig", l, c)))
                            nc.vector.tensor_tensor(gated_d[:, 0:w], ps[:, 0:w // 512, :].rearrange("p b n -> p (b n)"),
                                                    sig_d[:, 0:w], ALU.mult).then_inc(dve_done, dve_p.step(("gated", l, c)))
                        if q == L_LAST[l]["up", c] + SPLIT:
                            dve.wait_ge(dve_done, own())
                            nc.vector.tensor_tensor(hidden_d[:, 0:w], ps[:, 2:2 + w // 512, :].rearrange("p b n -> p (b n)"),
                                                    gated_d[:, 0:w], ALU.mult).then_inc(dve_done, dve_p.step(("hidden", l, c)))
                        if q == L_LAST[l]["up", c] + SPLIT + 2:
                            dve.wait_ge(act_done, at(("hid_hi", l, c)))
                            nc.vector.tensor_tensor(hid_lo[:, c % 2, 0:w], hidden_d[:, 0:w],
                                                    hid_hi[:, c % 2, 0:w].bitcast(F32), ALU.subtract).then_inc(dve_done, dve_p.step(("hid_lo", l, c)))
                dve.wait_ge(pe_done, at(("piece", l, len(L_PIECES[l]) - 1)))
                for a in range(TT):
                    for n in range(2):
                        part = xres[:, a, n * CH:(n + 1) * CH]
                        nc.vector.tensor_tensor(part, ps[:, 4 + 2 * a + n, :], part, ALU.add).then_inc(dve_done, dve_p.step(("ffn_add", l, a)))

            def nothing_to_scatter(g=0):
                nc.vector.memset(ps[:, 4:6, :].rearrange("p b n -> p (b n)"), 0.0).then_inc(dve_done, dve_p.step())
                nc.vector.memset(pick_gT[:].rearrange("p a s -> p (a s)"), 0.0).then_inc(dve_done, dve_p.step((g, "pass")))

            def route():
                iota8 = C("iota")[:, 0:NE]
                nc.vector.memset(rankm[:], -1.0).then_inc(dve_done, dve_p.step())
                dve.wait_ge(dve_done, own())
                nc.vector.memset(gates[:], 0.0).then_inc(dve_done, dve_p.step())
                dve.wait_ge(dve_done, own())
                dve.wait_ge(act_done, at(("ffn_n_done", DEPTH - 1, 1)))
                nothing_to_scatter()
                dve.wait_ge(pe_done, at("logits"))
                logits = stat_a[:, 0:16].rearrange("p (a n) -> p a n", a=TT)
                nc.vector.tensor_copy(logits, ps[:, 0:TT, 0:NE]).then_inc(dve_done, dve_p.step())
                dve.wait_ge(dve_done, own())
                for a in range(TT):
                    nc.vector.max(top[:, a, :], logits[:, a, :]).then_inc(dve_done, dve_p.step())
                    dve.wait_ge(dve_done, own())
                    nc.vector.max_index(top_at[:, a, :], top[:, a, :], logits[:, a, :]).then_inc(dve_done, dve_p.step())
                    dve.wait_ge(dve_done, own())
                found = stat_a[:, 16:32].rearrange("p (a n) -> p a n", a=TT)
                nc.vector.tensor_copy(found, top_at[:]).then_inc(dve_done, dve_p.step())
                dve.wait_ge(dve_done, own())
                gap = stat_a[:, 32:34].rearrange("p (a o) -> p a o", a=TT)
                nc.vector.tensor_tensor(gap, top[:, :, 0:1], top[:, :, 1:2], ALU.subtract).then_inc(dve_done, dve_p.step("gap"))
                dve.wait_ge(dve_done, own())
                dve.wait_ge(act_done, at("first_gate"))
                g1, g2 = stat_a[:, 34:36], stat_a[:, 36:38]
                nc.vector.tensor_scalar(stat_a[:, 38:40], g2, 1.0, None, ALU.add).then_inc(dve_done, dve_p.step())
                dve.wait_ge(dve_done, own())
                nc.vector.reciprocal(g1, stat_a[:, 38:40]).then_inc(dve_done, dve_p.step())
                dve.wait_ge(dve_done, own())
                nc.vector.tensor_tensor(g2, g2, g1, ALU.mult).then_inc(dve_done, dve_p.step())
                dve.wait_ge(dve_done, own())
                one = stat_a[:, 40:72].rearrange("p (i a n) -> p i a n", i=2, a=TT)
                for a in range(TT):
                    for i in range(2):
                        nc.vector.tensor_scalar(one[:, i, a, :], iota8, found[:, a, i:i + 1], None, ALU.is_equal).then_inc(dve_done, dve_p.step())
                        dve.wait_ge(dve_done, own())
                nc.vector.tensor_tensor(sel[:], one[:, 0], one[:, 1], ALU.add).then_inc(dve_done, dve_p.step("selected"))
                dve.wait_ge(dve_done, own())
                for a in range(TT):
                    nc.vector.tensor_scalar(one[:, 0, a, :], one[:, 0, a, :], g1[:, a:a + 1], None, ALU.mult).then_inc(dve_done, dve_p.step())
                    dve.wait_ge(dve_done, own())
                    nc.vector.scalar_tensor_tensor(gates[:, a, 0:NE], one[:, 1, a, :], g2[:, a:a + 1],
                                                         one[:, 0, a, :], ALU.mult, ALU.add).then_inc(dve_done, dve_p.step())
                    dve.wait_ge(dve_done, own())
                for a in range(TT):
                    dve.wait_ge(act_done, at("xn_hi"))
                    nc.vector.tensor_tensor(xn_lo[:, a, :], xn[:, a, :], xn_hi[:, a, :].bitcast(F32),
                                            ALU.subtract).then_inc(dve_done, dve_p.step("xn_lo"))
                dve.wait_ge(pe_done, at("ranks"))
                nc.vector.scalar_tensor_tensor(rankm[:, :, 0:NE],
                                                     ps[:, 2, 0:2 * NE].rearrange("p (a n) -> p a n", a=TT), 1.0,
                                                     sel[:], ALU.add, ALU.mult).then_inc(dve_done, dve_p.step())
                dve.wait_ge(dve_done, own())
                nc.vector.tensor_scalar(rankm[:, :, 0:NE], rankm[:, :, 0:NE], -1.0, None, ALU.add).then_inc(dve_done, dve_p.step())
                dve.wait_ge(dve_done, own())
                nc.vector.tensor_reduce(over[:, 0:1], ps[:, 2, 2 * NE:3 * NE], AX.X, ALU.max).then_inc(dve_done, dve_p.step())
                dve.wait_ge(dve_done, own())
                nc.vector.tensor_scalar(over[:, 1:2], over[:, 0:1], float(GROUP), None, ALU.is_gt).then_inc(dve_done, dve_p.step())
                dve.wait_ge(dve_done, own())
                nc.vector.tensor_copy(over_i[0:1, 0:1], over[0:1, 1:2]).then_inc(dve_done, dve_p.step("overflow"))
                dve.wait_ge(dve_done, own())

            def experts(g):
                slots = C("iota")[:, g * GROUP:(g + 1) * GROUP]

                def picks(key, e):
                    for a in range(TT):
                        r = rankm[:, a, 0:1] if e is None else rankm[:, a, bass.ds(e + 1, 1)]
                        w = gates[:, a, 0:1] if e is None else gates[:, a, bass.ds(e + 1, 1)]
                        nc.vector.tensor_scalar(pick[:, a, :], slots, r, None, ALU.is_equal).then_inc(dve_done, dve_p.step())
                        nc.vector.tensor_scalar(pick_g[:, a, :], slots, r, w, ALU.is_equal, ALU.mult).then_inc(dve_done, dve_p.step((g, key, "pick")))

                def add(it, key):
                    for q, bank in enumerate(SCATTER_BANKS):
                        dve.wait_ge(pe_done, at((g, "scatter" + key, q), it))
                        a, n = q // 2, q % 2
                        part = xres[:, a, n * CH:(n + 1) * CH]
                        nc.vector.tensor_tensor(part, ps[:, bank, :], part, ALU.add).then_inc(dve_done, dve_p.step((g, "add" + key, q)))

                def gathered_rest(key, it=None):
                    for n in range(2):
                        dve.wait_ge(act_done, at((g, key, "xgT_hi", n), it))
                        for k in range(4 * n, 4 * n + 4):
                            nc.vector.scalar_tensor_tensor(xgT_lo[:, k, :], ps[:, 6 + n, (k % 4) * P:(k % 4 + 1) * P],
                                                           G("ffn_g", DEPTH - 1)[:, k:k + 1],
                                                           xgT_hi[:, k, :].bitcast(F32), ALU.mult,
                                                           ALU.subtract).then_inc(dve_done, dve_p.step((g, key, "xgT_lo")))

                if g:
                    dve.wait_ge(pe_done, at((0, "scatter_end", 3)))
                    dve.wait_ge(act_done, at((0, "y_out_end")))
                    nothing_to_scatter(g)
                picks("first", None)
                if g == 0:
                    more.append(dve.value_load(over_i[0:1, 0:1], min_val=0, max_val=1))
                gathered_rest("first")
                dve_p.enter(("experts", g))
                with dve.Fori(0, NE) as e:
                    for q, ((kind, c), r) in enumerate(E_PIECES):
                        no = N_UNITS + g * NE * M_UNITS + MOE_NO[kind, c]
                        dve.wait_ge(act_done, at((g, "lead", q), e))
                        nc.vector.tensor_tensor(e_lo[:, q % SPLIT, :], slot_of(no)[:, r * PIECE:(r + 1) * PIECE],
                                                e_hi[:, q % SPLIT, :].bitcast(F32), ALU.subtract).then_inc(dve_done, dve_p.step((g, "rest", q)))
                        if q in AT_HIDT:
                            n = AT_HIDT[q]
                            dve.wait_ge(act_done, at((g, "hidT_hi", n), e))
                            nc.vector.tensor_tensor(hidT_lo[:, n % 2, :], ps[:, T_BANK[n], :],
                                                    hidT_hi[:, n % 2, :].bitcast(F32), ALU.subtract).then_inc(dve_done, dve_p.step((g, "hidT_lo", n)))
                        if q in AT_GATED:
                            n = AT_GATED[q]
                            dve.wait_ge(act_done, at((g, "sig", n), e))
                            nc.vector.tensor_tensor(gated, ps[:, n % 2, :], sig[:, n % 2, :], ALU.mult).then_inc(dve_done, dve_p.step((g, "gated", n)))
                        if q in AT_HID:
                            n = AT_HID[q]
                            dve.wait_ge(dve_done, at((g, "gated", n), e))
                            nc.vector.tensor_tensor(hid[:, n % 2, :], ps[:, 2 + n % 2, :], gated, ALU.mult).then_inc(dve_done, dve_p.step((g, "hid", n)))
                        if q == AT_ADD:
                            add(e, "")
                        if q == AT_PICKS:
                            picks("next", e)
                        if q == AT_GATHERED:
                            gathered_rest("next", e)
                dve_p.leave(NE)
                add(None, "_end")
                dve.wait_ge(dve_done, own())

            layer_mixers(0)
            dense(0)
            layer_mixers(1)
            route()
            experts(0)
            with dve.If(more[0] > 0):
                experts(1)
            nc.vector.memset(over[0:1, 2:3], 0.0).then_inc(result_ready, 1)

    return marks


def constants():
    c = np.zeros((P, N_CONST), np.float32)

    def put(name, value):
        a, w = CONST[name]
        c[:, a:a + w] = np.reshape(value, (-1, w))

    p = np.arange(P)[:, None]
    n = np.arange(P)[None, :]
    put("ident", p == n)
    half = ROPE // 2
    inv = (np.float32(10000.0) ** (-np.arange(half, dtype=np.float32) / np.float32(half))).astype(np.float32)
    pos = (np.arange(TT)[None, :] * P + p).astype(np.float32)
    ang = (pos[:, :, None] * inv).astype(np.float32)
    put("cos", np.cos(ang))
    put("sin", np.sin(ang))
    dist = np.concatenate([p - n, p + P - np.arange(T)[None, :]], 1)
    put("causal", np.where(dist >= 0, 0.0, NEG))
    put("negdist", np.where((dist >= 0) & (dist < P), -dist, NEG))
    before = np.concatenate([p < np.arange(T)[None, :], p < n], 1)
    put("stick_add", np.where(before, 0.0, NEG))
    put("stick_mul", before)
    put("neg_tri", -(p >= n).astype(np.float32))
    put("neg_ones", -1.0 * np.ones((P, P)))
    put("ones", np.ones((P, P)))
    put("rank_tri", p < n)
    put("iota", np.broadcast_to(np.arange(2 * GROUP), (P, 2 * GROUP)))
    swa = [HD ** -0.5 * 2.0 ** (h + 1) for h in range(HB)] + [1.0] * HKV
    put("swa_scale", np.broadcast_to(np.tile(swa, TT), (P, TT * (HB + HKV))))
    put("mla_scale", np.broadcast_to(np.tile([QK ** -0.5] * HA + [1.0] * HA, TT), (P, TT * 2 * HA)))
    return c


def small_weights(i):
    s = np.zeros((P, N_SMALL), np.float32)
    for l in range(DEPTH):
        for name, v in (("attn_g", i["attn_norm_g"][l]), ("ffn_g", i["ffn_norm_g"][l]), ("out_g", i["out_norm_g"][l]),
                        ("cq_g", i["mla_cq_norm_g"][l]), ("ckv_g", i["mla_ckv_norm_g"][l])):
            a, w = SMALL[name, l]
            s[:, a:a + w] = v.reshape(w, P).T
        for name, v in (("swa_q_g", i["swa_qn_g"][l]), ("swa_k_g", i["swa_kn_g"][l])):
            a, _ = SMALL[name, l]
            s[:, a] = np.concatenate([v, v])
        for name, v in (("qn_g", i["mla_qn_g"][l]), ("kn_g", i["mla_kn_g"][l]), ("sinks", i["swa_sinks"][l])):
            a, w = SMALL[name, l]
            s[:, a:a + w] = v[None, :]
    a, w = SMALL["router"]
    s[:, a:a + w] = i["router_w"][0].reshape(KD, P, NE).transpose(1, 0, 2).reshape(P, w)
    return s


def kernel(**inputs):
    import concourse.bacc as bacc
    from concourse.bass_utils import run_bass_kernel_spmd

    arrays = {name: np.ascontiguousarray(inputs[key]) for name, key in (
        ("x", "x"), ("w_in", "w_in"), ("w_uq", "mla_w_uq"), ("w_ukv", "mla_w_ukv"), ("w_out", "w_out"),
        ("dense_g", "dense_w_gate"), ("dense_u", "dense_w_up"), ("dense_d", "dense_w_down"),
        ("moe_g", "moe_w_gate"), ("moe_u", "moe_w_up"), ("moe_d", "moe_w_down"))}
    arrays["smalls"] = small_weights({k: np.asarray(v) for k, v in inputs.items()})
    arrays["cst"] = constants()
    known = None
    for _ in range(2):
        nc = bacc.Bacc("TRN2", target_bir_lowering=False, num_devices=1, dynamic_dma_scratch_size=1024)
        aps = {n: nc.dram_tensor(n, a.shape, F32, kind="ExternalInput").ap() for n, a in arrays.items()}
        out = nc.dram_tensor("out", (1, T, D), F32, kind="ExternalOutput").ap()
        known = trunk_program(nc, known, out=out, **aps)
    r = run_bass_kernel_spmd(nc, [arrays], core_ids=[0])
    return r.results[0]["out"]
```
